# Optimizing a Trainium2 kernel written in Bass

```python
import math
import jax, jax.numpy as jnp
from jax import lax
import numpy as np

D_MODEL = 1024
BATCH = 1
SEQ = 1024
DEPTH = 1

CHUNK = 64
Q_BLOCK = 128
EPS = 1e-6

DA_HEADS = 4
DA_HEAD_DIM = 64
DA_V_DIM = 2 * DA_HEAD_DIM
DA_WIDTH = DA_HEADS * DA_V_DIM
ALIBI_MAX = 8.0

RET_HEADS = 4
RET_QK_DIM = 64
RET_V_DIM = 128
RET_WIDTH = RET_HEADS * RET_V_DIM

MIX_WIDTH = DA_WIDTH + RET_WIDTH

DA_Q_COLS = DA_HEADS * 2 * DA_HEAD_DIM
DA_K_COLS = DA_HEADS * 2 * DA_HEAD_DIM
DA_V_COLS = DA_WIDTH
RET_Q_COLS = RET_HEADS * RET_QK_DIM
RET_K_COLS = RET_HEADS * RET_QK_DIM
RET_V_COLS = RET_WIDTH
RET_G_COLS = RET_WIDTH
IN_COLS = DA_Q_COLS + DA_K_COLS + DA_V_COLS + RET_Q_COLS + RET_K_COLS + RET_V_COLS + RET_G_COLS
IN_SPLITS = (DA_Q_COLS,
             DA_Q_COLS + DA_K_COLS,
             DA_Q_COLS + DA_K_COLS + DA_V_COLS,
             DA_Q_COLS + DA_K_COLS + DA_V_COLS + RET_Q_COLS,
             DA_Q_COLS + DA_K_COLS + DA_V_COLS + RET_Q_COLS + RET_K_COLS,
             DA_Q_COLS + DA_K_COLS + DA_V_COLS + RET_Q_COLS + RET_K_COLS + RET_V_COLS)

MOE_GROUPS = 4
MOE_EXPERTS_PER_GROUP = 8
MOE_EXPERTS = MOE_GROUPS * MOE_EXPERTS_PER_GROUP
MOE_TOP_K = 2
MOE_HIDDEN = 512
MOE_BLOCK = 128


def rmsnorm(x, g):
    xf = x.astype(jnp.float32)
    y = xf * lax.rsqrt(jnp.mean(xf * xf, axis=-1, keepdims=True) + EPS)
    return (y * g.astype(jnp.float32)).astype(x.dtype)

def head_rmsnorm(x):
    xf = x.astype(jnp.float32)
    return xf * lax.rsqrt(jnp.mean(xf * xf, axis=-1, keepdims=True) + EPS)

def alibi_slopes(n_heads):
    return jnp.exp2(-ALIBI_MAX * jnp.arange(1, n_heads + 1, dtype=jnp.float32) / n_heads)

def diff_attention(q, k, v, lam, subln_g, lambda_init):
    B, S = q.shape[0], q.shape[1]
    nb = S // Q_BLOCK
    scale = DA_HEAD_DIM ** -0.5
    slopes = alibi_slopes(DA_HEADS)
    k_pos = jnp.arange(S)
    k_chunk = k_pos // CHUNK
    qb = q.reshape(B, nb, Q_BLOCK, DA_HEADS, 2, DA_HEAD_DIM).transpose(1, 0, 2, 3, 4, 5)

    def one_block(args):
        i, q_blk = args
        q_pos = i * Q_BLOCK + jnp.arange(Q_BLOCK)
        s = jnp.einsum('bqhmd,bkhmd->bhmqk', q_blk, k,
                       preferred_element_type=jnp.float32) * scale
        dist = jnp.abs(q_pos[:, None] - k_pos[None, :]).astype(jnp.float32)
        bias = -slopes[:, None, None, None] * dist[None, None]
        allowed = k_chunk[None, :] <= (q_pos // CHUNK)[:, None]
        s = jnp.where(allowed, s + bias, -jnp.inf)
        p = jax.nn.softmax(s, axis=-1)
        a = p[:, :, 0] - lam * p[:, :, 1]
        return jnp.einsum('bhqk,bkhe->bqhe', a.astype(v.dtype), v)

    o = lax.map(one_block, (jnp.arange(nb), qb))
    o = o.transpose(1, 0, 2, 3, 4).reshape(B, S, DA_HEADS, DA_V_DIM)
    o = rmsnorm(o, subln_g) * (1.0 - lambda_init)
    return o.reshape(B, S, DA_WIDTH)

def retention(q, k, v, g):
    B, S = q.shape[0], q.shape[1]
    nc = S // CHUNK
    f32 = jnp.float32
    log_gamma = jnp.log1p(-jnp.exp2(-5.0 - jnp.arange(RET_HEADS, dtype=f32)))
    qc = q.astype(f32).reshape(B, nc, CHUNK, RET_HEADS, RET_QK_DIM)
    kc = (k.astype(f32) * RET_QK_DIM ** -0.5).reshape(B, nc, CHUNK, RET_HEADS, RET_QK_DIM)
    vc = v.astype(f32).reshape(B, nc, CHUNK, RET_HEADS, RET_V_DIM)
    pos = jnp.arange(CHUNK, dtype=f32)
    rel = pos[:, None] - pos[None, :]
    intra_decay = jnp.where(rel >= 0, jnp.exp(log_gamma[:, None, None] * jnp.maximum(rel, 0.0)), 0.0)
    s = jnp.einsum('bnchd,bnshd->bnhcs', qc, kc) * intra_decay
    intra = jnp.einsum('bnhcs,bnshe->bnche', s, vc)
    k_decay = jnp.exp(log_gamma[:, None] * (CHUNK - 1 - pos)[None, :])
    kv = jnp.einsum('bnshd,hs,bnshe->bnhde', kc, k_decay, vc)
    chunk_decay = jnp.exp(log_gamma * CHUNK)[:, None, None]

    def step(state, kv_n):
        return state * chunk_decay + kv_n, state

    init = jnp.zeros((B, RET_HEADS, RET_QK_DIM, RET_V_DIM), f32)
    _, prev = lax.scan(step, init, kv.transpose(1, 0, 2, 3, 4))
    prev = prev.transpose(1, 0, 2, 3, 4)
    q_decay = jnp.exp(log_gamma[:, None] * (pos + 1.0)[None, :])
    cross = jnp.einsum('bnchd,hc,bnhde->bnche', qc, q_decay, prev)
    o = head_rmsnorm((intra + cross).reshape(B, S, RET_HEADS, RET_V_DIM))
    o = jax.nn.silu(g.astype(f32)) * o
    return o.reshape(B, S, RET_WIDTH).astype(q.dtype)

def hier_moe(xn, wg, bg, we, be, w_gate, w_up, w_down):
    B, S, D = xn.shape
    T = B * S
    f32 = jnp.float32
    xt = xn.reshape(T, D)
    g_prob = jax.nn.softmax((xt @ wg + bg).astype(f32), axis=-1)
    g_top_p, g_top_i = lax.top_k(g_prob, 1)
    grp = g_top_i[:, 0]
    e_logits = (xt @ we + be).astype(f32).reshape(T, MOE_GROUPS, MOE_EXPERTS_PER_GROUP)
    idx = jnp.broadcast_to(grp[:, None, None], (T, 1, MOE_EXPERTS_PER_GROUP))
    e_logits = jnp.take_along_axis(e_logits, idx, axis=1)[:, 0]
    top_val, top_idx = lax.top_k(e_logits, MOE_TOP_K)
    weights = g_top_p * jax.nn.softmax(top_val, axis=-1)
    expert_id = grp[:, None] * MOE_EXPERTS_PER_GROUP + top_idx

    N = T * MOE_TOP_K
    e_flat = expert_id.reshape(N).astype(jnp.int32)
    w_flat = weights.reshape(N)
    tok_flat = jnp.repeat(jnp.arange(T, dtype=jnp.int32), MOE_TOP_K)
    order = jnp.argsort(e_flat)
    sorted_e = e_flat[order]
    counts = jnp.zeros((MOE_EXPERTS,), jnp.int32).at[e_flat].add(1)
    start = jnp.cumsum(counts) - counts
    padded = (counts + MOE_BLOCK - 1) // MOE_BLOCK * MOE_BLOCK
    pad_end = jnp.cumsum(padded)
    pad_start = pad_end - padded
    dest = pad_start[sorted_e] + jnp.arange(N, dtype=jnp.int32) - start[sorted_e]
    n_blocks = (N + MOE_BLOCK - 1) // MOE_BLOCK + MOE_EXPERTS
    nbuf = n_blocks * MOE_BLOCK
    buf_tok = jnp.full((nbuf,), T, jnp.int32).at[dest].set(tok_flat[order])
    buf_w = jnp.zeros((nbuf,), f32).at[dest].set(w_flat[order])
    block_e = jnp.minimum(jnp.searchsorted(pad_end, jnp.arange(n_blocks, dtype=jnp.int32) * MOE_BLOCK,
                                           side='right'), MOE_EXPERTS - 1)
    x_pad = jnp.concatenate([xt, jnp.zeros((1, D), xt.dtype)], axis=0)
    xb = x_pad[buf_tok].reshape(n_blocks, MOE_BLOCK, D)

    def expert_block(args):
        xblk, e = args
        h = jax.nn.silu(xblk @ w_gate[e]) * (xblk @ w_up[e])
        return h @ w_down[e]

    yb = lax.map(expert_block, (xb, block_e)).reshape(nbuf, D)
    y = jnp.zeros((T + 1, D), f32).at[buf_tok].add(yb.astype(f32) * buf_w[:, None])[:T]
    return y.reshape(B, S, D).astype(xn.dtype)

def first_inputs(seed: int = 0) -> dict:
    key = jax.random.key(seed)
    ks = jax.random.split(key, 20)
    f32 = jnp.float32
    L, D = DEPTH, D_MODEL

    def nrm(k, shape, scale):
        return jax.random.normal(k, shape, f32) * scale

    return {
        "x": nrm(ks[0], (BATCH, SEQ, D), 1.0),
        "attn_norm_g": 1.0 + nrm(ks[1], (L, D), 0.02),
        "w_in": nrm(ks[2], (L, D, IN_COLS), D ** -0.5),
        "da_lambda_q1": nrm(ks[3], (L, DA_HEAD_DIM), 0.1),
        "da_lambda_k1": nrm(ks[4], (L, DA_HEAD_DIM), 0.1),
        "da_lambda_q2": nrm(ks[5], (L, DA_HEAD_DIM), 0.1),
        "da_lambda_k2": nrm(ks[6], (L, DA_HEAD_DIM), 0.1),
        "da_subln_g": 1.0 + nrm(ks[7], (L, DA_V_DIM), 0.02),
        "w_out": nrm(ks[8], (L, MIX_WIDTH, D), MIX_WIDTH ** -0.5),
        "ffn_norm_g": 1.0 + nrm(ks[9], (L, D), 0.02),
        "router_group_w": nrm(ks[10], (L, D, MOE_GROUPS), D ** -0.5),
        "router_group_b": nrm(ks[11], (L, MOE_GROUPS), 0.01),
        "router_expert_w": nrm(ks[12], (L, D, MOE_EXPERTS), D ** -0.5),
        "router_expert_b": nrm(ks[13], (L, MOE_EXPERTS), 0.01),
        "expert_w_gate": nrm(ks[14], (L, MOE_EXPERTS, D, MOE_HIDDEN), D ** -0.5),
        "expert_w_up": nrm(ks[15], (L, MOE_EXPERTS, D, MOE_HIDDEN), D ** -0.5),
        "expert_w_down": nrm(ks[16], (L, MOE_EXPERTS, MOE_HIDDEN, D), MOE_HIDDEN ** -0.5),
        "final_norm_g": 1.0 + nrm(ks[17], (D,), 0.02),
    }

def first_block(x, attn_norm_g, w_in, da_lambda_q1, da_lambda_k1, da_lambda_q2, da_lambda_k2,
              da_subln_g, w_out, ffn_norm_g, router_group_w, router_group_b, router_expert_w,
              router_expert_b, expert_w_gate, expert_w_up, expert_w_down, final_norm_g):
    B, S, _ = x.shape
    h = x
    for l in range(DEPTH):
        xn = rmsnorm(h, attn_norm_g[l])
        proj = xn @ w_in[l]
        q_da, k_da, v_da, q_r, k_r, v_r, g_r = jnp.split(proj, IN_SPLITS, axis=-1)
        lambda_init = 0.8 - 0.6 * math.exp(-0.3 * l)
        lam = (jnp.exp(jnp.sum(da_lambda_q1[l].astype(jnp.float32) * da_lambda_k1[l].astype(jnp.float32)))
               - jnp.exp(jnp.sum(da_lambda_q2[l].astype(jnp.float32) * da_lambda_k2[l].astype(jnp.float32)))
               + lambda_init)
        o_da = diff_attention(q_da.reshape(B, S, DA_HEADS, 2, DA_HEAD_DIM),
                              k_da.reshape(B, S, DA_HEADS, 2, DA_HEAD_DIM),
                              v_da.reshape(B, S, DA_HEADS, DA_V_DIM),
                              lam, da_subln_g[l], lambda_init)
        o_r = retention(q_r.reshape(B, S, RET_HEADS, RET_QK_DIM),
                        k_r.reshape(B, S, RET_HEADS, RET_QK_DIM),
                        v_r.reshape(B, S, RET_HEADS, RET_V_DIM),
                        g_r.reshape(B, S, RET_HEADS, RET_V_DIM))
        mix = jnp.concatenate([o_da.astype(h.dtype), o_r.astype(h.dtype)], axis=-1)
        h = h + mix @ w_out[l]
        xn = rmsnorm(h, ffn_norm_g[l])
        h = h + hier_moe(xn, router_group_w[l], router_group_b[l], router_expert_w[l],
                         router_expert_b[l], expert_w_gate[l], expert_w_up[l], expert_w_down[l])
    return rmsnorm(h, final_norm_g)


N_MIXERS = 4
D_FF = 4 * D_MODEL
RMS_EPS = 1e-6
CONV_KERNEL = 31
SHORT_CONV = 3
FOX_HEADS = 16
FOX_HEAD_DIM = D_MODEL // FOX_HEADS
GLA_HEADS = 4
GLA_DK = D_MODEL // 2
GLA_DV = D_MODEL
GLA_DK_HEAD = GLA_DK // GLA_HEADS
GLA_DV_HEAD = GLA_DV // GLA_HEADS
GLA_GATE_RANK = 16
GLA_TAU = 16.0
GLA_CHUNK = 64


def _layers_of(m):
    return len(range(m, DEPTH, N_MIXERS))

def rms_norm(x, g):
    x32 = x.astype(jnp.float32)
    y = x32 * lax.rsqrt(jnp.mean(x32 * x32, axis=-1, keepdims=True) + RMS_EPS)
    return (y * g.astype(jnp.float32)).astype(x.dtype)

def layer_norm(x, g, b):
    x32 = x.astype(jnp.float32)
    mu = jnp.mean(x32, axis=-1, keepdims=True)
    xc = x32 - mu
    y = xc * lax.rsqrt(jnp.mean(xc * xc, axis=-1, keepdims=True) + RMS_EPS)
    return (y * g.astype(jnp.float32) + b.astype(jnp.float32)).astype(x.dtype)

def conformer_conv(x, w_in, b_in, conv_w, conv_b, ln_g, ln_b, w_out, b_out):
    a, g = jnp.split(x @ w_in + b_in, 2, axis=-1)
    h = a * jax.nn.sigmoid(g)
    h = lax.conv_general_dilated(
        h, conv_w[:, None, :].astype(h.dtype), window_strides=(1,),
        padding=[(CONV_KERNEL - 1, 0)],
        dimension_numbers=("NWC", "WIO", "NWC"),
        feature_group_count=D_MODEL) + conv_b
    h = jax.nn.silu(layer_norm(h, ln_g, ln_b))
    return h @ w_out + b_out

def short_gated_conv(x, w_in, conv_w, w_out):
    S = x.shape[1]
    gate_b, gate_c, h = jnp.split(x @ w_in, 3, axis=-1)
    u = gate_c * h
    up = jnp.pad(u, ((0, 0), (SHORT_CONV - 1, 0), (0, 0)))
    conv = conv_w[0] * up[:, 0:S]
    for k in range(1, SHORT_CONV):
        conv = conv + conv_w[k] * up[:, k:k + S]
    return (gate_b * conv) @ w_out

def forgetting_attention(x, w_qkv, q_g, k_g, w_f, b_f, w_out):
    Bsz, S, _ = x.shape
    q, k, v = jnp.split(x @ w_qkv, 3, axis=-1)
    heads = lambda t: t.reshape(Bsz, S, FOX_HEADS, FOX_HEAD_DIM).transpose(0, 2, 1, 3)
    q = rms_norm(heads(q), q_g)
    k = rms_norm(heads(k), k_g)
    v = heads(v)
    log_f = jax.nn.log_sigmoid((x @ w_f + b_f).astype(jnp.float32))
    c = jnp.cumsum(log_f, axis=1).transpose(0, 2, 1)
    n_blk = S // Q_BLOCK
    qb = q.reshape(Bsz, FOX_HEADS, n_blk, Q_BLOCK, FOX_HEAD_DIM).transpose(2, 0, 1, 3, 4)
    cb = c.reshape(Bsz, FOX_HEADS, n_blk, Q_BLOCK).transpose(2, 0, 1, 3)
    starts = jnp.arange(n_blk, dtype=jnp.int32) * Q_BLOCK
    key_pos = jnp.arange(S, dtype=jnp.int32)
    scale = FOX_HEAD_DIM ** -0.5

    def block(args):
        q_i, c_i, start = args
        s = jnp.einsum("bhqd,bhkd->bhqk", q_i, k).astype(jnp.float32) * scale
        s = s + c_i[..., :, None] - c[:, :, None, :]
        q_pos = start + jnp.arange(Q_BLOCK, dtype=jnp.int32)
        s = jnp.where(key_pos[None, :] <= q_pos[:, None], s, -jnp.inf)
        p = jax.nn.softmax(s, axis=-1)
        return jnp.einsum("bhqk,bhkd->bhqd", p.astype(v.dtype), v)

    o = lax.map(block, (qb, cb, starts))
    o = o.transpose(1, 0, 3, 2, 4).reshape(Bsz, S, D_MODEL)
    return o @ w_out

def gated_linear_attention(x, w_in, w_g1, w_g2, b_g, o_g, w_out):
    Bsz, S, _ = x.shape
    q, k, v, r = jnp.split(x @ w_in, [GLA_DK, 2 * GLA_DK, 2 * GLA_DK + GLA_DV], axis=-1)
    log_a = jax.nn.log_sigmoid(((x @ w_g1) @ w_g2 + b_g).astype(jnp.float32)) / GLA_TAU
    nc = S // GLA_CHUNK

    def chunks(t, dh):
        return t.astype(jnp.float32).reshape(Bsz, nc, GLA_CHUNK, GLA_HEADS, dh).transpose(1, 0, 3, 2, 4)

    qc = chunks(q, GLA_DK_HEAD) * (GLA_DK_HEAD ** -0.5)
    kc = chunks(k, GLA_DK_HEAD)
    vc = chunks(v, GLA_DV_HEAD)
    b = jnp.cumsum(chunks(log_a, GLA_DK_HEAD), axis=-2)
    b_last = b[..., -1:, :]
    q_t = qc * jnp.exp(b)
    k_t = kc * jnp.exp(-b)
    k_dec = kc * jnp.exp(b_last - b)
    causal = jnp.tril(jnp.ones((GLA_CHUNK, GLA_CHUNK), dtype=bool))
    att = jnp.where(causal, jnp.einsum("nbhtd,nbhsd->nbhts", q_t, k_t), 0.0)
    o_intra = jnp.einsum("nbhts,nbhse->nbhte", att, vc)

    def step(state, inp):
        q_i, kd_i, v_i, dl_i = inp
        o_i = jnp.einsum("bhtd,bhde->bhte", q_i, state)
        state = state * jnp.exp(dl_i)[..., None] + jnp.einsum("bhsd,bhse->bhde", kd_i, v_i)
        return state, o_i

    s0 = jnp.zeros((Bsz, GLA_HEADS, GLA_DK_HEAD, GLA_DV_HEAD), jnp.float32)
    _, o_inter = lax.scan(step, s0, (q_t, k_dec, vc, b_last[..., 0, :]))
    o = rms_norm(o_intra + o_inter, o_g)
    o = o.transpose(1, 0, 3, 2, 4).reshape(Bsz, S, GLA_DV).astype(x.dtype)
    return (o * jax.nn.silu(r)) @ w_out

def squared_relu_mlp(x, w1, w2):
    return jnp.square(jax.nn.relu(x @ w1)) @ w2

def second_inputs(seed: int = 0) -> dict:
    key = jax.random.key(seed)
    ks = iter(jax.random.split(key, 40))
    f32 = jnp.float32

    def nrm(shape, scale):
        return jax.random.normal(next(ks), shape, f32) * scale

    def gain(shape):
        return 1.0 + nrm(shape, 0.05)

    nA, nB, nC, nD = (_layers_of(m) for m in range(N_MIXERS))
    D = D_MODEL
    return {
        "x": nrm((BATCH, SEQ, D), 1.0),
        "mix_norm": gain((DEPTH, D)),
        "mlp_norm": gain((DEPTH, D)),
        "mlp_w1": nrm((DEPTH, D, D_FF), D ** -0.5),
        "mlp_w2": nrm((DEPTH, D_FF, D), D_FF ** -0.5),
        "a_w_in": nrm((nA, D, 2 * D), D ** -0.5),
        "a_b_in": nrm((nA, 2 * D), 0.02),
        "a_conv_w": nrm((nA, CONV_KERNEL, D), CONV_KERNEL ** -0.5),
        "a_conv_b": nrm((nA, D), 0.02),
        "a_ln_g": gain((nA, D)),
        "a_ln_b": nrm((nA, D), 0.02),
        "a_w_out": nrm((nA, D, D), D ** -0.5),
        "a_b_out": nrm((nA, D), 0.02),
        "b_w_in": nrm((nB, D, 3 * D), D ** -0.5),
        "b_conv_w": nrm((nB, SHORT_CONV, D), SHORT_CONV ** -0.5),
        "b_w_out": nrm((nB, D, D), D ** -0.5),
        "c_w_qkv": nrm((nC, D, 3 * D), D ** -0.5),
        "c_q_norm": gain((nC, FOX_HEAD_DIM)),
        "c_k_norm": gain((nC, FOX_HEAD_DIM)),
        "c_w_f": nrm((nC, D, FOX_HEADS), 0.1 * D ** -0.5),
        "c_b_f": 2.0 + nrm((nC, FOX_HEADS), 1.0),
        "c_w_out": nrm((nC, D, D), D ** -0.5),
        "d_w_in": nrm((nD, D, 2 * GLA_DK + 2 * GLA_DV), D ** -0.5),
        "d_w_g1": nrm((nD, D, GLA_GATE_RANK), D ** -0.5),
        "d_w_g2": nrm((nD, GLA_GATE_RANK, GLA_DK), GLA_GATE_RANK ** -0.5),
        "d_b_g": nrm((nD, GLA_DK), 0.02),
        "d_o_norm": gain((nD, GLA_DV_HEAD)),
        "d_w_out": nrm((nD, GLA_DV, D), GLA_DV ** -0.5),
    }

def second_block(x, mix_norm, mlp_norm, mlp_w1, mlp_w2,
              a_w_in, a_b_in, a_conv_w, a_conv_b, a_ln_g, a_ln_b, a_w_out, a_b_out,
              b_w_in, b_conv_w, b_w_out,
              c_w_qkv, c_q_norm, c_k_norm, c_w_f, c_b_f, c_w_out,
              d_w_in, d_w_g1, d_w_g2, d_b_g, d_o_norm, d_w_out):
    for i in range(DEPTH):
        m, j = i % N_MIXERS, i // N_MIXERS
        h = rms_norm(x, mix_norm[i])
        if m == 0:
            y = conformer_conv(h, a_w_in[j], a_b_in[j], a_conv_w[j], a_conv_b[j],
                               a_ln_g[j], a_ln_b[j], a_w_out[j], a_b_out[j])
        elif m == 1:
            y = short_gated_conv(h, b_w_in[j], b_conv_w[j], b_w_out[j])
        elif m == 2:
            y = forgetting_attention(h, c_w_qkv[j], c_q_norm[j], c_k_norm[j],
                                     c_w_f[j], c_b_f[j], c_w_out[j])
        else:
            y = gated_linear_attention(h, d_w_in[j], d_w_g1[j], d_w_g2[j], d_b_g[j],
                                       d_o_norm[j], d_w_out[j])
        x = x + y
        x = x + squared_relu_mlp(rms_norm(x, mlp_norm[i]), mlp_w1[i], mlp_w2[i])
    return x


def setup_inputs(seed=0):
    out = dict(first_inputs(seed))
    for name, value in second_inputs(seed + 1).items():
        if name != "x":
            out[name + "_2"] = value
    return out


def reference(
    x, attn_norm_g, w_in, da_lambda_q1, da_lambda_k1, da_lambda_q2, da_lambda_k2, da_subln_g,
    w_out, ffn_norm_g, router_group_w, router_group_b, router_expert_w, router_expert_b,
    expert_w_gate, expert_w_up, expert_w_down, final_norm_g, mix_norm_2, mlp_norm_2, mlp_w1_2,
    mlp_w2_2, a_w_in_2, a_b_in_2, a_conv_w_2, a_conv_b_2, a_ln_g_2, a_ln_b_2, a_w_out_2,
    a_b_out_2, b_w_in_2, b_conv_w_2, b_w_out_2, c_w_qkv_2, c_q_norm_2, c_k_norm_2, c_w_f_2,
    c_b_f_2, c_w_out_2, d_w_in_2, d_w_g1_2, d_w_g2_2, d_b_g_2, d_o_norm_2, d_w_out_2,
):
    x = first_block(
        x, attn_norm_g, w_in, da_lambda_q1, da_lambda_k1, da_lambda_q2, da_lambda_k2,
        da_subln_g, w_out, ffn_norm_g, router_group_w, router_group_b, router_expert_w,
        router_expert_b, expert_w_gate, expert_w_up, expert_w_down, final_norm_g,
    )
    return second_block(
        x, mix_norm_2, mlp_norm_2, mlp_w1_2, mlp_w2_2, a_w_in_2, a_b_in_2, a_conv_w_2,
        a_conv_b_2, a_ln_g_2, a_ln_b_2, a_w_out_2, a_b_out_2, b_w_in_2, b_conv_w_2, b_w_out_2,
        c_w_qkv_2, c_q_norm_2, c_k_norm_2, c_w_f_2, c_b_f_2, c_w_out_2, d_w_in_2, d_w_g1_2,
        d_w_g2_2, d_b_g_2, d_o_norm_2, d_w_out_2,
    )


_drawn_inputs = setup_inputs


def setup_inputs(seed=0):
    import zlib

    import numpy as np

    out = dict(_drawn_inputs(seed))
    spreads = {}
    factors = {'da_lambda_q2': 8.0,
     'router_group_b': 4.538,
     'router_expert_b': 3.091,
     'a_b_in_2': 4.532,
     'a_ln_b_2': 5.151,
     'a_b_out_2': 3.086}
    for name, (base, spread) in spreads.items():
        noise = np.random.default_rng([zlib.crc32(name.encode()), seed]).standard_normal(out[name].shape)
        drawn = base * np.exp(spread * noise) if base else spread * noise
        out[name] = __import__('jax').numpy.asarray(drawn.astype(out[name].dtype))
    for name, factor in factors.items():
        out[name] = (out[name] * factor).astype(out[name].dtype)
    return out
```

```python
import math
from contextlib import ExitStack

import numpy as np
import concourse.bass as bass
from concourse import mybir

F32 = mybir.dt.float32
F16 = mybir.dt.float16
BF16 = mybir.dt.bfloat16
I32 = mybir.dt.int32
ALU = mybir.AluOpType
ACT = mybir.ActivationFunctionType
AX = mybir.AxisListType

P = 128
S = 1024
D = 1024
TT = S // P
KT = D // P
NH = 4
DH = 64
DV = 128
CHUNK = 64
EPS = 1e-6
NE = 32
NG = 4
EG = NE // NG
HID = 512
DFF = 4 * D
TAPS = 31
LAMBDA_INIT = 0.8 - 0.6 * math.exp(-0.3 * 0)
WS = 64.0
IWS = 1.0 / WS
UC = 512
UK = 4
SLOTS = 4
BLK_MAX = NE + 15
NOVER = BLK_MAX - NE
PAD = TAPS - 1

DENSE_A = 16
MOE_UNITS = 6 * NE
DENSE_B = 12 + 32


def constants():
    p = np.arange(P)
    slopes = 2.0 ** (-8.0 * np.arange(1, NH + 1) / NH)
    lg = np.log1p(-(2.0 ** (-5.0 - np.arange(NH))))
    rel = p[None, :] - p[:, None]
    by_bank = [0, 2, 1, 3]
    dec = np.where(rel[:, None, :] >= 0, np.exp(lg[None, :, None] * np.maximum(rel, 0)[:, None, :]), 0.0) * DH ** -0.5
    dec = dec[:, by_bank]
    kdec = np.repeat(np.exp(lg[None, :] * (P - 1 - p)[:, None]) * DH ** -0.5, DH, axis=1)
    head_of = lambda t: 2 * t + (p // DH)
    qdec = np.stack([np.where((p // DH == h % 2)[:, None], np.exp(lg[h] * (p + 1.0))[None, :], 0.0)
                     for h in range(NH)], axis=1)
    cdec = np.stack([np.repeat(np.exp(lg[head_of(t)] * P)[:, None], DV, axis=1) for t in range(2)], axis=1)
    ret = np.concatenate([dec.reshape(P, -1), kdec, qdec.reshape(P, -1), cdec.reshape(P, -1)], axis=1)
    ar = lambda n: np.tile(np.arange(n, dtype=np.float64), (P, 1))
    tok = np.arange(TT)[None, :] * P + p[:, None]
    misc = np.concatenate([np.eye(P), ar(P), ar(BLK_MAX + 1), NE - ar(NE), tok,
                           np.full((P, 1), EPS), np.ones((P, P))], axis=1)
    k, q = p[None, :], p[:, None]
    corr = np.stack([np.where(k // CHUNK > q // CHUNK, -1e30, np.where(k > q, -2.0 * s * (k - q), 0.0))
                     for s in slopes], axis=1)
    half = np.concatenate([np.eye(P), corr.reshape(P, -1), np.triu(np.ones((P, P)), 1), np.ones((P, P))],
                          axis=1).astype(np.float32)
    half = np.ascontiguousarray((half.view(np.uint32) >> 16).astype(np.uint16)).view(np.float32)
    pos_k = np.stack([np.arange(S) - (S - P), np.ones(S)])
    pos_q = np.stack([np.repeat(slopes, P), np.concatenate([-s * p for s in slopes])])
    pos = np.concatenate([pos_k, pos_q], axis=1).astype(np.float16)
    return {"c_ret": ret.astype(np.float32), "c_misc": misc.astype(np.float32), "c_half": half, "c_pos": pos}


RET_COLS = NH * P + NH * DH + NH * P + 2 * DV
M_ID, M_IO, M_IOB = 0, P, 2 * P
M_REV = M_IOB + BLK_MAX + 1
M_TOK = M_REV + NE
M_EPS = M_TOK + TT
M_ONE = M_EPS + 1
MISC_COLS = M_ONE + P


class Chain:

    def __init__(self, engine, sem, base=0):
        self.engine, self.sem, self.n, self.base = engine, sem, 0, base

    def done(self, instruction):
        self.n += 1
        instruction.then_inc(self.sem, 1)
        self.engine.wait_ge(self.sem, self.base + self.n)


def build(nc, a, out, stop=None):
    with ExitStack() as ctx:
        def sb(name, cols, dt=F32, rows=P):
            return ctx.enter_context(nc.sbuf_tensor(name, [rows, cols], dt))

        def sem(name):
            return ctx.enter_context(nc.semaphore(name))

        H = sb("resid", TT * D)[:, :].rearrange("p (t d) -> p t d", t=TT)
        XTF = sb("xt", 2 * KT * S // 2)
        XH = XTF[:, 0:4096].bitcast(F16).rearrange("p (k t) -> p k t", k=KT)
        XL = XTF[:, 4096:8192].bitcast(F16).rearrange("p (k t) -> p k t", k=KT)
        stage = sb("stage", SLOTS * UK * UC)
        split = sb("split", SLOTS * 2 * UK * UC, F16)
        AR = sb("arena", 12288)
        xn = sb("xn", 2 * D)[:, :].rearrange("p (b d) -> p b d", b=2)
        junk = sb("junk", D)
        gb = sb("gb", D)
        misc = sb("misc", MISC_COLS)
        halfw = sb("half", 7 * P // 2)
        Z = sb("zone", 2304)
        cols = sb("cols", 512)

        ident = misc[:, M_ID:M_ID + P]
        eps = misc[:, M_EPS:M_EPS + 1]
        half = halfw[:, :].bitcast(BF16)
        identb = half[:, 0:P]
        corr = half[:, P:P + NH * P].rearrange("p (h k) -> p h k", h=NH)
        tri = half[:, 5 * P:6 * P]
        onesb = half[:, 6 * P:7 * P]
        ret = Z[:, 0:RET_COLS]
        decT = ret[:, 0:512].rearrange("p (b c) -> p b c", b=2)
        kdec = ret[:, 512:768]
        qdec = ret[:, 768:1280].rearrange("p (t j c) -> p t j c", t=2, j=2)
        cdec = ret[:, 1280:1536]
        pos = Z[0:2, RET_COLS:RET_COLS + (S + NH * P) // 2].bitcast(F16)
        pos_k = pos[:, 0:S]
        pos_q = pos[:, S:S + NH * P].rearrange("p (h q) -> p h q", h=NH)

        ss = cols[:, 0:8]
        std = cols[:, 8:16]
        rstd = cols[:, 16:24]
        ss4, std4, rst4 = cols[:, 24:28], cols[:, 28:32], cols[:, 32:36]
        lsum, lexp, neglam = cols[:, 36:38], cols[:, 38:40], cols[:, 40:41]
        c1 = cols[:, 41:42]
        negmax, rows_sum, rows_rec = cols[:, 64:128], cols[:, 128:192], cols[:, 192:256]
        ssA, stdA, rstA = cols[:, 256:288], cols[:, 288:320], cols[:, 320:352]
        subg = cols[:, 384:512]
        wk = cols[:, 64:80].rearrange("p (k t) -> p k t", k=2)
        slot = cols[:, 80:96].bitcast(I32).rearrange("p (k t) -> p k t", k=2)
        tok_of = cols[:, 96:96 + BLK_MAX + 1].bitcast(I32)
        idx = [cols[:, 144 + i:145 + i].bitcast(I32) for i in range(2)]
        over_e = cols[0:1, 146:146 + NOVER + 1].bitcast(I32)
        n_over = cols[0:1, 162:163].bitcast(I32)

        rw = Z[:, 0:288]
        rwh = Z[:, 288:432].bitcast(F16)
        rwl = Z[:, 432:576].bitcast(F16)
        rb = Z[:, 576:612]
        gm = Z[:, 1280:2304]
        WORK = AR[:, 8192:12288]
        y = [AR[:, 8192 + 1024 * i:9216 + 1024 * i] for i in range(2)]
        hbuf = AR[:, 10240:10752]
        tbuf = AR[:, 10752:11264]
        sig = AR[:, 11264:11776]
        hTh = AR[:, 11776:12032].bitcast(F16).rearrange("p (k t) -> p k t", k=4)
        hTl = AR[:, 12032:12288].bitcast(F16).rearrange("p (k t) -> p k t", k=4)
        XG = [XTF[:, 1024 * i:1024 * i + 1024] for i in range(2)]
        xeh = [XTF[:, 2048 + 1024 * i:2560 + 1024 * i].bitcast(F16).rearrange("p (k t) -> p k t", k=KT)
               for i in range(2)]
        xel = [XTF[:, 2560 + 1024 * i:3072 + 1024 * i].bitcast(F16).rearrange("p (k t) -> p k t", k=KT)
               for i in range(2)]
        YG = [[AR[:, 2048 * i + 1024 * k:2048 * i + 1024 * k + 1024] for k in range(2)] for i in range(4)]
        XO, XOT = XTF[:, 4096:5120], XTF[:, 5120:6144]
        hO, hOT, sO = XTF[:, 6144:6656], XTF[:, 6656:7168], XTF[:, 7168:7680]
        wO = AR[:, 0:2048]
        cconv = Z[:, 0:288]
        cw = cconv[:, 0:248].rearrange("p (k j) -> p k j", k=KT)
        cb, lng, lnb, b_in = cconv[:, 248:256], cconv[:, 256:264], cconv[:, 264:272], cconv[:, 272:288]
        U = AR[:, 0:KT * (PAD + S)].rearrange("p (k t) -> p k t", k=KT)
        prod = [AR[:, 8448 + 1024 * i:9472 + 1024 * i] for i in range(3)]
        av = [junk[:, 512 * i:512 * i + 512] for i in range(2)]
        sv = [xn[:, 0, 512 * i:512 * i + 512] for i in range(2)]
        mean, rdev, var = xn[:, 0, :], xn[:, 1, :], junk[:, :]
        bo = AR[:, 0:1024]
        HTh = AR[:, 0:2048].bitcast(F16).rearrange("p (k t) -> p k t", k=4)
        HTl = AR[:, 2048:4096].bitcast(F16).rearrange("p (k t) -> p k t", k=4)
        relu = [AR[:, 4096 + 512 * i:4608 + 512 * i] for i in range(2)]
        relu2 = [AR[:, 5120 + 512 * i:5632 + 512 * i] for i in range(2)]
        gbj = [XTF[:, 0:1024], XTF[:, 1024:2048]]
        xn_rows = nc.dram_tensor("xn_rows", (S, D), F32, kind="Internal").ap()
        y_rows = nc.dram_tensor("y_rows", ((BLK_MAX + 1) * P, D), F32, kind="Internal").ap()
        x2_rows = nc.dram_tensor("x2_rows", (TT, P, D), F32, kind="Internal").ap()

        PS = ctx.enter_context(nc.psum_tensor("ps", [P, 4, 512], F32))
        PT = ctx.enter_context(nc.psum_tensor("pt", [P, 4, 512], F32))

        def tpair(par):
            return PT[:, 2 * par:2 * par + 2, :].rearrange("p b (k c) -> p (b k) c", k=4)

        def wstage(s):
            return stage[:, s * 2048:(s + 1) * 2048] if s < SLOTS else AR[:, (s - 4) * 2048:(s - 3) * 2048]

        def whi(s):
            if s < SLOTS:
                return split[:, s * 4096:s * 4096 + 2048]
            return AR[:, 4096 + (s - 4) * 2048:4096 + (s - 4) * 2048 + 1024].bitcast(F16)

        def wlo(s):
            if s < SLOTS:
                return split[:, s * 4096 + 2048:(s + 1) * 4096]
            return AR[:, 4096 + (s - 4) * 2048 + 1024:4096 + (s - 3) * 2048].bitcast(F16)

        QR = AR[:, 0:2048].rearrange("p (t s) -> p t s", t=2)
        KR = AR[:, 2048:4096].rearrange("p (t s) -> p t s", t=2)
        VR = AR[:, 4096:8192].rearrange("p (t v) -> p t v", t=TT)
        SG = AR[:, 8192:12288].rearrange("p (t v) -> p t v", t=TT)
        Q = AR[:, 0:4096].rearrange("p (h s) -> p h s", h=NH)
        K = AR[:, 4096:8192].rearrange("p (h s) -> p h s", h=NH)
        V = AR[:, 8192:12288].rearrange("p (t v) -> p t v", t=TT)

        s_const = sem("const_loaded")
        s_gain = sem("gain_loaded")
        s_x = [sem(f"x_loaded{i}") for i in range(TT)]
        s_wl = [sem(f"w_landed{i}") for i in range(6)]
        s_wh = [sem(f"w_hi{i}") for i in range(6)]
        s_wo = [sem(f"w_lo{i}") for i in range(6)]
        s_full = [sem(f"bank_full{i}") for i in range(4)]
        s_free = [sem(f"bank_free{i}") for i in range(4)]
        s_std = sem("norm_std")
        s_xn = sem("norm_xn")
        s_tr = sem("norm_transposed")
        s_xh = sem("xt_hi")
        s_xl = sem("xt_lo")
        s_dve = sem("dve_step")
        s_act = sem("act_step")
        s_sig = sem("gate_sigmoid")
        s_rsc = sem("ret_scores")
        s_rm = sem("ret_masked")
        s_rst = sem("ret_state")
        s_ro = sem("ret_out")
        s_rss = sem("ret_std")
        s_rmix = sem("ret_mix")
        s_lam = sem("lambda")
        s_as = sem("att_scores")
        s_amx = sem("att_max")
        s_ae = sem("att_exp")
        s_aa = sem("att_mixed")
        s_at = sem("att_transposed")
        s_aea = sem("att_t_act")
        s_aed = sem("att_t_dve")
        s_ao = sem("att_out")
        s_aoe = sem("att_out_read")
        s_router_w = sem("router_loaded")
        s_rws = sem("router_split")
        s_xs = [sem(f"xn_stored{i}") for i in range(2)]
        s_lg = sem("logits")
        s_rt = sem("router_ready")
        s_rp = sem("router_products")
        s_rx = sem("router_exp")
        s_rd = sem("router_diff")
        s_slots = sem("slots_known")
        s_gx = [sem(f"x_gathered{i}") for i in range(2)]
        s_zero = sem("zero_tile")
        s_cleared = sem("overflow_rows_cleared")
        s_ix = sem("index_column")
        s_ixw = sem("index_column_seen")
        s_xt = sem("x_transposed")
        s_xeh = sem("x_hi")
        s_xel = sem("x_lo")
        s_g = sem("gate_done")
        s_u = sem("up_done")
        s_es = sem("expert_sigmoid")
        s_t = sem("gate_silu")
        s_h = sem("hidden")
        s_ht = sem("hidden_transposed")
        s_hh = sem("hidden_hi")
        s_hl = sem("hidden_lo")
        s_d = [sem(f"down_done{i}") for i in range(2)]
        s_y = [sem(f"y_half{i}") for i in range(2)]
        s_ys = [sem(f"y_stored{i}") for i in range(2)]
        s_yg = [sem(f"y_gathered{i}") for i in range(4)]
        s_cmb = sem("combined")
        s_x2 = sem("second_input")
        s_x2s = sem("second_input_stored")
        s_ox = sem("over_rows_gathered")
        s_oix = sem("over_index_column")
        s_oixw = sem("over_index_seen")
        s_ow = sem("over_unit_landed")
        s_ou = sem("over_unit_used")
        s_ot = sem("over_transposed")
        s_oc = sem("over_copied")
        s_os = sem("over_sigmoid")
        s_og = sem("over_silu")
        s_oh = sem("over_hidden")
        s_oy = sem("over_output")
        s_oys = sem("over_stored")
        s_tab = sem("conv_tables_loaded")
        s_pad = sem("conv_pad")
        s_av = sem("conv_gate")
        s_cu = sem("conv_input")
        s_pr = sem("conv_product")
        s_ca = sem("conv_added")
        s_cd = sem("conv_dve")
        s_c0 = sem("conv_first_tap")
        s_sq = sem("conv_squares")
        s_st = sem("conv_stats")
        s_va = sem("conv_var")
        s_rd2 = sem("conv_dev")
        s_z = sem("conv_normed")
        s_si = sem("conv_silu")
        s_ch = sem("conv_hi")
        s_cl = sem("conv_lo")
        s_bo = sem("bias_loaded")
        s_relu = sem("mlp_relu")
        s_mh = sem("mlp_hi")
        s_ml = sem("mlp_lo")
        s_out = sem("out_stored")

        block = ctx.enter_context(nc.Block())

        def load_unit(eng, n):
            s, r = n % SLOTS, n // SLOTS
            if r:
                eng.wait_ge(s_wh[s], r)
                eng.wait_ge(s_wo[s], r)
            eng.dma_start(wstage(s), a["w_dense_a"][n]).then_inc(s_wl[s], 16)

        def split_hi(act, n):
            s, r = n % SLOTS, n // SLOTS
            act.wait_ge(s_wl[s], 16 * (r + 1))
            if r:
                g = last_group(n - SLOTS)
                act.wait_ge(s_full[g % 4], g // 4 + 1)
            nc.scalar.activation(whi(s), wstage(s), ACT.Copy, scale=WS).then_inc(s_wh[s], 1)

        def split_lo(dve, n):
            s, r = n % SLOTS, n // SLOTS
            dve.wait_ge(s_wh[s], r + 1)
            nc.vector.scalar_tensor_tensor(out=wlo(s), in0=wstage(s), scalar=WS, in1=whi(s),
                                           op0=ALU.mult, op1=ALU.subtract).then_inc(s_wo[s], 1)

        def product(pe, out_ap, lh, ll, rh, rl, start, stop):
            nc.tensor.matmul(out_ap, lh, rh, start=start, stop=False)
            nc.tensor.matmul(out_ap, lh, rl, start=False, stop=False)
            return nc.tensor.matmul(out_ap, ll, rh, start=False, stop=stop)

        def last_group(n):
            return 8 * (n // 2) + 7 if n < 12 else 62 + (n - 12) // 2

        def group(pe, g, units, feature_major, ft, tk):
            if g >= 4:
                pe.wait_ge(s_free[g % 4], g // 4)
            for ui, n in enumerate(units):
                s, r = n % SLOTS, n // SLOTS
                pe.wait_ge(s_wo[s], r + 1)
                for kk in range(UK):
                    k = ui * UK + kk
                    if feature_major:
                        c = slice(kk * UC + ft * P, kk * UC + ft * P + P)
                        t = slice(tk * 512, tk * 512 + 512)
                        i = product(pe, PS[:, g % 4, :], whi(s)[:, c], wlo(s)[:, c], XH[:, k, t], XL[:, k, t],
                                    k == 0, k == KT - 1)
                    else:
                        c = slice(kk * UC, kk * UC + UC)
                        t = slice(tk * P, tk * P + P)
                        i = product(pe, PS[:, g % 4, :], XH[:, k, t], XL[:, k, t], whi(s)[:, c], wlo(s)[:, c],
                                    k == 0, k == KT - 1)
            i.then_inc(s_full[g % 4], 1)
            return i

        def norm_stats(act, ch, t):
            ch.done(nc.scalar.activation(junk[:, :], H[:, t, :], ACT.Square, accum_out=ss[:, t:t + 1]))
            nc.scalar.activation(std[:, t:t + 1], ss[:, t:t + 1], ACT.Sqrt, bias=eps, scale=1.0 / D)\
                .then_inc(s_std, 1)

        def xn_wait(dve, r, t):
            n = TT * r + t
            if n >= 2:
                dve.wait_ge(s_tr, n - 1)

        def norm_scale(dve, ch, r, t, nstd):
            dve.wait_ge(s_std, nstd)
            ch.done(nc.vector.reciprocal(rstd[:, t:t + 1], std[:, t:t + 1]))
            xn_wait(dve, r, t)
            nc.vector.scalar_tensor_tensor(out=xn[:, t % 2, :], in0=H[:, t, :], scalar=rstd[:, t:t + 1],
                                           in1=gb[:, :], op0=ALU.mult, op1=ALU.mult).then_inc(s_xn, 1)

        def transposes(pe, r, t, src):
            n = TT * r + t
            pe.wait_ge(s_xn, n + 1)
            if n >= 2:
                pe.wait_ge(s_xl, n - 1)
            for k in range(KT):
                i = nc.tensor.transpose(tpair(t % 2)[:, k, :], src(t, k), ident)
            i.then_inc(s_tr, 1)

        def xt_hi(act, r, t):
            act.wait_ge(s_tr, TT * r + t + 1)
            nc.scalar.activation(XH[:, :, t * P:(t + 1) * P], tpair(t % 2), ACT.Copy).then_inc(s_xh, 1)

        def xt_lo(dve, r, t):
            dve.wait_ge(s_xh, TT * r + t + 1)
            nc.vector.tensor_tensor(XL[:, :, t * P:(t + 1) * P], tpair(t % 2), XH[:, :, t * P:(t + 1) * P],
                                    ALU.subtract).then_inc(s_xl, 1)

        FM = [True, False, False, True, True, False]

        def chunk_groups(c):
            if FM[c]:
                return [(8 * c + 2 * ft + th, ft, th) for ft in range(4) for th in range(2)]
            return [(8 * c + t, 0, t) for t in range(TT)]

        def chunk_dest(c, ft, tk):
            tok = slice(tk * 512, tk * 512 + 512)
            return [lambda: (QR if ft < 2 else KR)[:, ft % 2, tok], lambda: VR[:, tk, :], lambda: SG[:, tk, :],
                    lambda: Q[:, ft, tok], lambda: K[:, ft, tok], lambda: V[:, tk, :]][c]()

        CHUNK_SCALE = [IWS, IWS, IWS, IWS * DH ** -0.5, IWS, IWS]
        NB = NH * TT

        def aT(par):
            return XTF[:, 4096 + par * 1024:4096 + (par + 1) * 1024].rearrange("p (k q) -> p k q", k=KT)

        def PB(par, m):
            return XTF[:, (2 * par + m) * 1024:(2 * par + m + 1) * 1024]

        def SC(m):
            return PS[:, 2 * m:2 * m + 2, :].rearrange("p b c -> p (b c)")

        sT = [xn[:, 0, 0:512], xn[:, 0, 512:1024]]
        qd = [xn[:, 1, 0:512], xn[:, 1, 512:1024]]
        ktok = [junk[:, 256:512], junk[:, 512:768]]
        state = junk[:, 0:256]

        BASE = [4, 4, 4, 4, 0, 0]
        FIRST_PAIRS = [(0, True, False), (NE // 2 - 1, False, True)]

        def expert_load(sp, kind, e):
            s0 = {"up": 0, "gate": 2, "down": 4}[kind]
            for i in range(2):
                s = s0 + i
                if not (isinstance(e, int) and BASE[s] + e == 0):
                    sp.wait_ge(s_wh[s], BASE[s] + e)
                    sp.wait_ge(s_wo[s], BASE[s] + e)
                src = a["w_" + kind][bass.ds(2 * e + i, 1), :, :].rearrange("o p c -> (o p) c")
                sp.dma_start(wstage(s), src).then_inc(s_wl[s], 16)

        def expert_hi(act, s, e):
            act.wait_ge(s_wl[s], 16 * (BASE[s] + 1) + 16 * e)
            if not (isinstance(e, int) and e == 0):
                act.wait_ge([s_u, s_u, s_g, s_g, s_d[0], s_d[1]][s], e)
            nc.scalar.activation(whi(s), wstage(s), ACT.Copy, scale=WS).then_inc(s_wh[s], 1)

        def expert_lo(dve, s, e):
            dve.wait_ge(s_wh[s], BASE[s] + 1 + e)
            nc.vector.scalar_tensor_tensor(out=wlo(s), in0=wstage(s), scalar=WS, in1=whi(s),
                                           op0=ALU.mult, op1=ALU.subtract).then_inc(s_wo[s], 1)

        def expert_product(pe, bank, s0, e, lh, ll, done):
            for i in range(2):
                s = s0 + i
                pe.wait_ge(s_wo[s], BASE[s] + 1 + e)
                for kk in range(UK):
                    k, c = i * UK + kk, slice(kk * UC, kk * UC + UC)
                    m = product(pe, bank, lh[:, k, :], ll[:, k, :], whi(s)[:, c], wlo(s)[:, c], k == 0, k == KT - 1)
            m.then_inc(done, 1)

        def overflow(eng, body):
            eng.wait_ge(s_slots, 1)
            n = eng.value_load(n_over, min_val=0, max_val=NOVER)
            with eng.If(n > 0):
                with eng.Fori(0, NOVER) as j:
                    with eng.If(j < n):
                        body(j)

        RB = BASE[0] + NE

        def load_b(sp, m):
            s, r = m % SLOTS, RB + m // SLOTS
            sp.wait_ge(s_wh[s], r)
            sp.wait_ge(s_wo[s], r)
            sp.dma_start(wstage(s), a["w_dense_b"][m]).then_inc(s_wl[s], 16)

        def last_group_b(m):
            return 79 + 16 * (m // 4) if m < 8 else 110 + (m - 8) // 2

        def hi_b(act, m):
            s, r = m % SLOTS, RB + m // SLOTS
            act.wait_ge(s_wl[s], 16 * (r + 1))
            if m >= SLOTS:
                g = last_group_b(m - SLOTS)
                act.wait_ge(s_full[g % 4], g // 4 + 1)
            nc.scalar.activation(whi(s), wstage(s), ACT.Copy, scale=WS).then_inc(s_wh[s], 1)

        def lo_b(dve, m):
            s, r = m % SLOTS, RB + m // SLOTS
            dve.wait_ge(s_wh[s], r + 1)
            nc.vector.scalar_tensor_tensor(out=wlo(s), in0=wstage(s), scalar=WS, in1=whi(s),
                                           op0=ALU.mult, op1=ALU.subtract).then_inc(s_wo[s], 1)

        def group_b(pe, g, units, feature_major, ft, tk):
            pe.wait_ge(s_free[g % 4], g // 4)
            for ui, m in enumerate(units):
                s, r = m % SLOTS, RB + m // SLOTS
                pe.wait_ge(s_wo[s], r + 1)
                for kk in range(UK):
                    k = ui * UK + kk
                    if feature_major:
                        c = slice(kk * UC + ft * P, kk * UC + ft * P + P)
                        t = slice(tk * 512, tk * 512 + 512)
                        i = product(pe, PS[:, g % 4, :], whi(s)[:, c], wlo(s)[:, c], XH[:, k, t], XL[:, k, t],
                                    k == 0, k == KT - 1)
                    else:
                        c = slice(kk * UC, kk * UC + UC)
                        t = slice(tk * P, tk * P + P)
                        i = product(pe, PS[:, g % 4, :], XH[:, k, t], XL[:, k, t], whi(s)[:, c], wlo(s)[:, c],
                                    k == 0, k == KT - 1)
            i.then_inc(s_full[g % 4], 1)

        RM = RB + 3
        G_MLP = 112 // 4
        NC = DFF // UC
        CONV_DVE, CONV_ACT = [(0, 1), (2, 4), (5,)], [3, 6, 7]
        CONV_DONE = [0, 1, 3, 2, 4, 6, 5, 7]

        def mlp_hi(act, s, c):
            act.wait_ge(s_wl[s], 16 * (RM + 1) + 16 * c)
            nc.scalar.activation(whi(s), wstage(s), ACT.Copy, scale=WS).then_inc(s_wh[s], 1)

        def mlp_lo(dve, s, c):
            dve.wait_ge(s_wh[s], RM + 1 + c)
            nc.vector.scalar_tensor_tensor(out=wlo(s), in0=wstage(s), scalar=WS, in1=whi(s),
                                           op0=ALU.mult, op1=ALU.subtract).then_inc(s_wo[s], 1)

        def mlp_chunks(eng, body):
            with eng.Fori(0, NC - 1) as c:
                body(c, False)
            body(NC - 1, True)

        def taps(k, u_of):
            return [(k, j) for j in range(TAPS)]

        def conv_wait(eng, k):
            if k in CONV_ACT:
                eng.wait_ge(s_ca, (TAPS - 1) * (CONV_ACT.index(k) + 1))
            else:
                eng.wait_ge(s_cd, [0, 1, 2, 4, 5].index(k) + 1)

        def SQ(i):
            return gbj[i % 2]

        def pairs(body, eng):
            for q in range(2):
                body(q, q, True, False)
            with eng.Fori(1, NE // 2 - 1) as k:
                for q in range(2):
                    body(2 * k + q, q, False, False)
            for q in range(2):
                body(NE - 2 + q, q, False, True)

        def first_dev(u):
            return max(1, 2 * u)

        def second_dev(u):
            return 2 * u + 3 if u < TT - 1 else 2 * TT

        off = [0]

        def work(n, *shape):
            v = WORK[:, off[0]:off[0] + n]
            off[0] += n
            if len(shape) == 2:
                return v.rearrange("p (a b) -> p a b", a=shape[0])
            if len(shape) == 3:
                return v.rearrange("p (a b c) -> p a b c", a=shape[0], b=shape[1])
            return v

        BIG = 1e38
        rL = work(TT * 36, TT, 36)
        rG, rE = rL[:, :, 0:NG], rL[:, :, NG:NG + NE]
        rgm, rgx = work(TT), work(TT)
        rgo = work(TT * NG, TT, NG)
        rex = work(TT * NG, TT, NG)
        rEm = work(TT * NE, TT, NE)
        rtmp = work(TT * NE, TT, NE)
        roh = [work(TT * NE, TT, NE) for _ in range(2)]
        rm = [work(TT), work(TT)]
        rix = work(2 * TT, 2, TT)
        rde, rgs = work(TT), work(TT)
        rM = work(TT * NE // 2).bitcast(BF16).rearrange("p (t e) -> p t e", t=TT)
        rex_t = work(1)
        rcmp = work(NE)
        rexb = work(P // 2).bitcast(BF16)
        rthr = work(8)
        rrank, rbq, rst_ = work(2 * TT, 2, TT), work(2 * TT, 2, TT), work(2 * TT, 2, TT)
        rblk, rpos, rv = work(2 * TT, 2, TT), work(2 * TT, 2, TT), work(2 * TT, 2, TT)
        rc7 = work(2 * TT * 7, 2 * TT, 7)
        rinc = work(NE)
        rov = work((NOVER + 1) * NE, NOVER + 1, NE)
        rbe = work(NOVER + 1)
        off[0] = 2700
        rA = work(2 * TT * P // 2).bitcast(F16).rearrange("p (n c) -> p n c", n=2 * TT)
        rB = junk[:, 0:TT * (BLK_MAX + 1)].bitcast(F16).rearrange("p (n c) -> p n c", n=2 * TT)

        def bc(ap, n):
            return ap.unsqueeze(2).to_broadcast([P, ap.shape[1], n])

        def router(dve, ch):
            V_ = nc.vector
            io, iob = misc[:, M_IO:M_IO + P], misc[:, M_IOB:M_IOB + BLK_MAX + 1]
            rev = misc[:, M_REV:M_REV + NE]
            tok = misc[:, M_TOK:M_TOK + TT]
            dve.wait_ge(s_lg, 1)
            ch.done(V_.scalar_tensor_tensor(
                out=rL, in0=PS[:, 0, 0:TT * 36].rearrange("p (t c) -> p t c", t=TT), scalar=IWS,
                in1=rb.unsqueeze(1).to_broadcast([P, TT, 36]), op0=ALU.mult, op1=ALU.add))
            ch.done(V_.tensor_reduce(rgm, rG, AX.X, ALU.max))
            ch.done(V_.tensor_tensor(rex, rG, bc(rgm, NG), ALU.subtract))
            V_.tensor_scalar(rgo, rex, 0.0, None, ALU.is_ge).then_inc(s_rd, 1)
            dve.wait_ge(s_rd, 1)
            ch.done(V_.tensor_tensor(rgo, rgo, rev[:, NE - NG:NE].unsqueeze(1).to_broadcast([P, TT, NG]), ALU.mult))
            ch.done(V_.tensor_reduce(rgx, rgo, AX.X, ALU.max))
            ch.done(V_.tensor_tensor(rgo, rgo, bc(rgx, NG), ALU.is_equal))
            r4 = lambda v: v.rearrange("p t (g e) -> p (t g) e", g=NG)
            go = rgo.rearrange("p t g -> p (t g)")
            rE4 = [rE[:, :, g * EG:(g + 1) * EG] for g in range(NG)]
            for g in range(NG):
                V_.tensor_tensor(rEm[:, :, g * EG:(g + 1) * EG], rE4[g], bc(rgo[:, :, g], EG), ALU.mult)
            ch.done(V_.tensor_scalar(rtmp[:, :, 0:NG], rgo, BIG, -BIG, ALU.mult, ALU.add))
            for g in range(NG):
                part = rEm[:, :, g * EG:(g + 1) * EG]
                i = V_.tensor_tensor(part, part, bc(rtmp[:, :, g], EG), ALU.add)
            ch.done(i)
            for k in range(2):
                if k:
                    ch.done(V_.scalar_tensor_tensor(out=rEm, in0=roh[0], scalar=-BIG, in1=rEm,
                                                    op0=ALU.mult, op1=ALU.add))
                ch.done(V_.tensor_reduce(rm[k], rEm, AX.X, ALU.max))
                ch.done(V_.tensor_tensor(roh[k], rEm, bc(rm[k], NE), ALU.is_ge))
                ch.done(V_.tensor_tensor(roh[k], roh[k], rev.unsqueeze(1).to_broadcast([P, TT, NE]), ALU.mult))
                ch.done(V_.tensor_reduce(rix[:, k, :], roh[k], AX.X, ALU.max))
                ch.done(V_.tensor_tensor(roh[k], roh[k], bc(rix[:, k, :], NE), ALU.is_equal))
            V_.tensor_tensor(rde, rm[1], rm[0], ALU.subtract).then_inc(s_rd, 1)
            ch.done(V_.tensor_scalar(rix, rix, -1.0, float(NE), ALU.mult, ALU.add))
            V_.tensor_tensor(rM, roh[0], roh[1], ALU.add).then_inc(s_rt, 1)
            dve.wait_ge(s_rx, 2)
            ch.done(V_.tensor_reduce(rgs, rex, AX.X, ALU.add))
            ch.done(V_.tensor_scalar(rm[0], rde, 1.0, None, ALU.add))
            ch.done(V_.tensor_tensor(rgs, rgs, rm[0], ALU.mult))
            ch.done(V_.reciprocal(wk[:, 0, :], rgs))
            ch.done(V_.tensor_tensor(wk[:, 1, :], wk[:, 0, :], rde, ALU.mult))
            dve.wait_ge(s_rp, 1)
            ch.done(V_.tensor_copy(rex_t[0:NE, :], PS[0:NE, 2, 0:1]))
            ch.done(V_.tensor_scalar(rcmp[0:NE, 0:7], io[0:NE, 1:8], float(P), rex_t[0:NE, :], ALU.mult, ALU.is_lt))
            ch.done(V_.tensor_reduce(rex_t[0:NE, :], rcmp[0:NE, 0:7], AX.X, ALU.add))
            V_.tensor_scalar(rexb[0:NE, :], misc[0:NE, M_ONE:M_ONE + P], rex_t[0:NE, :], None, ALU.mult)\
                .then_inc(s_rt, 1)
            for k in range(2):
                ch.done(V_.tensor_tensor(rtmp, PS[:, 1, 0:TT * NE].rearrange("p (t e) -> p t e", t=TT), roh[k],
                                         ALU.mult))
                ch.done(V_.tensor_reduce(rrank[:, k, :], rtmp, AX.X, ALU.add))
            ch.done(V_.tensor_scalar(rthr[:, 0:7], io[:, 1:8], float(P), None, ALU.mult))
            rank = rrank.rearrange("p k t -> p (k t)")
            ch.done(V_.tensor_tensor(rc7, bc(rank, 7), rthr[:, 0:7].unsqueeze(1).to_broadcast([P, 2 * TT, 7]),
                                     ALU.is_ge))
            ch.done(V_.tensor_reduce(rbq.rearrange("p k t -> p (k t)"), rc7, AX.X, ALU.add))
            ch.done(V_.scalar_tensor_tensor(out=rpos, in0=rbq, scalar=-float(P), in1=rrank,
                                            op0=ALU.mult, op1=ALU.add))
            dve.wait_ge(s_rp, 2)
            for k in range(2):
                ch.done(V_.tensor_tensor(rtmp, PS[:, 3, 0:NE].unsqueeze(1).to_broadcast([P, TT, NE]), roh[k],
                                         ALU.mult))
                ch.done(V_.tensor_reduce(rst_[:, k, :], rtmp, AX.X, ALU.add))
            ch.done(V_.tensor_copy(rinc, PS[:, 3, NE:2 * NE]))
            ch.done(V_.tensor_tensor(rv, rst_, rbq, ALU.add))
            ch.done(V_.tensor_tensor(rv, rv, rix, ALU.subtract))
            ch.done(V_.tensor_scalar(rblk, rbq, 0.0, None, ALU.is_gt))
            ch.done(V_.scalar_tensor_tensor(out=rv, in0=rv, scalar=float(NE - 1), in1=rblk,
                                            op0=ALU.add, op1=ALU.mult))
            ch.done(V_.tensor_tensor(rblk, rv, rix, ALU.add))
            V_.scalar_tensor_tensor(out=slot, in0=rblk, scalar=float(P), in1=rpos, op0=ALU.mult, op1=ALU.add)
            V_.tensor_tensor(rA, io.unsqueeze(1).to_broadcast([P, 2 * TT, P]),
                             bc(rpos.rearrange("p k t -> p (k t)"), P), ALU.is_equal)
            ch.done(V_.tensor_tensor(rB, iob.unsqueeze(1).to_broadcast([P, 2 * TT, BLK_MAX + 1]),
                                     bc(rblk.rearrange("p k t -> p (k t)"), BLK_MAX + 1), ALU.is_equal))
            for k in range(2):
                i = V_.tensor_tensor(rB[:, k * TT:(k + 1) * TT, :], rB[:, k * TT:(k + 1) * TT, :],
                                     bc(tok, BLK_MAX + 1), ALU.mult)
            i.then_inc(s_rt, 1)
            ch.done(V_.tensor_tensor(rov[0:1], rinc[0:1, :].unsqueeze(1).to_broadcast([1, NOVER + 1, NE]),
                                     iob[0:1, 0:NOVER + 1].unsqueeze(2).to_broadcast([1, NOVER + 1, NE]),
                                     ALU.is_le))
            ch.done(V_.tensor_reduce(rbe[0:1, :], rov[0:1], AX.X, ALU.add))
            V_.tensor_scalar(over_e, rbe[0:1, :], float(NE - 1), None, ALU.min)
            V_.tensor_copy(n_over, rinc[0:1, NE - 1:NE])
            dve.wait_ge(s_rp, 3)
            V_.tensor_copy(tok_of, PS[:, 0, 0:BLK_MAX + 1]).then_inc(s_slots, 1)

        @block.sync
        def _(sp):
            for t in range(TT):
                sp.dma_start(H[:, t, :], a["x"][t]).then_inc(s_x[t], 16)
                if t == 0:
                    sp.dma_start(gb[:, :], a["gains"][0:1, :].to_broadcast([P, D])).then_inc(s_gain, 16)
                    sp.dma_start(misc[:, :], a["c_misc"]).then_inc(s_const, 16)
            for n in range(2):
                load_unit(sp, n)
            sp.dma_start(halfw[:, :], a["c_half"]).then_inc(s_const, 16)
            sp.dma_start(ret, a["c_ret"]).then_inc(s_const, 16)
            sp.dma_start(pos, a["c_pos"]).then_inc(s_const, 16)
            sp.dma_start(subg, a["subln_g"].to_broadcast([P, DV])).then_inc(s_const, 16)
            for j in range(4):
                sp.dma_start(junk[:, j * DH:(j + 1) * DH], a["lambdas"][j:j + 1, :].to_broadcast([P, DH]))\
                    .then_inc(s_const, 16)
            for n in range(2, DENSE_A):
                load_unit(sp, n)
            for t in range(TT):
                sp.wait_ge(s_tr, TT + t + 1)
                sp.dma_start(H[:, t, :], a["x"][t]).then_inc(s_x[t], 16)
            sp.dma_start(rw, a["router_w"]).then_inc(s_router_w, 16)
            sp.dma_start(rb, a["router_b"].to_broadcast([P, NG + NE])).then_inc(s_router_w, 16)
            sp.dma_start(gb[:, :], a["gains"][1:2, :].to_broadcast([P, D])).then_inc(s_gain, 16)

            expert_load(sp, "gate", 0)

            def body(e, q, first, last):
                expert_load(sp, "up", e)
                if not (last and q):
                    expert_load(sp, "gate", e + 1)
                expert_load(sp, "down", e)

            pairs(body, sp)

            def over(j):
                e = sp.value_load(over_e[:, bass.ds(j, 1)], min_val=0, max_val=NE - 1)
                for i in range(2):
                    sp.wait_ge(s_wh[4 + i], NE)
                    sp.wait_ge(s_wo[4 + i], NE)
                for u in range(6):
                    w = a[("w_gate", "w_up", "w_down")[u // 2]]
                    sp.wait_ge(s_ou, 6 * j + u)
                    sp.dma_start(wO, w[bass.ds(2 * e + u % 2, 1), :, :].rearrange("o p c -> (o p) c"))\
                        .then_inc(s_ow, 16)

            overflow(sp, over)
            sp.wait_ge(s_tr, 3 * TT)
            sp.wait_ge(s_xn, 3 * TT)
            sp.dma_start(gb[:, :], a["gains"][2:3, :].to_broadcast([P, D])).then_inc(s_gain, 16)
            sp.dma_start(gm, a["gains"][3:4, :].to_broadcast([P, D])).then_inc(s_gain, 16)
            for m in range(SLOTS):
                load_b(sp, m)
            sp.dma_start(cconv, a["conv_tables"]).then_inc(s_tab, 16)
            for t in range(TT):
                sp.wait_ge(s_x2, t + 1)
                sp.dma_start(x2_rows[t], H[:, t, :]).then_inc(s_x2s, 16)
            for m in range(SLOTS, 12):
                load_b(sp, m)
            sp.wait_ge(s_st, 1)
            sp.dma_start(bo, a["gains"][5:6, :].to_broadcast([P, D])).then_inc(s_bo, 16)
            sp.dma_start(gb[:, :], a["gains"][4:5, :].to_broadcast([P, D])).then_inc(s_gain, 16)
            sp.wait_ge(s_x2s, 16 * TT)
            for t in range(TT):
                sp.wait_ge(s_cl, t + 1)
                sp.dma_start(H[:, t, :], x2_rows[t]).then_inc(s_x[t], 16)

            def body(c, last):
                for s in range(SLOTS):
                    sp.wait_ge(s_wh[s], RM + c)
                    sp.wait_ge(s_wo[s], RM + c)
                    src = a["w_mlp"][bass.ds(SLOTS * c + s, 1), :, :].rearrange("o p c -> (o p) c")
                    sp.dma_start(wstage(s), src).then_inc(s_wl[s], 16)

            mlp_chunks(sp, body)
            for t in range(TT):
                for n in range(2):
                    j = 8 + 2 * t + n
                    sp.wait_ge(s_free[j % 4], G_MLP + 6 * (NC - 1) + j // 4 + 1)
                sp.dma_start(out[t * P:(t + 1) * P, :], H[:, t, :]).then_inc(s_out, 16)
            sp.wait_ge(s_out, 16 * TT)

        @block.gpsimd
        def _(pool):
            zero = AR[:, 11264:12288]
            nc.gpsimd.memset(zero, 0.0).then_inc(s_zero, 1)
            pool.wait_ge(s_zero, 1)
            for b in range(NE, BLK_MAX + 1):
                pool.dma_start(y_rows[b * P:(b + 1) * P, :], zero).then_inc(s_cleared, 16)
            for t in range(TT):
                pool.wait_ge(s_xn, 2 * TT + t + 1)
                pool.dma_start(xn_rows[t * P:(t + 1) * P, :], xn[:, t % 2, :]).then_inc(s_xs[t % 2], 16)
            for i in range(2):
                pool.wait_ge(s_xs[i], 16 * TT // 2)
            pool.wait_ge(s_slots, 1)
            pool.wait_ge(s_tr, 3 * TT)

            def gather(e, q):
                nc.gpsimd.tensor_copy(idx[q], tok_of[:, bass.ds(e, 1)]).then_inc(s_ix, 1)
                pool.wait_ge(s_ix, e + 1)
                pool.sem_inc(s_ixw, 1)
                pool.indirect_dma_start(out=XG[q], out_offset=None, in_=xn_rows,
                                        in_offset=bass.IndirectOffsetOnAxis(ap=idx[q], axis=0))\
                    .then_inc(s_gx[q], 16)

            def store(e, q):
                pool.wait_ge(s_y[0], e + 1)
                pool.wait_ge(s_y[1], e + 1)
                dst = y_rows[bass.ds(e * P, P), :]
                pool.dma_start(dst, y[q]).then_inc(s_ys[q], 16)

            gather(0, 0)
            gather(1, 1)
            pool.wait_ge(s_xt, 1)
            pool.wait_ge(s_gx[0], 16)
            gather(2, 0)

            def body(e, q, first, last):
                if not last:
                    pool.wait_ge(s_xt, e + 2)
                    gather(e + 3, 1 - q)
                if not (first and q == 0):
                    store(e - 1, 1 - q)

            pairs(body, pool)
            store(NE - 1, 1)
            for i in range(2):
                pool.wait_ge(s_ys[i], 16 * NE // 2)
            pool.wait_ge(s_gx[0], 16 * (NE // 2 + 1))

            def over(j):
                nc.gpsimd.tensor_copy(idx[0], tok_of[:, bass.ds(j + NE, 1)]).then_inc(s_oix, 1)
                pool.wait_ge(s_oix, j + 1)
                pool.sem_inc(s_oixw, 1)
                pool.indirect_dma_start(out=XO, out_offset=None, in_=xn_rows,
                                        in_offset=bass.IndirectOffsetOnAxis(ap=idx[0], axis=0)).then_inc(s_ox, 16)
                pool.wait_ge(s_oy, j + 1)
                pool.dma_start(y_rows[bass.ds((j + NE) * P, P), :], y[0]).then_inc(s_oys, 16)
                pool.wait_ge(s_oys, 16 * j + 16)
                pool.sem_inc(s_oixw, 1)

            overflow(pool, over)
            for t in range(TT):
                if t >= 4:
                    pool.wait_ge(s_cmb, 2 * (t - 3))
                for k in range(2):
                    pool.indirect_dma_start(out=YG[t % 4][k], out_offset=None, in_=y_rows,
                                            in_offset=bass.IndirectOffsetOnAxis(ap=slot[:, k, t:t + 1], axis=0))\
                        .then_inc(s_yg[t % 4], 16)
            pool.wait_ge(s_cmb, 2 * TT)
            nc.gpsimd.memset(U[:, :, 0:PAD], 0.0).then_inc(s_pad, 1)
            n = 0
            for i, k in enumerate(CONV_ACT):
                pool.wait_ge(s_c0, i + 1)
                for j in range(1, TAPS):
                    n += 1
                    pool.wait_ge(s_pr, n)
                    if j > 1:
                        pool.wait_ge(s_ca, n - 1)
                    nc.gpsimd.tensor_tensor(H[:, k, :], H[:, k, :], prod[n % 3], ALU.add).then_inc(s_ca, 1)

        @block.scalar
        def _(act):
            ch = Chain(act, s_act)
            act.wait_ge(s_const, 16 * 9)
            act.wait_ge(s_lam, 1)
            ch.done(nc.scalar.activation(lexp, lsum, ACT.Exp))
            for t in range(TT + 1):
                if t < TT:
                    act.wait_ge(s_x[t], 16)
                    norm_stats(act, ch, t)
                if t:
                    xt_hi(act, 0, t - 1)
                if t in (1, 2, 3, 4):
                    split_hi(act, t - 1)

            def chunk(c):
                for g, ft, tk in chunk_groups(c):
                    if c == 2:
                        act.wait_ge(s_full[g % 4], g // 4 + 1)
                        if tk >= 2:
                            act.wait_ge(s_free[(g - 2) % 4], (g - 2) // 4 + 1)
                        nc.scalar.activation(xn[:, 0, (tk % 2) * 512:(tk % 2) * 512 + 512], PS[:, g % 4, :],
                                             ACT.Sigmoid, scale=IWS).then_inc(s_sig, 1)
                    elif g % 2 == 0:
                        act.wait_ge(s_full[g % 4], g // 4 + 1)
                        nc.scalar.activation(chunk_dest(c, ft, tk), PS[:, g % 4, :], ACT.Copy,
                                             scale=CHUNK_SCALE[c]).then_inc(s_free[g % 4], 1)
                for n in (2 * c + 4, 2 * c + 5):
                    split_hi(act, n)

            for c in range(3):
                chunk(c)
            for n in range(TT):
                act.wait_ge(s_ro, n + 1)
                if n:
                    act.wait_ge(s_rmix, n)
                for h in range(NH):
                    i = nc.scalar.activation(gb[:, h * DV:(h + 1) * DV],
                                             PT[:, 2 + n % 2, h * DV:(h + 1) * DV], ACT.Square,
                                             accum_out=ss4[:, h:h + 1])
                ch.done(i)
                nc.scalar.activation(std4, ss4, ACT.Sqrt, bias=eps, scale=1.0 / DV).then_inc(s_rss, 1)
            for c in range(3, 6):
                chunk(c)

            def t_evac(b):
                i, par = b % TT, b % 2
                act.wait_ge(s_at, b + 1)
                if b >= 2:
                    act.wait_ge(s_ao, b - 1)
                n = min(4, i + 1)
                nc.scalar.activation(aT(par)[:, 0:n, :], tpair(0)[:, 0:n, :], ACT.Copy).then_inc(s_aea, 1)

            def o_evac(b):
                h, i = b // TT, b % TT
                act.wait_ge(s_ao, b + 1)
                nc.scalar.activation(H[:, i, h * DV:(h + 1) * DV], PT[:, 2 + b % 2, 0:DV], ACT.Copy)
                nc.scalar.activation(gb[:, b % 8 * DV:b % 8 * DV + DV], PT[:, 2 + b % 2, 0:DV],
                                     ACT.Square, accum_out=ssA[:, b:b + 1]).then_inc(s_aoe, 1)

            for b in range(NB + 2):
                if b < NB:
                    W = P * (b % TT + 1)
                    for m in range(2):
                        act.wait_ge(s_amx, 2 * b + m + 1)
                        if b >= 2:
                            act.wait_ge(s_at, b - 1)
                        nc.scalar.activation(PB(b % 2, m)[:, 0:W], SC(m)[:, 0:W], ACT.Exp,
                                             bias=negmax[:, 2 * b + m:2 * b + m + 1],
                                             accum_out=rows_sum[:, 2 * b + m:2 * b + m + 1]).then_inc(s_ae, 1)
                if 1 <= b <= NB:
                    t_evac(b - 1)
                if b >= 2:
                    o_evac(b - 2)
            act.wait_ge(s_aoe, NB)
            nc.scalar.activation(stdA, ssA, ACT.Sqrt, bias=eps, scale=1.0 / DV).then_inc(s_std, 1)
            for t in range(TT):
                xt_hi(act, 1, t)
            for t in range(TT + 2):
                if t < TT:
                    g = 49 + 2 * t
                    act.wait_ge(s_free[g % 4], g // 4 + 1)
                    act.wait_ge(s_free[(g - 1) % 4], (g - 1) // 4 + 1)
                    norm_stats(act, ch, t)
                if t >= 2:
                    xt_hi(act, 2, t - 2)
            act.wait_ge(s_rd, 1)
            nc.scalar.activation(rex, rex, ACT.Exp).then_inc(s_rx, 1)
            act.wait_ge(s_rd, 2)
            nc.scalar.activation(rde, rde, ACT.Exp).then_inc(s_rx, 1)
            for g in range(60, 64):
                act.wait_ge(s_full[g % 4], 16)

            for i in range(2):
                expert_hi(act, 2 + i, 0)
            for i in range(2):
                expert_hi(act, i, 0)

            def xe_hi(e, q):
                act.wait_ge(s_xt, e + 1)
                nc.scalar.activation(xeh[q], tpair(0), ACT.Copy).then_inc(s_xeh, 1)

            for q in range(2):
                xe_hi(q, q)
            for i in range(2):
                expert_hi(act, 4 + i, 0)
            for i in range(2):
                expert_hi(act, 2 + i, 1)

            def body(e, q, first, last):
                act.wait_ge(s_g, e + 1)
                if not (first and q == 0):
                    act.wait_ge(s_t, e)
                nc.scalar.activation(sig, PS[:, q, :], ACT.Sigmoid, scale=IWS).then_inc(s_es, 1)
                if not (last and q):
                    for s in (0, 1):
                        expert_hi(act, s, e + 1)
                act.wait_ge(s_ht, e + 1)
                nc.scalar.activation(hTh, PS[:, 3, :].rearrange("p (k t) -> p k t", k=4), ACT.Copy)\
                    .then_inc(s_hh, 1)
                if not last:
                    xe_hi(e + 2, q)
                    for s in (2, 3):
                        expert_hi(act, s, e + 2)
                act.wait_ge(s_d[0], e + 1)
                if not (first):
                    act.wait_ge(s_ys[q], 8 * e if q == 0 else 8 * (e - 1))
                nc.scalar.activation(y[q][:, 0:512], PT[:, 2, :], ACT.Copy, scale=IWS).then_inc(s_y[0], 1)
                if not (last and q):
                    for s in (4, 5):
                        expert_hi(act, s, e + 1)

            pairs(body, act)

            def over(j):
                act.wait_ge(s_ot, 2 * j + 1)
                nc.scalar.activation(XOT.rearrange("p (k t) -> p k t", k=KT), tpair(0), ACT.Copy).then_inc(s_oc, 1)
                act.wait_ge(s_ou, 6 * j + 2)
                nc.scalar.activation(sO, PS[:, 0, :], ACT.Sigmoid).then_inc(s_os, 1)
                act.wait_ge(s_ot, 2 * j + 2)
                nc.scalar.activation(hOT, PS[:, 3, :], ACT.Copy).then_inc(s_oc, 1)
                act.wait_ge(s_ou, 6 * j + 6)
                act.wait_ge(s_ys[0], 16 * NE // 2)
                act.wait_ge(s_oys, 16 * j)
                nc.scalar.activation(y[0], PT[:, 2:4, :].rearrange("p b c -> p (b c)"), ACT.Copy).then_inc(s_oy, 1)

            overflow(act, over)
            for m in range(SLOTS):
                if m == 0:
                    act.wait_ge(s_u, NE)
                    act.wait_ge(s_g, NE)
                hi_b(act, m)
            for t in range(TT + 2):
                if t < TT:
                    act.wait_ge(s_cmb, 2 * t + 2)
                    norm_stats(act, ch, t)
                if 1 <= t <= TT:
                    act.wait_ge(s_x2, t)
                    norm_stats(act, ch, t - 1)
                if t >= 2:
                    xt_hi(act, 3, t - 2)
            act.wait_ge(s_tab, 16)

            def gated(p):
                hf, ft, th = p // 8, p % 8 // 2, p % 2
                k = 4 * hf + ft
                if p >= 2:
                    act.wait_ge(s_cu, p - 1)
                for g, dst, fn, bias in ((64 + 2 * p, av[p % 2], ACT.Identity, b_in[:, k:k + 1]),
                                         (65 + 2 * p, sv[p % 2], ACT.Sigmoid, b_in[:, 8 + k:9 + k])):
                    act.wait_ge(s_full[g % 4], g // 4 + 1)
                    i = nc.scalar.activation(dst, PS[:, g % 4, :], fn, bias=bias, scale=IWS)
                    i.then_inc(s_free[g % 4], 1)

            n = [0]

            def product_tap(i, j):
                k = CONV_ACT[i]
                if j == 0:
                    act.wait_ge(s_cu, 2 * k + 2)
                    act.wait_ge(s_pad, 1)
                    act.wait_ge(s_x2s, 16 * TT)
                    act.wait_ge(s_xn, 4 * TT)
                    nc.scalar.activation(H[:, k, :], U[:, k, 0:S], ACT.Identity, bias=cb[:, k:k + 1],
                                         scale=cw[:, k, 0:1]).then_inc(s_c0, 1)
                    return
                n[0] += 1
                if n[0] > 3:
                    act.wait_ge(s_ca, n[0] - 3)
                nc.scalar.activation(prod[n[0] % 3], U[:, k, j:j + S], ACT.Identity, scale=cw[:, k, j:j + 1])\
                    .then_inc(s_pr, 1)

            todo = [(i, j) for i in range(len(CONV_ACT)) for j in range(TAPS)]
            for p in range(16):
                if p == 8:
                    for m in range(4, 8):
                        hi_b(act, m)
                gated(p)
                if 8 <= p < 15:
                    for _ in range(4):
                        if todo and todo[0][0] == 0:
                            product_tap(*todo.pop(0))
            for m in range(8, 12):
                hi_b(act, m)
            done_sq = [0]

            def squares():
                k = CONV_DONE[done_sq[0]]
                conv_wait(act, k)
                if done_sq[0] >= 2:
                    act.wait_ge(s_st, done_sq[0] - 1)
                nc.scalar.activation(SQ(done_sq[0]), H[:, k, :], ACT.Square).then_inc(s_sq, 1)
                done_sq[0] += 1

            while todo:
                product_tap(*todo.pop(0))
                if todo and todo[0] == (1, 10):
                    squares(), squares(), squares()
                if todo and todo[0] == (2, 20):
                    squares(), squares()
            while done_sq[0] < KT:
                squares()
            act.wait_ge(s_va, 1)
            nc.scalar.activation(rdev, var, ACT.Sqrt, bias=eps, scale=1.0).then_inc(s_rd2, 1)
            for k in range(KT + 1):
                if k < KT:
                    act.wait_ge(s_z, k + 1)
                    if k >= 3:
                        act.wait_ge(s_cl, k - 2)
                    nc.scalar.activation(prod[k % 3], H[:, k, :], ACT.Silu, bias=lnb[:, k:k + 1],
                                         scale=lng[:, k:k + 1]).then_inc(s_si, 1)
                if k:
                    act.wait_ge(s_si, k)
                    nc.scalar.activation(XH[:, k - 1, :], prod[(k - 1) % 3], ACT.Copy).then_inc(s_ch, 1)
            for t in range(TT + 2):
                if t < TT:
                    g = 97 + 2 * t
                    act.wait_ge(s_free[g % 4], g // 4 + 1)
                    act.wait_ge(s_free[(g - 1) % 4], (g - 1) // 4 + 1)
                    norm_stats(act, ch, t)
                if t >= 2:
                    xt_hi(act, 4, t - 2)
            for s in range(SLOTS):
                mlp_hi(act, s, 0)

            def body(c, last):
                for j in range(9):
                    if j < 8:
                        act.wait_ge(s_full[j % 4], G_MLP + 6 * c + j // 4 + 1)
                        if j >= 2:
                            act.wait_ge(s_ml, 8 * c + j - 1)
                        elif not (isinstance(c, int) and c == 0):
                            act.wait_ge(s_ml, 8 * c + j - 1 + (1 if j == 0 else 0))
                        nc.scalar.activation(relu[j % 2], PS[:, j % 4, :], ACT.Relu, scale=IWS)\
                            .then_inc(s_free[j % 4], 1)
                    if j:
                        h = j - 1
                        act.wait_ge(s_free[h % 4], G_MLP + 6 * c + h // 4 + 1)
                        nc.scalar.activation(HTh[:, h % 4, (h // 4) * 512:(h // 4) * 512 + 512], relu[h % 2],
                                             ACT.Square).then_inc(s_mh, 1)
                if not last:
                    for s in (0, 1):
                        act.wait_ge(s_full[3], G_MLP + 6 * c + 2)
                        mlp_hi(act, s, c + 1)
                    for s in (2, 3):
                        act.wait_ge(s_full[3], G_MLP + 6 * c + 6)
                        act.wait_ge(s_full[2], G_MLP + 6 * c + 6)
                        mlp_hi(act, s, c + 1)

            mlp_chunks(act, body)

        @block.vector
        def _(dve):
            ch = Chain(dve, s_dve)
            dve.wait_ge(s_const, 16 * 9)
            lam = junk[:, 0:256].rearrange("p (j d) -> p j d", j=4)
            dot = junk[:, 256:384].rearrange("p (j d) -> p j d", j=2)
            for j in range(2):
                ch.done(nc.vector.tensor_tensor(dot[:, j, :], lam[:, 2 * j, :], lam[:, 2 * j + 1, :], ALU.mult))
            nc.vector.tensor_reduce(lsum, dot, AX.X, ALU.add).then_inc(s_lam, 1)
            dve.wait_ge(s_act, 1)
            ch.done(nc.vector.tensor_tensor(neglam, lexp[:, 1:2], lexp[:, 0:1], ALU.subtract))
            ch.done(nc.vector.tensor_scalar(neglam, neglam, LAMBDA_INIT, None, ALU.subtract))
            ch.done(nc.vector.tensor_scalar(subg, subg, 1.0 - LAMBDA_INIT, None, ALU.mult))
            dve.wait_ge(s_gain, 16)
            for t in range(TT + 1):
                if t < TT:
                    norm_scale(dve, ch, 0, t, t + 1)
                if t:
                    xt_lo(dve, 0, t - 1)
                if t in (1, 2, 3, 4):
                    split_lo(dve, t - 1)

            def chunk(c):
                for g, ft, tk in chunk_groups(c):
                    if c == 2:
                        dve.wait_ge(s_sig, tk + 1)
                        nc.vector.scalar_tensor_tensor(
                            out=chunk_dest(c, ft, tk), in0=PS[:, g % 4, :], scalar=IWS,
                            in1=xn[:, 0, (tk % 2) * 512:(tk % 2) * 512 + 512], op0=ALU.mult, op1=ALU.mult)\
                            .then_inc(s_free[g % 4], 1)
                    elif g % 2 == 1:
                        dve.wait_ge(s_full[g % 4], g // 4 + 1)
                        nc.vector.tensor_scalar(chunk_dest(c, ft, tk), PS[:, g % 4, :], CHUNK_SCALE[c], None,
                                                ALU.mult).then_inc(s_free[g % 4], 1)
                for n in (2 * c + 4, 2 * c + 5):
                    split_lo(dve, n)

            for c in range(3):
                if c == 2:
                    dve.wait_ge(s_cleared, 16 * (NOVER + 1))
                chunk(c)

            def masked(n):
                par, blk = n % 2, slice(n * P, (n + 1) * P)
                dve.wait_ge(s_rsc, n + 1)
                if n >= 2:
                    dve.wait_ge(s_ro, n - 1)
                nc.vector.tensor_tensor(sT[par].rearrange("p (b c) -> p b c", b=2),
                                        PS[:, 2 * par:2 * par + 2, 0:256], decT, ALU.mult)
                nc.vector.tensor_tensor(ktok[par], PT[:, par, 0:256], kdec, ALU.mult)
                for t in range(2):
                    i = nc.vector.tensor_tensor(
                        qd[par][:, t * 256:t * 256 + 256].rearrange("p (j c) -> p j c", j=2),
                        QR[:, t:t + 1, blk].to_broadcast([P, 2, P]), qdec[:, t, :, :], ALU.mult)
                i.then_inc(s_rm, 1)

            def update(n):
                dve.wait_ge(s_ro, n + 1)
                if n == 0:
                    nc.vector.tensor_copy(state, PT[:, n % 2, 256:512]).then_inc(s_rst, 1)
                else:
                    ch.done(nc.vector.tensor_tensor(state, state, cdec, ALU.mult))
                    nc.vector.tensor_tensor(state, PT[:, n % 2, 256:512], state, ALU.add).then_inc(s_rst, 1)

            def mix(n):
                dve.wait_ge(s_rss, n + 1)
                ch.done(nc.vector.reciprocal(rst4, std4))
                for h in range(NH):
                    hs = slice(h * DV, (h + 1) * DV)
                    i = nc.vector.scalar_tensor_tensor(
                        out=H[:, n, 512 + h * DV:512 + (h + 1) * DV], in0=PT[:, 2 + n % 2, hs],
                        scalar=rst4[:, h:h + 1], in1=SG[:, n, hs], op0=ALU.mult, op1=ALU.mult)
                i.then_inc(s_rmix, 1)

            for n in range(TT + 1):
                if n < TT:
                    masked(n)
                if n:
                    update(n - 1)
                    mix(n - 1)
            for c in range(3, 6):
                chunk(c)

            for b in range(NB + 1):
                if b < NB:
                    W = P * (b % TT + 1)
                    for m in range(2):
                        dve.wait_ge(s_as, 2 * b + m + 1)
                        nc.vector.tensor_reduce(negmax[:, 2 * b + m:2 * b + m + 1], SC(m)[:, 0:W], AX.X, ALU.max,
                                                negate=True).then_inc(s_amx, 1)
                if b:
                    q, i = b - 1, (b - 1) % TT
                    W = P * (i + 1)
                    dve.wait_ge(s_ae, 2 * q + 2)
                    ch.done(nc.vector.reciprocal(rows_rec[:, 2 * q:2 * q + 2], rows_sum[:, 2 * q:2 * q + 2]))
                    ch.done(nc.vector.tensor_tensor(c1, rows_rec[:, 2 * q + 1:2 * q + 2], neglam, ALU.mult))
                    p0, p1 = PB(q % 2, 0)[:, 0:W], PB(q % 2, 1)[:, 0:W]
                    ch.done(nc.vector.tensor_scalar(p1, p1, c1, None, ALU.mult))
                    nc.vector.scalar_tensor_tensor(out=p0, in0=p0, scalar=rows_rec[:, 2 * q:2 * q + 1], in1=p1,
                                                   op0=ALU.mult, op1=ALU.add).then_inc(s_aa, 1)
                    if i >= 4:
                        dve.wait_ge(s_at, q + 1)
                        if q >= 2:
                            dve.wait_ge(s_ao, q - 1)
                        nc.vector.tensor_copy(aT(q % 2)[:, 4:i + 1, :], tpair(0)[:, 4:i + 1, :])\
                            .then_inc(s_aed, 1)
            dve.wait_ge(s_std, TT + 1)
            ch.done(nc.vector.reciprocal(rstA, stdA))
            dve.wait_ge(s_rmix, TT)
            for t in range(TT + 1):
                if t < TT:
                    xn_wait(dve, 1, t)
                    for h in range(NH):
                        hs = slice(h * DV, (h + 1) * DV)
                        i = nc.vector.scalar_tensor_tensor(
                            out=xn[:, t % 2, hs], in0=H[:, t, hs], scalar=rstA[:, h * TT + t:h * TT + t + 1],
                            in1=subg, op0=ALU.mult, op1=ALU.mult)
                    i.then_inc(s_xn, 1)
                if t:
                    xt_lo(dve, 1, t - 1)
            dve.wait_ge(s_router_w, 32)
            ch.done(nc.vector.tensor_scalar(rwh, rw, WS, None, ALU.mult))
            nc.vector.scalar_tensor_tensor(out=rwl, in0=rw, scalar=WS, in1=rwh, op0=ALU.mult, op1=ALU.subtract)\
                .then_inc(s_rws, 1)
            dve.wait_ge(s_gain, 32)
            for t in range(TT + 2):
                if t < TT:
                    dve.wait_ge(s_x[t], 32)
                    for c in range(2):
                        g = 48 + 2 * t + c
                        dve.wait_ge(s_full[g % 4], g // 4 + 1)
                        nc.vector.scalar_tensor_tensor(out=H[:, t, c * 512:c * 512 + 512], in0=PS[:, g % 4, :],
                                                       scalar=IWS, in1=H[:, t, c * 512:c * 512 + 512],
                                                       op0=ALU.mult, op1=ALU.add).then_inc(s_free[g % 4], 1)
                if 1 <= t <= TT:
                    if t >= 3:
                        dve.wait_ge(s_xs[(t - 1) % 2], 16 * ((t - 1) // 2))
                    norm_scale(dve, ch, 2, t - 1, TT + 1 + t)
                if t >= 2:
                    xt_lo(dve, 2, t - 2)
            router(dve, ch)

            for i in range(2):
                expert_lo(dve, 2 + i, 0)
            for i in range(2):
                expert_lo(dve, i, 0)

            def xe_lo(e, q):
                dve.wait_ge(s_xeh, e + 1)
                nc.vector.tensor_tensor(xel[q], tpair(0), xeh[q], ALU.subtract).then_inc(s_xel, 1)

            for q in range(2):
                xe_lo(q, q)
            for i in range(2):
                expert_lo(dve, 4 + i, 0)
            for i in range(2):
                expert_lo(dve, 2 + i, 1)

            def body(e, q, first, last):
                dve.wait_ge(s_es, e + 1)
                nc.vector.scalar_tensor_tensor(out=tbuf, in0=PS[:, q, :], scalar=IWS, in1=sig,
                                               op0=ALU.mult, op1=ALU.mult).then_inc(s_t, 1)
                dve.wait_ge(s_u, e + 1)
                dve.wait_ge(s_t, e + 1)
                if not (first and q == 0):
                    dve.wait_ge(s_ht, e)
                nc.vector.scalar_tensor_tensor(out=hbuf, in0=PS[:, 2, :], scalar=IWS, in1=tbuf,
                                               op0=ALU.mult, op1=ALU.mult).then_inc(s_h, 1)
                if not (last and q):
                    for s in (0, 1):
                        expert_lo(dve, s, e + 1)
                dve.wait_ge(s_hh, e + 1)
                nc.vector.tensor_tensor(hTl, PS[:, 3, :].rearrange("p (k t) -> p k t", k=4), hTh, ALU.subtract)\
                    .then_inc(s_hl, 1)
                if not last:
                    xe_lo(e + 2, q)
                    for s in (2, 3):
                        expert_lo(dve, s, e + 2)
                dve.wait_ge(s_d[1], e + 1)
                if not (first):
                    dve.wait_ge(s_ys[q], 8 * e if q == 0 else 8 * (e - 1))
                nc.vector.tensor_scalar(y[q][:, 512:1024], PT[:, 3, :], IWS, None, ALU.mult).then_inc(s_y[1], 1)
                if not (last and q):
                    for s in (4, 5):
                        expert_lo(dve, s, e + 1)

            pairs(body, dve)

            def over(j):
                dve.wait_ge(s_os, j + 1)
                nc.vector.tensor_tensor(sO, PS[:, 0, :], sO, ALU.mult).then_inc(s_og, 1)
                dve.wait_ge(s_og, j + 1)
                dve.wait_ge(s_ou, 6 * j + 4)
                nc.vector.tensor_tensor(hO, PS[:, 1, :], sO, ALU.mult).then_inc(s_oh, 1)

            overflow(dve, over)
            for m in range(SLOTS):
                lo_b(dve, m)
            dve.wait_ge(s_gain, 64)
            for t in range(TT + 3):
                if t < TT:
                    dve.wait_ge(s_yg[t % 4], 32 * (t // 4 + 1))
                    for k in range(2):
                        nc.vector.scalar_tensor_tensor(out=H[:, t, :], in0=YG[t % 4][k], scalar=wk[:, k, t:t + 1],
                                                       in1=H[:, t, :], op0=ALU.mult, op1=ALU.add).then_inc(s_cmb, 1)
                        dve.wait_ge(s_cmb, 2 * t + k + 1)
                if 1 <= t <= TT:
                    u = t - 1
                    dve.wait_ge(s_std, 2 * TT + 1 + first_dev(u))
                    ch.done(nc.vector.reciprocal(rstd[:, u:u + 1], std[:, u:u + 1]))
                    nc.vector.scalar_tensor_tensor(out=H[:, u, :], in0=H[:, u, :], scalar=rstd[:, u:u + 1],
                                                   in1=gb[:, :], op0=ALU.mult, op1=ALU.mult).then_inc(s_x2, 1)
                if 2 <= t <= TT + 1:
                    u = t - 2
                    dve.wait_ge(s_std, 2 * TT + 1 + second_dev(u))
                    ch.done(nc.vector.reciprocal(rstd[:, u:u + 1], std[:, u:u + 1]))
                    xn_wait(dve, 3, u)
                    nc.vector.scalar_tensor_tensor(out=xn[:, u % 2, :], in0=H[:, u, :], scalar=rstd[:, u:u + 1],
                                                   in1=gm, op0=ALU.mult, op1=ALU.mult).then_inc(s_xn, 1)
                if t >= 3:
                    xt_lo(dve, 3, t - 3)

            def conv_taps(ks):
                for j in range(TAPS):
                    for k in ks:
                        yield ks, k, j

            steps = [x for ks in CONV_DVE for x in conv_taps(ks)]
            nw = [0]
            last_of = {}

            def tap():
                ks, k, j = steps.pop(0)
                if j == 0:
                    dve.wait_ge(s_cu, 2 * k + 2)
                    if not last_of:
                        dve.wait_ge(s_pad, 1)
                        dve.wait_ge(s_x2s, 16 * TT)
                    i = nc.vector.tensor_scalar(H[:, k, :], U[:, k, 0:S], cw[:, k, 0:1], cb[:, k:k + 1],
                                                ALU.mult, ALU.add)
                else:
                    dve.wait_ge(s_dve, last_of[k])
                    i = nc.vector.scalar_tensor_tensor(out=H[:, k, :], in0=U[:, k, j:j + S], scalar=cw[:, k, j:j + 1],
                                                       in1=H[:, k, :], op0=ALU.mult, op1=ALU.add)
                if j == TAPS - 1:
                    i.then_inc(s_cd, 1)
                else:
                    i.then_inc(s_dve, 1)
                    ch.n += 1
                    last_of[k] = ch.n

            for p in range(16):
                k, th = 4 * (p // 8) + p % 8 // 2, p % 2
                g = 65 + 2 * p
                if p == 8:
                    for m in range(4, 8):
                        lo_b(dve, m)
                dve.wait_ge(s_free[g % 4], g // 4 + 1)
                dve.wait_ge(s_free[(g - 1) % 4], (g - 1) // 4 + 1)
                nc.vector.tensor_tensor(U[:, k, PAD + th * 512:PAD + th * 512 + 512], av[p % 2], sv[p % 2], ALU.mult)\
                    .then_inc(s_cu, 1)
                if 8 <= p < 15:
                    for _ in range(7):
                        if steps[0][1] < 2:
                            tap()
            for m in range(8, 12):
                lo_b(dve, m)
            while steps:
                tap()
            dve.wait_ge(s_st, KT)
            s1 = PS[:, 0:2, :].rearrange("p b c -> p (b c)")
            s2 = PS[:, 2:4, :].rearrange("p b c -> p (b c)")
            ch.done(nc.vector.tensor_scalar(mean, s1, 1.0 / D, None, ALU.mult))
            ch.done(nc.vector.tensor_tensor(var, mean, mean, ALU.mult))
            nc.vector.scalar_tensor_tensor(out=var, in0=s2, scalar=1.0 / D, in1=var, op0=ALU.mult, op1=ALU.subtract)\
                .then_inc(s_va, 1)
            dve.wait_ge(s_rd2, 1)
            ch.done(nc.vector.reciprocal(rdev, rdev))
            for k in range(KT + 2):
                if k < KT:
                    ch.done(nc.vector.tensor_tensor(H[:, k, :], H[:, k, :], mean, ALU.subtract))
                    nc.vector.tensor_tensor(H[:, k, :], H[:, k, :], rdev, ALU.mult).then_inc(s_z, 1)
                if k >= 2:
                    dve.wait_ge(s_ch, k - 1)
                    nc.vector.tensor_tensor(XL[:, k - 2, :], prod[(k - 2) % 3], XH[:, k - 2, :], ALU.subtract)\
                        .then_inc(s_cl, 1)
            dve.wait_ge(s_bo, 16)
            dve.wait_ge(s_gain, 80)
            for t in range(TT + 2):
                if t < TT:
                    dve.wait_ge(s_x[t], 48)
                    ch.done(nc.vector.tensor_tensor(H[:, t, :], H[:, t, :], bo, ALU.add))
                    for c in range(2):
                        g = 96 + 2 * t + c
                        dve.wait_ge(s_full[g % 4], g // 4 + 1)
                        nc.vector.scalar_tensor_tensor(out=H[:, t, c * 512:c * 512 + 512], in0=PS[:, g % 4, :],
                                                       scalar=IWS, in1=H[:, t, c * 512:c * 512 + 512],
                                                       op0=ALU.mult, op1=ALU.add).then_inc(s_free[g % 4], 1)
                if 1 <= t <= TT:
                    norm_scale(dve, ch, 4, t - 1, 4 * TT + 1 + t)
                if t >= 2:
                    xt_lo(dve, 4, t - 2)
            for s in range(SLOTS):
                mlp_lo(dve, s, 0)

            def body(c, last):
                for j in range(9):
                    if j < 8:
                        dve.wait_ge(s_free[j % 4], G_MLP + 6 * c + j // 4 + 1)
                        nc.vector.tensor_tensor(relu2[j % 2], relu[j % 2], relu[j % 2], ALU.mult).then_inc(s_relu, 1)
                    if j:
                        h = j - 1
                        dve.wait_ge(s_mh, 8 * c + j)
                        dve.wait_ge(s_relu, 8 * c + j)
                        nc.vector.tensor_tensor(HTl[:, h % 4, (h // 4) * 512:(h // 4) * 512 + 512], relu2[h % 2],
                                                HTh[:, h % 4, (h // 4) * 512:(h // 4) * 512 + 512], ALU.subtract)\
                            .then_inc(s_ml, 1)
                if not last:
                    for s in (0, 1):
                        mlp_lo(dve, s, c + 1)
                for j in range(8, 24):
                    t, n = (j - 8) // 2, j % 2
                    hs = slice(n * 512, n * 512 + 512)
                    dve.wait_ge(s_full[j % 4], G_MLP + 6 * c + j // 4 + 1)
                    nc.vector.scalar_tensor_tensor(out=H[:, t, hs], in0=PS[:, j % 4, :], scalar=IWS, in1=H[:, t, hs],
                                                   op0=ALU.mult, op1=ALU.add).then_inc(s_free[j % 4], 1)
                if not last:
                    for s in (2, 3):
                        mlp_lo(dve, s, c + 1)

            mlp_chunks(dve, body)

        @block.tensor
        def _(pe):
            pe.wait_ge(s_const, 16 * 9)
            for t in range(TT):
                transposes(pe, 0, t, lambda t, k: xn[:, t % 2, k * P:(k + 1) * P])
            pe.wait_ge(s_xl, TT)

            def chunk(c):
                gs = chunk_groups(c)
                for g, ft, tk in gs:
                    group(pe, g, (2 * c, 2 * c + 1), FM[c], ft, tk)

            for c in range(3):
                chunk(c)
            for b in range(4):
                pe.wait_ge(s_free[b], 6)

            def scores(n):
                par, blk = n % 2, slice(n * P, (n + 1) * P)
                if n >= 2:
                    pe.wait_ge(s_rm, n - 1)
                    pe.wait_ge(s_rst, n - 1)
                for h in range(NH):
                    t, r = h // 2, slice(DH * (h % 2), DH * (h % 2) + DH)
                    nc.tensor.matmul(PS[:, 2 * par + h % 2, t * P:(t + 1) * P], KR[r, t, blk], QR[r, t, blk],
                                     start=True, stop=True)
                for t in range(2):
                    i = nc.tensor.transpose(PT[:, par, t * P:(t + 1) * P], KR[:, t, blk], ident)
                i.then_inc(s_rsc, 1)

            def outputs(n):
                par = n % 2
                pe.wait_ge(s_rm, n + 1)
                if n:
                    pe.wait_ge(s_rst, n)
                for h in range(NH):
                    t, r0 = h // 2, DH * (h % 2)
                    nc.tensor.matmul(PT[r0:r0 + DH, par, 256 + t * DV:256 + (t + 1) * DV], ktok[par][:, h * DH:(h + 1) * DH],
                                     VR[:, n, h * DV:(h + 1) * DV], start=True, stop=True)
                if n >= 2:
                    pe.wait_ge(s_rmix, n - 1)
                for h in range(NH):
                    t, j = h // 2, 2 * (h % 2) + h // 2
                    o = PT[:, 2 + par, h * DV:(h + 1) * DV]
                    i = nc.tensor.matmul(o, sT[par][:, j * P:(j + 1) * P], VR[:, n, h * DV:(h + 1) * DV],
                                         start=True, stop=n == 0)
                    if n:
                        i = nc.tensor.matmul(o, qd[par][:, h * P:(h + 1) * P], state[:, t * DV:(t + 1) * DV],
                                             start=False, stop=True)
                i.then_inc(s_ro, 1)

            for n in range(TT + 1):
                if n < TT:
                    scores(n)
                if n:
                    outputs(n - 1)
            for c in range(3, 6):
                if c == 3:
                    pe.wait_ge(s_rm, TT)
                    pe.wait_ge(s_rst, TT)
                    pe.wait_ge(s_rmix, TT)
                chunk(c)
            for b in range(4):
                pe.wait_ge(s_free[b], 12)

            def att_scores(b):
                h, i = b // TT, b % TT
                W = P * (i + 1)
                qs = slice(i * P, (i + 1) * P)
                for m in range(2):
                    r = slice(m * DH, (m + 1) * DH)
                    if b:
                        pe.wait_ge(s_ae, 2 * (b - 1) + m + 1)
                    for c0 in range(0, W, 512):
                        n = min(512, W - c0)
                        o = SC(m)[:, c0:c0 + n]
                        diag = c0 + n == W
                        nc.tensor.matmul(o, Q[r, h, qs], K[r, h, c0:c0 + n], start=True, stop=False)
                        j = nc.tensor.matmul(o, pos_q[:, h, :], pos_k[:, S - W + c0:S - W + c0 + n],
                                             start=False, stop=not diag)
                        if diag:
                            j = nc.tensor.matmul(SC(m)[:, W - P:W], identb, corr[:, h, :], start=False, stop=True)
                    j.then_inc(s_as, 1)

            def att_transposes(b):
                i = b % TT
                pe.wait_ge(s_aa, b + 1)
                if b:
                    pe.wait_ge(s_aea, b)
                    pe.wait_ge(s_aed, late(b))
                for k in range(i + 1):
                    j = nc.tensor.transpose(tpair(0)[:, k, :], PB(b % 2, 0)[:, k * P:(k + 1) * P], ident)
                j.then_inc(s_at, 1)

            def late(b):
                return sum(1 for q in range(b) if q % TT >= 4)

            def att_out(b):
                h, i = b // TT, b % TT
                pe.wait_ge(s_aea, b + 1)
                pe.wait_ge(s_aed, late(b + 1))
                if b >= 2:
                    pe.wait_ge(s_aoe, b - 1)
                for k in range(i + 1):
                    j = nc.tensor.matmul(PT[:, 2 + b % 2, 0:DV], aT(b % 2)[:, k, :], V[:, k, h * DV:(h + 1) * DV],
                                         start=k == 0, stop=k == i)
                j.then_inc(s_ao, 1)

            for b in range(NB + 2):
                if b < NB:
                    att_scores(b)
                if 1 <= b <= NB:
                    att_transposes(b - 1)
                if b >= 2:
                    att_out(b - 2)
            for t in range(TT):
                transposes(pe, 1, t, lambda t, k: xn[:, t % 2, k * P:(k + 1) * P] if k < 4
                           else H[:, t, k * P:(k + 1) * P])
            pe.wait_ge(s_xl, 2 * TT)
            for t in range(TT + 2):
                if t < TT:
                    for c in range(2):
                        g = 48 + 2 * t + c
                        group(pe, g, (12 + 2 * c, 13 + 2 * c), False, 0, t)
                if t >= 2:
                    if t == 2:
                        pass
                    u = t - 2
                    if u < TT - 2:
                        transposes(pe, 2, u, lambda t, k: xn[:, t % 2, k * P:(k + 1) * P])
                    else:
                        transposes(pe, 2, u, lambda t, k: xn[:, t % 2, k * P:(k + 1) * P])
            pe.wait_ge(s_rws, 1)
            pe.wait_ge(s_xl, 3 * TT)
            for b in range(4):
                pe.wait_ge(s_free[b], 16)
            for t in range(TT):
                for k in range(KT):
                    tk, c = slice(t * P, (t + 1) * P), slice(k * 36, k * 36 + 36)
                    i = product(pe, PS[:, 0, t * 36:(t + 1) * 36], XH[:, k, tk], XL[:, k, tk], rwh[:, c], rwl[:, c],
                                k == 0, k == KT - 1)
            i.then_inc(s_lg, 1)
            pe.wait_ge(s_rt, 1)
            for t in range(TT):
                for j in range(t + 1):
                    nc.tensor.matmul(PS[:, 1, t * NE:(t + 1) * NE], tri if j == t else onesb, rM[:, j, :],
                                     start=j == 0, stop=j == t)
            for j in range(TT):
                i = nc.tensor.matmul(PS[0:NE, 2, 0:1], rM[:, j, :], onesb[:, 0:1], start=j == 0, stop=j == TT - 1)
            i.then_inc(s_rp, 1)
            pe.wait_ge(s_rt, 2)
            nc.tensor.matmul(PS[:, 3, 0:NE], rexb[0:NE, :], tri[0:NE, 0:NE], start=True, stop=True)
            nc.tensor.matmul(PS[:, 3, NE:2 * NE], rexb[0:NE, :], tri[0:NE, 0:NE], start=True, stop=False)
            nc.tensor.matmul(PS[:, 3, NE:2 * NE], rexb[0:NE, :], identb[0:NE, 0:NE], start=False, stop=True)\
                .then_inc(s_rp, 1)
            pe.wait_ge(s_rt, 3)
            for n in range(2 * TT):
                i = nc.tensor.matmul(PS[:, 0, 0:BLK_MAX + 1], rA[:, n, :], rB[:, n, :],
                                     start=n == 0, stop=n == 2 * TT - 1)
            i.then_inc(s_rp, 1)

            def x_transposes(e, q):
                pe.wait_ge(s_gx[q], 16 * (e // 2 + 1) if isinstance(e, int) else 8 * (e - q) + 16)
                if not (isinstance(e, int) and e == 0):
                    pe.wait_ge(s_xel, e)
                for k in range(KT):
                    i = nc.tensor.transpose(tpair(0)[:, k, :], XG[q][:, k * P:(k + 1) * P], ident)
                i.then_inc(s_xt, 1)

            pe.wait_ge(s_slots, 1)
            for q in range(2):
                x_transposes(q, q)
            pe.wait_ge(s_xel, 1)
            expert_product(pe, PS[:, 0, :], 2, 0, xeh[0], xel[0], s_g)

            def body(e, q, first, last):
                if not (first and q == 0):
                    pe.wait_ge(s_h, e)
                expert_product(pe, PS[:, 2, :], 0, e, xeh[q], xel[q], s_u)
                if not (last and q):
                    if not (first and q == 0):
                        pe.wait_ge(s_t, e)
                    pe.wait_ge(s_xel, e + 2)
                    expert_product(pe, PS[:, 1 - q, :], 2, e + 1, xeh[1 - q], xel[1 - q], s_g)
                pe.wait_ge(s_h, e + 1)
                if not (first and q == 0):
                    pe.wait_ge(s_hl, e)
                for k in range(4):
                    i = nc.tensor.transpose(PS[:, 3, k * P:(k + 1) * P], hbuf[:, k * P:(k + 1) * P], ident)
                i.then_inc(s_ht, 1)
                if not last:
                    x_transposes(e + 2, q)
                pe.wait_ge(s_hl, e + 1)
                for i in range(2):
                    s = 4 + i
                    pe.wait_ge(s_wo[s], BASE[s] + 1 + e)
                    if not (first and q == 0):
                        pe.wait_ge(s_y[i], e)
                    for k in range(UK):
                        c = slice(k * UC, k * UC + UC)
                        m = product(pe, PT[:, 2 + i, :], hTh[:, k, :], hTl[:, k, :], whi(s)[:, c], wlo(s)[:, c],
                                    k == 0, k == UK - 1)
                    m.then_inc(s_d[i], 1)

            pairs(body, pe)

            def over(j):
                for c in (s_h, s_t, s_hl, s_xel, s_y[0], s_y[1]):
                    pe.wait_ge(c, NE)
                pe.wait_ge(s_ox, 16 * j + 16)
                for k in range(KT):
                    i = nc.tensor.transpose(tpair(0)[:, k, :], XO[:, k * P:(k + 1) * P], ident)
                i.then_inc(s_ot, 1)
                pe.wait_ge(s_oc, 2 * j + 1)
                pe.wait_ge(s_oy, j)
                for u in range(6):
                    pe.wait_ge(s_ow, 96 * j + 16 * u + 16)
                    if u == 4:
                        pe.wait_ge(s_oh, j + 1)
                        for k in range(4):
                            i = nc.tensor.transpose(PS[:, 3, k * P:(k + 1) * P], hO[:, k * P:(k + 1) * P], ident)
                        i.then_inc(s_ot, 1)
                        pe.wait_ge(s_oc, 2 * j + 2)
                    for kk in range(UK):
                        c = slice(kk * UC, kk * UC + UC)
                        if u < 4:
                            k = u % 2 * UK + kk
                            i = nc.tensor.matmul(PS[:, u // 2, :], XOT[:, k * P:(k + 1) * P], wO[:, c],
                                                 start=k == 0, stop=k == KT - 1)
                        else:
                            i = nc.tensor.matmul(PT[:, u - 2, :], hOT[:, kk * P:(kk + 1) * P], wO[:, c],
                                                 start=kk == 0, stop=kk == UK - 1)
                    i.then_inc(s_ou, 1)

            overflow(pe, over)
            from_xn = lambda t, k: xn[:, t % 2, k * P:(k + 1) * P]
            for t in range(TT):
                transposes(pe, 3, t, from_xn)
            pe.wait_ge(s_xl, 4 * TT)
            for c in (s_h, s_t, s_hl):
                pe.wait_ge(c, NE)
            for p in range(16):
                hf, ft, th = p // 8, p % 8 // 2, p % 2
                for i in range(2):
                    group_b(pe, 64 + 2 * p + i, (4 * hf + 2 * i, 4 * hf + 2 * i + 1), True, ft, th)
            for b in range(4):
                pe.wait_ge(s_free[b], 24)
            ones = misc[:, M_ONE:M_ONE + P]
            for n, k in enumerate(CONV_DONE):
                conv_wait(pe, k)
                pe.wait_ge(s_sq, n + 1)
                for th in range(2):
                    hs = slice(th * 512, th * 512 + 512)
                    nc.tensor.matmul(PS[:, th, :], ones, H[:, k, hs], start=n == 0, stop=n == KT - 1)
                    i = nc.tensor.matmul(PS[:, 2 + th, :], ones, SQ(n)[:, hs], start=n == 0, stop=n == KT - 1)
                i.then_inc(s_st, 1)
            pe.wait_ge(s_cl, KT)
            for t in range(TT + 2):
                if t < TT:
                    for c in range(2):
                        group_b(pe, 96 + 2 * t + c, (8 + 2 * c, 9 + 2 * c), False, 0, t)
                if t >= 2:
                    transposes(pe, 4, t - 2, from_xn)
            pe.wait_ge(s_xl, 5 * TT)

            def body(c, last):
                for j in range(8):
                    th, ft = j // 4, j % 4
                    pe.wait_ge(s_free[j % 4], G_MLP + 6 * c + j // 4)
                    for s in range(2):
                        pe.wait_ge(s_wo[s], RM + 1 + c)
                        for kk in range(UK):
                            k = s * UK + kk
                            cs = slice(kk * UC + ft * P, kk * UC + ft * P + P)
                            ts = slice(th * 512, th * 512 + 512)
                            i = product(pe, PS[:, j % 4, :], whi(s)[:, cs], wlo(s)[:, cs], XH[:, k, ts], XL[:, k, ts],
                                        k == 0, k == KT - 1)
                    i.then_inc(s_full[j % 4], 1)
                for j in range(8, 24):
                    t, n = (j - 8) // 2, j % 2
                    s = 2 + n
                    pe.wait_ge(s_free[j % 4], G_MLP + 6 * c + j // 4)
                    pe.wait_ge(s_wo[s], RM + 1 + c)
                    pe.wait_ge(s_ml, 8 * c + (4 if t < 4 else 8))
                    ts = slice(t * P, (t + 1) * P)
                    for k in range(UK):
                        cs = slice(k * UC, k * UC + UC)
                        i = product(pe, PS[:, j % 4, :], HTh[:, k, ts], HTl[:, k, ts], whi(s)[:, cs], wlo(s)[:, cs],
                                    k == 0, k == UK - 1)
                    i.then_inc(s_full[j % 4], 1)

            mlp_chunks(pe, body)


def unit_layout(w):
    k, n = w.shape
    u = w.reshape(k // (UK * P), UK, P, n // UC, UC).transpose(3, 0, 2, 1, 4)
    return u.reshape(-1, P, UK * UC)


def by_channel(v):
    return v.reshape(-1, P).T


def expert_layout(w):
    return np.concatenate([unit_layout(v) for v in w])


def kernel(**inputs):
    import concourse.bacc as _bacc
    from concourse.bass_utils import run_bass_kernel_spmd as _run

    f = {k: np.ascontiguousarray(v) for k, v in inputs.items()}
    w_in = unit_layout(f["w_in"][0])
    order = [3, 4, 5, 0, 1, 2]
    w_ai = unit_layout(f["a_w_in_2"][0])
    NCH = DFF // UC
    w_a = np.concatenate([w_in[2 * c:2 * c + 2] for c in order] + [unit_layout(f["w_out"][0])])
    arrays = {
        "x": f["x"].reshape(TT, P, D),
        "gains": np.concatenate([f["attn_norm_g"], f["ffn_norm_g"], f["final_norm_g"][None], f["mix_norm_2"],
                                 f["mlp_norm_2"], f["a_b_out_2"]]),
        "lambdas": np.concatenate([f["da_lambda_q1"], f["da_lambda_k1"], f["da_lambda_q2"], f["da_lambda_k2"]]),
        "subln_g": f["da_subln_g"],
        "w_dense_a": w_a,
        "router_w": np.concatenate([f["router_group_w"][0], f["router_expert_w"][0]], axis=1)
        .reshape(KT, P, NG + NE).transpose(1, 0, 2).reshape(P, -1),
        "router_b": np.concatenate([f["router_group_b"], f["router_expert_b"]], axis=1),
        "conv_tables": np.concatenate([
            f["a_conv_w_2"][0].reshape(TAPS, KT, P).transpose(2, 1, 0).reshape(P, -1),
            by_channel(f["a_conv_b_2"]), by_channel(f["a_ln_g_2"]), by_channel(f["a_ln_b_2"]),
            by_channel(f["a_b_in_2"])], axis=1),
        "w_dense_b": np.concatenate([w_ai[0:2], w_ai[4:6], w_ai[2:4], w_ai[6:8], unit_layout(f["a_w_out_2"][0])]),
        "w_mlp": np.concatenate([unit_layout(f["mlp_w1_2"][0]).reshape(NCH, 2, P, UK * UC),
                                 unit_layout(f["mlp_w2_2"][0]).reshape(2, NCH, P, UK * UC).transpose(1, 0, 2, 3)],
                                axis=1).reshape(-1, P, UK * UC),
        "w_gate": expert_layout(f["expert_w_gate"][0]),
        "w_up": expert_layout(f["expert_w_up"][0]),
        "w_down": expert_layout(f["expert_w_down"][0]),
        **constants(),
    }
    nc = _bacc.Bacc("TRN2", target_bir_lowering=False, num_devices=1)
    sent, aps = {}, {}
    for name, value in arrays.items():
        value = np.ascontiguousarray(value)
        sent["in_" + name] = value
        aps[name] = nc.dram_tensor("in_" + name, value.shape, mybir.dt.from_np(value.dtype),
                                   kind="ExternalInput").ap()
    out = nc.dram_tensor("out_0", (S, D), F32, kind="ExternalOutput").ap()
    build(nc, aps, out)
    r = _run(nc, [sent], core_ids=[0])
    return r.results[0]["out_0"].reshape(1, S, D)
```

```python
import math
from contextlib import ExitStack

import numpy as np
import concourse.bass as bass
from concourse import mybir

F32 = mybir.dt.float32
F16 = mybir.dt.float16
BF16 = mybir.dt.bfloat16
I32 = mybir.dt.int32
ALU = mybir.AluOpType
ACT = mybir.ActivationFunctionType
AX = mybir.AxisListType

P = 128
S = 1024
D = 1024
TT = S // P
KT = D // P
NH = 4
DH = 64
DV = 128
CHUNK = 64
EPS = 1e-6
NE = 32
NG = 4
EG = NE // NG
HID = 512
DFF = 4 * D
TAPS = 31
LAMBDA_INIT = 0.8 - 0.6 * math.exp(-0.3 * 0)
WS = 64.0
IWS = 1.0 / WS
UC = 512
UK = 4
SLOTS = 4
BLK_MAX = NE + 15
NOVER = BLK_MAX - NE
PAD = TAPS - 1

DENSE_A = 16
MOE_UNITS = 6 * NE
DENSE_B = 12 + 32


def constants():
    p = np.arange(P)
    slopes = 2.0 ** (-8.0 * np.arange(1, NH + 1) / NH)
    lg = np.log1p(-(2.0 ** (-5.0 - np.arange(NH))))
    rel = p[None, :] - p[:, None]
    by_bank = [0, 2, 1, 3]
    dec = np.where(rel[:, None, :] >= 0, np.exp(lg[None, :, None] * np.maximum(rel, 0)[:, None, :]), 0.0) * DH ** -0.5
    dec = dec[:, by_bank]
    kdec = np.repeat(np.exp(lg[None, :] * (P - 1 - p)[:, None]) * DH ** -0.5, DH, axis=1)
    head_of = lambda t: 2 * t + (p // DH)
    qdec = np.stack([np.where((p // DH == h % 2)[:, None], np.exp(lg[h] * (p + 1.0))[None, :], 0.0)
                     for h in range(NH)], axis=1)
    cdec = np.stack([np.repeat(np.exp(lg[head_of(t)] * P)[:, None], DV, axis=1) for t in range(2)], axis=1)
    ret = np.concatenate([dec.reshape(P, -1), kdec, qdec.reshape(P, -1), cdec.reshape(P, -1)], axis=1)
    ar = lambda n: np.tile(np.arange(n, dtype=np.float64), (P, 1))
    tok = np.arange(TT)[None, :] * P + p[:, None]
    misc = np.concatenate([np.eye(P), ar(P), ar(BLK_MAX + 1), NE - ar(NE), tok,
                           np.full((P, 1), EPS), np.ones((P, P))], axis=1)
    k, q = p[None, :], p[:, None]
    corr = np.stack([np.where(k // CHUNK > q // CHUNK, -1e30, np.where(k > q, -2.0 * s * (k - q), 0.0))
                     for s in slopes], axis=1)
    half = np.concatenate([np.eye(P), corr.reshape(P, -1), np.triu(np.ones((P, P)), 1), np.ones((P, P))],
                          axis=1).astype(np.float32)
    half = np.ascontiguousarray((half.view(np.uint32) >> 16).astype(np.uint16)).view(np.float32)
    pos_k = np.stack([np.arange(S) - (S - P), np.ones(S)])
    pos_q = np.stack([np.repeat(slopes, P), np.concatenate([-s * p for s in slopes])])
    pos = np.concatenate([pos_k, pos_q], axis=1).astype(np.float16)
    return {"c_ret": ret.astype(np.float32), "c_misc": misc.astype(np.float32), "c_half": half, "c_pos": pos}


RET_COLS = NH * P + NH * DH + NH * P + 2 * DV
M_ID, M_IO, M_IOB = 0, P, 2 * P
M_REV = M_IOB + BLK_MAX + 1
M_TOK = M_REV + NE
M_EPS = M_TOK + TT
M_ONE = M_EPS + 1
MISC_COLS = M_ONE + P


class Chain:

    def __init__(self, engine, sem, base=0):
        self.engine, self.sem, self.n, self.base = engine, sem, 0, base

    def done(self, instruction):
        self.n += 1
        instruction.then_inc(self.sem, 1)
        self.engine.wait_ge(self.sem, self.base + self.n)


def build(nc, a, out, stop=None):
    with ExitStack() as ctx:
        def sb(name, cols, dt=F32, rows=P):
            return ctx.enter_context(nc.sbuf_tensor(name, [rows, cols], dt))

        def sem(name):
            return ctx.enter_context(nc.semaphore(name))

        H = sb("resid", TT * D)[:, :].rearrange("p (t d) -> p t d", t=TT)
        XTF = sb("xt", 2 * KT * S // 2)
        XH = XTF[:, 0:4096].bitcast(F16).rearrange("p (k t) -> p k t", k=KT)
        XL = XTF[:, 4096:8192].bitcast(F16).rearrange("p (k t) -> p k t", k=KT)
        stage = sb("stage", SLOTS * UK * UC)
        split = sb("split", SLOTS * 2 * UK * UC, F16)
        AR = sb("arena", 12288)
        xn = sb("xn", 2 * D)[:, :].rearrange("p (b d) -> p b d", b=2)
        junk = sb("junk", D)
        gb = sb("gb", D)
        misc = sb("misc", MISC_COLS)
        halfw = sb("half", 7 * P // 2)
        Z = sb("zone", 2304)
        cols = sb("cols", 512)

        ident = misc[:, M_ID:M_ID + P]
        eps = misc[:, M_EPS:M_EPS + 1]
        half = halfw[:, :].bitcast(BF16)
        identb = half[:, 0:P]
        corr = half[:, P:P + NH * P].rearrange("p (h k) -> p h k", h=NH)
        tri = half[:, 5 * P:6 * P]
        onesb = half[:, 6 * P:7 * P]
        ret = Z[:, 0:RET_COLS]
        decT = ret[:, 0:512].rearrange("p (b c) -> p b c", b=2)
        kdec = ret[:, 512:768]
        qdec = ret[:, 768:1280].rearrange("p (t j c) -> p t j c", t=2, j=2)
        cdec = ret[:, 1280:1536]
        pos = Z[0:2, RET_COLS:RET_COLS + (S + NH * P) // 2].bitcast(F16)
        pos_k = pos[:, 0:S]
        pos_q = pos[:, S:S + NH * P].rearrange("p (h q) -> p h q", h=NH)

        ss = cols[:, 0:8]
        std = cols[:, 8:16]
        rstd = cols[:, 16:24]
        ss4, std4, rst4 = cols[:, 24:28], cols[:, 28:32], cols[:, 32:36]
        lsum, lexp, neglam = cols[:, 36:38], cols[:, 38:40], cols[:, 40:41]
        c1 = cols[:, 41:42]
        negmax, rows_sum, rows_rec = cols[:, 64:128], cols[:, 128:192], cols[:, 192:256]
        ssA, stdA, rstA = cols[:, 256:288], cols[:, 288:320], cols[:, 320:352]
        subg = cols[:, 384:512]
        wk = cols[:, 64:80].rearrange("p (k t) -> p k t", k=2)
        slot = cols[:, 80:96].bitcast(I32).rearrange("p (k t) -> p k t", k=2)
        tok_of = cols[:, 96:96 + BLK_MAX + 1].bitcast(I32)
        idx = [cols[:, 144 + i:145 + i].bitcast(I32) for i in range(2)]
        over_e = cols[0:1, 146:146 + NOVER + 1].bitcast(I32)
        n_over = cols[0:1, 162:163].bitcast(I32)

        rw = Z[:, 0:288]
        rwh = Z[:, 288:432].bitcast(F16)
        rwl = Z[:, 432:576].bitcast(F16)
        rb = Z[:, 576:612]
        gm = Z[:, 1280:2304]
        WORK = AR[:, 8192:12288]
        y = [AR[:, 8192 + 1024 * i:9216 + 1024 * i] for i in range(2)]
        hbuf = AR[:, 10240:10752]
        tbuf = AR[:, 10752:11264]
        sig = AR[:, 11264:11776]
        hTh = AR[:, 11776:12032].bitcast(F16).rearrange("p (k t) -> p k t", k=4)
        hTl = AR[:, 12032:12288].bitcast(F16).rearrange("p (k t) -> p k t", k=4)
        XG = [XTF[:, 1024 * i:1024 * i + 1024] for i in range(2)]
        xeh = [XTF[:, 2048 + 1024 * i:2560 + 1024 * i].bitcast(F16).rearrange("p (k t) -> p k t", k=KT)
               for i in range(2)]
        xel = [XTF[:, 2560 + 1024 * i:3072 + 1024 * i].bitcast(F16).rearrange("p (k t) -> p k t", k=KT)
               for i in range(2)]
        YG = [[AR[:, 2048 * i + 1024 * k:2048 * i + 1024 * k + 1024] for k in range(2)] for i in range(4)]
        XO, XOT = XTF[:, 4096:5120], XTF[:, 5120:6144]
        hO, hOT, sO = XTF[:, 6144:6656], XTF[:, 6656:7168], XTF[:, 7168:7680]
        wO = AR[:, 0:2048]
        cconv = Z[:, 0:288]
        cw = cconv[:, 0:248].rearrange("p (k j) -> p k j", k=KT)
        cb, lng, lnb, b_in = cconv[:, 248:256], cconv[:, 256:264], cconv[:, 264:272], cconv[:, 272:288]
        U = AR[:, 0:KT * (PAD + S)].rearrange("p (k t) -> p k t", k=KT)
        prod = [AR[:, 8448 + 1024 * i:9472 + 1024 * i] for i in range(3)]
        av = [junk[:, 512 * i:512 * i + 512] for i in range(2)]
        sv = [xn[:, 0, 512 * i:512 * i + 512] for i in range(2)]
        mean, rdev, var = xn[:, 0, :], xn[:, 1, :], junk[:, :]
        bo = AR[:, 0:1024]
        HTh = AR[:, 0:2048].bitcast(F16).rearrange("p (k t) -> p k t", k=4)
        HTl = AR[:, 2048:4096].bitcast(F16).rearrange("p (k t) -> p k t", k=4)
        relu = [AR[:, 4096 + 512 * i:4608 + 512 * i] for i in range(2)]
        relu2 = [AR[:, 5120 + 512 * i:5632 + 512 * i] for i in range(2)]
        gbj = [XTF[:, 0:1024], XTF[:, 1024:2048]]
        xn_rows = nc.dram_tensor("xn_rows", (S, D), F32, kind="Internal").ap()
        y_rows = nc.dram_tensor("y_rows", ((BLK_MAX + 1) * P, D), F32, kind="Internal").ap()
        x2_rows = nc.dram_tensor("x2_rows", (TT, P, D), F32, kind="Internal").ap()

        PS = ctx.enter_context(nc.psum_tensor("ps", [P, 4, 512], F32))
        PT = ctx.enter_context(nc.psum_tensor("pt", [P, 4, 512], F32))

        def tpair(par):
            return PT[:, 2 * par:2 * par + 2, :].rearrange("p b (k c) -> p (b k) c", k=4)

        def wstage(s):
            return stage[:, s * 2048:(s + 1) * 2048] if s < SLOTS else AR[:, (s - 4) * 2048:(s - 3) * 2048]

        def whi(s):
            if s < SLOTS:
                return split[:, s * 4096:s * 4096 + 2048]
            return AR[:, 4096 + (s - 4) * 2048:4096 + (s - 4) * 2048 + 1024].bitcast(F16)

        def wlo(s):
            if s < SLOTS:
                return split[:, s * 4096 + 2048:(s + 1) * 4096]
            return AR[:, 4096 + (s - 4) * 2048 + 1024:4096 + (s - 3) * 2048].bitcast(F16)

        QR = AR[:, 0:2048].rearrange("p (t s) -> p t s", t=2)
        KR = AR[:, 2048:4096].rearrange("p (t s) -> p t s", t=2)
        VR = AR[:, 4096:8192].rearrange("p (t v) -> p t v", t=TT)
        SG = AR[:, 8192:12288].rearrange("p (t v) -> p t v", t=TT)
        Q = AR[:, 0:4096].rearrange("p (h s) -> p h s", h=NH)
        K = AR[:, 4096:8192].rearrange("p (h s) -> p h s", h=NH)
        V = AR[:, 8192:12288].rearrange("p (t v) -> p t v", t=TT)

        s_const = sem("const_loaded")
        s_misc = sem("tables_loaded")
        s_gain = sem("gain_loaded")
        s_x = [sem(f"x_loaded{i}") for i in range(TT)]
        s_wl = [sem(f"w_landed{i}") for i in range(6)]
        s_wh = [sem(f"w_hi{i}") for i in range(6)]
        s_wo = [sem(f"w_lo{i}") for i in range(6)]
        s_full = [sem(f"bank_full{i}") for i in range(4)]
        s_free = [sem(f"bank_free{i}") for i in range(4)]
        s_std = sem("norm_std")
        s_xn = sem("norm_xn")
        s_tr = sem("norm_transposed")
        s_xh = sem("xt_hi")
        s_xl = sem("xt_lo")
        s_dve = sem("dve_step")
        s_act = sem("act_step")
        s_sig = sem("gate_sigmoid")
        s_rsc = sem("ret_scores")
        s_rm = sem("ret_masked")
        s_rst = sem("ret_state")
        s_ro = sem("ret_out")
        s_rss = sem("ret_std")
        s_rmix = sem("ret_mix")
        s_lam = sem("lambda")
        s_lx = sem("lambda_exp")
        s_as = sem("att_scores")
        s_amx = sem("att_max")
        s_ae = sem("att_exp")
        s_aa = sem("att_mixed")
        s_at = sem("att_transposed")
        s_aea = sem("att_t_act")
        s_aed = sem("att_t_dve")
        s_ao = sem("att_out")
        s_aoe = sem("att_out_read")
        s_router_w = sem("router_loaded")
        s_rws = sem("router_split")
        s_xs = [sem(f"xn_stored{i}") for i in range(2)]
        s_lg = sem("logits")
        s_rt = sem("router_ready")
        s_rp = sem("router_products")
        s_rx = sem("router_exp")
        s_rd = sem("router_diff")
        s_slots = sem("slots_known")
        s_gx = [sem(f"x_gathered{i}") for i in range(2)]
        s_zero = sem("zero_tile")
        s_cleared = sem("overflow_rows_cleared")
        s_sc = sem("unit_scaled")
        s_seen = sem("wait_seen")
        s_ix = sem("index_column")
        s_xt = sem("x_transposed")
        s_xeh = sem("x_hi")
        s_xel = sem("x_lo")
        s_g = sem("gate_done")
        s_u = sem("up_done")
        s_es = sem("expert_sigmoid")
        s_t = sem("gate_silu")
        s_h = sem("hidden")
        s_ht = sem("hidden_transposed")
        s_hh = sem("hidden_hi")
        s_hl = sem("hidden_lo")
        s_d = [sem(f"down_done{i}") for i in range(2)]
        s_y = [sem(f"y_half{i}") for i in range(2)]
        s_ys = [sem(f"y_stored{i}") for i in range(2)]
        s_yg = [sem(f"y_gathered{i}") for i in range(4)]
        s_cmb = sem("combined")
        s_x2 = sem("second_input")
        s_x2s = sem("second_input_stored")
        s_ox = sem("over_rows_gathered")
        s_oix = sem("over_index_column")
        s_ow = sem("over_unit_landed")
        s_ou = sem("over_unit_used")
        s_ot = sem("over_transposed")
        s_oc = sem("over_copied")
        s_os = sem("over_sigmoid")
        s_og = sem("over_silu")
        s_oh = sem("over_hidden")
        s_oy = sem("over_output")
        s_oys = sem("over_stored")
        s_tab = sem("conv_tables_loaded")
        s_pad = sem("conv_pad")
        s_av = sem("conv_gate")
        s_cu = sem("conv_input")
        s_pr = sem("conv_product")
        s_ca = sem("conv_added")
        s_cd = sem("conv_dve")
        s_c0 = sem("conv_first_tap")
        s_sq = sem("conv_squares")
        s_st = sem("conv_stats")
        s_va = sem("conv_var")
        s_rd2 = sem("conv_dev")
        s_z = sem("conv_normed")
        s_zp = sem("conv_normed_gpsimd")
        s_zq = sem("conv_centred_gpsimd")
        s_rv = sem("conv_rdev")
        s_si = sem("conv_silu")
        s_ch = sem("conv_hi")
        s_cl = sem("conv_lo")
        s_bo = sem("bias_loaded")
        s_relu = sem("mlp_relu")
        s_mh = sem("mlp_hi")
        s_ml = sem("mlp_lo")
        s_out = sem("out_stored")

        block = ctx.enter_context(nc.Block())

        def load_unit(eng, n):
            s, r = n % SLOTS, n // SLOTS
            if r:
                eng.wait_ge(s_wh[s], r)
                eng.wait_ge(s_wo[s], r)
            eng.dma_start(wstage(s), a["w_dense_a"][n]).then_inc(s_wl[s], 16)

        def split_hi(act, n):
            s, r = n % SLOTS, n // SLOTS
            act.wait_ge(s_wl[s], 16 * (r + 1))
            if r:
                g = last_group(n - SLOTS)
                act.wait_ge(s_full[g % 4], g // 4 + 1)
            nc.scalar.activation(whi(s), wstage(s), ACT.Copy, scale=WS).then_inc(s_wh[s], 1)

        def split_lo(dve, n):
            s, r = n % SLOTS, n // SLOTS
            dve.wait_ge(s_wh[s], r + 1)
            nc.vector.scalar_tensor_tensor(out=wlo(s), in0=wstage(s), scalar=WS, in1=whi(s),
                                           op0=ALU.mult, op1=ALU.subtract).then_inc(s_wo[s], 1)

        def product(pe, out_ap, lh, ll, rh, rl, start, stop):
            nc.tensor.matmul(out_ap, lh, rh, start=start, stop=False)
            nc.tensor.matmul(out_ap, lh, rl, start=False, stop=False)
            return nc.tensor.matmul(out_ap, ll, rh, start=False, stop=stop)

        def last_group(n):
            return 8 * (n // 2) + 7 if n < 12 else 62 + (n - 12) // 2

        def group(pe, g, units, feature_major, ft, tk):
            if g >= 4:
                pe.wait_ge(s_free[g % 4], g // 4)
            for ui, n in enumerate(units):
                s, r = n % SLOTS, n // SLOTS
                pe.wait_ge(s_wo[s], r + 1)
                for kk in range(UK):
                    k = ui * UK + kk
                    if feature_major:
                        c = slice(kk * UC + ft * P, kk * UC + ft * P + P)
                        t = slice(tk * 512, tk * 512 + 512)
                        i = product(pe, PS[:, g % 4, :], whi(s)[:, c], wlo(s)[:, c], XH[:, k, t], XL[:, k, t],
                                    k == 0, k == KT - 1)
                    else:
                        c = slice(kk * UC, kk * UC + UC)
                        t = slice(tk * P, tk * P + P)
                        i = product(pe, PS[:, g % 4, :], XH[:, k, t], XL[:, k, t], whi(s)[:, c], wlo(s)[:, c],
                                    k == 0, k == KT - 1)
            i.then_inc(s_full[g % 4], 1)
            return i

        def norm_stats(act, ch, t):
            ch.done(nc.scalar.activation(junk[:, :], H[:, t, :], ACT.Square, accum_out=ss[:, t:t + 1]))
            nc.scalar.activation(std[:, t:t + 1], ss[:, t:t + 1], ACT.Sqrt, bias=eps, scale=1.0 / D)\
                .then_inc(s_std, 1)

        def xn_wait(dve, r, t):
            n = TT * r + t
            if n >= 2:
                dve.wait_ge(s_tr, n - 1)

        def norm_scale(dve, ch, r, t, nstd):
            dve.wait_ge(s_std, nstd)
            ch.done(nc.vector.reciprocal(rstd[:, t:t + 1], std[:, t:t + 1]))
            xn_wait(dve, r, t)
            nc.vector.scalar_tensor_tensor(out=xn[:, t % 2, :], in0=H[:, t, :], scalar=rstd[:, t:t + 1],
                                           in1=gb[:, :], op0=ALU.mult, op1=ALU.mult).then_inc(s_xn, 1)

        def transposes(pe, r, t, src):
            n = TT * r + t
            pe.wait_ge(s_xn, n + 1)
            if n >= 2:
                pe.wait_ge(s_xl, n - 1)
            for k in range(KT):
                i = nc.tensor.transpose(tpair(t % 2)[:, k, :], src(t, k), ident)
            i.then_inc(s_tr, 1)

        def xt_hi(act, r, t):
            act.wait_ge(s_tr, TT * r + t + 1)
            nc.scalar.activation(XH[:, :, t * P:(t + 1) * P], tpair(t % 2), ACT.Copy).then_inc(s_xh, 1)

        def xt_lo(dve, r, t):
            dve.wait_ge(s_xh, TT * r + t + 1)
            nc.vector.tensor_tensor(XL[:, :, t * P:(t + 1) * P], tpair(t % 2), XH[:, :, t * P:(t + 1) * P],
                                    ALU.subtract).then_inc(s_xl, 1)

        FM = [True, False, False, True, True, False]

        def chunk_groups(c):
            if c == 0:
                return [(4 * th + ft, ft, th) for th in range(2) for ft in range(4)]
            if FM[c]:
                return [(8 * c + 2 * ft + th, ft, th) for ft in range(4) for th in range(2)]
            return [(8 * c + t, 0, t) for t in range(TT)]

        def chunk_dest(c, ft, tk):
            tok = slice(tk * 512, tk * 512 + 512)
            return [lambda: (QR if ft < 2 else KR)[:, ft % 2, tok], lambda: VR[:, tk, :], lambda: SG[:, tk, :],
                    lambda: Q[:, ft, tok], lambda: K[:, ft, tok], lambda: V[:, tk, :]][c]()

        CHUNK_SCALE = [IWS, IWS, IWS, IWS * DH ** -0.5, IWS, IWS]
        NB = NH * TT

        def aT(par):
            return XTF[:, 4096 + par * 1024:4096 + (par + 1) * 1024].rearrange("p (k q) -> p k q", k=KT)

        def PB(par, m):
            return XTF[:, (2 * par + m) * 1024:(2 * par + m + 1) * 1024]

        def SC(m):
            return PS[:, 2 * m:2 * m + 2, :].rearrange("p b c -> p (b c)")

        sT = [xn[:, 0, 0:512], xn[:, 0, 512:1024]]
        qd = [xn[:, 1, 0:512], xn[:, 1, 512:1024]]
        ktok = [junk[:, 256:512], junk[:, 512:768]]
        state = junk[:, 0:256]
        lam_in = AR[:, 10240:10496]
        lam_dot = AR[:, 10496:10624].rearrange("p (j d) -> p j d", j=2)

        BASE = [4, 4, 4, 4, 0, 0]
        FIRST_PAIRS = [(0, True, False), (NE // 2 - 1, False, True)]

        def expert_load(sp, kind, e):
            s0 = {"up": 0, "gate": 2, "down": 4}[kind]
            for i in range(2):
                s = s0 + i
                if not (isinstance(e, int) and BASE[s] + e == 0):
                    sp.wait_ge(s_wh[s], BASE[s] + e)
                    sp.wait_ge(s_wo[s], BASE[s] + e)
                src = a["w_" + kind][bass.ds(2 * e + i, 1), :, :].rearrange("o p c -> (o p) c")
                sp.dma_start(wstage(s), src).then_inc(s_wl[s], 16)

        def expert_hi(act, s, e):
            act.wait_ge(s_wl[s], 16 * (BASE[s] + 1) + 16 * e)
            if not (isinstance(e, int) and e == 0):
                act.wait_ge([s_u, s_u, s_g, s_g, s_d[0], s_d[1]][s], e)
            nc.scalar.activation(whi(s), wstage(s), ACT.Copy, scale=WS).then_inc(s_wh[s], 1)

        def expert_lo(dve, s, e):
            dve.wait_ge(s_wh[s], BASE[s] + 1 + e)
            nc.vector.scalar_tensor_tensor(out=wlo(s), in0=wstage(s), scalar=WS, in1=whi(s),
                                           op0=ALU.mult, op1=ALU.subtract).then_inc(s_wo[s], 1)

        def expert_lo_pool(pool, e):
            s = 5
            pool.wait_ge(s_wh[s], BASE[s] + 1 + e)
            pool.sem_inc(s_seen, 1)
            nc.gpsimd.tensor_scalar(wstage(s), wstage(s), WS, None, ALU.mult).then_inc(s_sc, 1)
            pool.wait_ge(s_sc, e)
            nc.gpsimd.tensor_tensor(wlo(s), wstage(s), whi(s), ALU.subtract).then_inc(s_wo[s], 1)

        def expert_product(pe, bank, s0, e, lh, ll, done, between=None):
            for i in range(2):
                s = s0 + i
                if i and between:
                    between()
                pe.wait_ge(s_wo[s], BASE[s] + 1 + e)
                for kk in range(UK):
                    k, c = i * UK + kk, slice(kk * UC, kk * UC + UC)
                    m = product(pe, bank, lh[:, k, :], ll[:, k, :], whi(s)[:, c], wlo(s)[:, c], k == 0, k == KT - 1)
            m.then_inc(done, 1)

        def overflow(eng, body):
            eng.wait_ge(s_slots, 1)
            n = eng.value_load(n_over, min_val=0, max_val=NOVER)
            with eng.If(n > 0):
                with eng.Fori(0, NOVER) as j:
                    with eng.If(j < n):
                        body(j)

        RB = BASE[0] + NE

        def load_b(sp, m):
            s, r = m % SLOTS, RB + m // SLOTS
            sp.wait_ge(s_wh[s], r)
            sp.wait_ge(s_wo[s], r)
            sp.dma_start(wstage(s), a["w_dense_b"][m]).then_inc(s_wl[s], 16)

        def last_group_b(m):
            return 77 + 16 * (m // 4) + m % 4 // 2 * 2 if m < 8 else 110 + (m - 8) // 2

        def hi_b(act, m):
            s, r = m % SLOTS, RB + m // SLOTS
            act.wait_ge(s_wl[s], 16 * (r + 1))
            if m >= SLOTS:
                g = last_group_b(m - SLOTS)
                act.wait_ge(s_full[g % 4], g // 4 + 1)
            nc.scalar.activation(whi(s), wstage(s), ACT.Copy, scale=WS).then_inc(s_wh[s], 1)

        def lo_b(dve, m):
            s, r = m % SLOTS, RB + m // SLOTS
            dve.wait_ge(s_wh[s], r + 1)
            nc.vector.scalar_tensor_tensor(out=wlo(s), in0=wstage(s), scalar=WS, in1=whi(s),
                                           op0=ALU.mult, op1=ALU.subtract).then_inc(s_wo[s], 1)

        def group_b(pe, g, units, feature_major, ft, tk):
            pe.wait_ge(s_free[g % 4], g // 4)
            for ui, m in enumerate(units):
                s, r = m % SLOTS, RB + m // SLOTS
                pe.wait_ge(s_wo[s], r + 1)
                for kk in range(UK):
                    k = ui * UK + kk
                    if feature_major:
                        c = slice(kk * UC + ft * P, kk * UC + ft * P + P)
                        t = slice(tk * 512, tk * 512 + 512)
                        i = product(pe, PS[:, g % 4, :], whi(s)[:, c], wlo(s)[:, c], XH[:, k, t], XL[:, k, t],
                                    k == 0, k == KT - 1)
                    else:
                        c = slice(kk * UC, kk * UC + UC)
                        t = slice(tk * P, tk * P + P)
                        i = product(pe, PS[:, g % 4, :], XH[:, k, t], XL[:, k, t], whi(s)[:, c], wlo(s)[:, c],
                                    k == 0, k == KT - 1)
            i.then_inc(s_full[g % 4], 1)

        RM = RB + 3
        G_MLP = 112 // 4
        NC = DFF // UC
        CONV_DVE, CONV_ACT = [0, 2, 3, 5, 6], [1, 4, 7]
        CONV_DONE = list(range(KT))
        GATED = [(0, 0), (1, 0), (0, 1), (1, 1)] + [(k, th) for k in range(2, KT) for th in range(2)]

        def gate_groups(p):
            if p < 4:
                return 64 + 2 * p, 65 + 2 * p
            return 64 + 2 * (p - p % 2) + p % 2, 66 + 2 * (p - p % 2) + p % 2

        def input_done(k):
            return GATED.index((k, 1)) + 1

        def conv_in_group(g):
            for p, (k, th) in enumerate(GATED):
                if g in gate_groups(p):
                    return gate_groups(p).index(g), k, th

        def mlp_hi(act, s, c):
            act.wait_ge(s_wl[s], 16 * (RM + 1) + 16 * c)
            nc.scalar.activation(whi(s), wstage(s), ACT.Copy, scale=WS).then_inc(s_wh[s], 1)

        def mlp_lo(dve, s, c):
            dve.wait_ge(s_wh[s], RM + 1 + c)
            nc.vector.scalar_tensor_tensor(out=wlo(s), in0=wstage(s), scalar=WS, in1=whi(s),
                                           op0=ALU.mult, op1=ALU.subtract).then_inc(s_wo[s], 1)

        def mlp_chunks(eng, body):
            with eng.Fori(0, NC - 1) as c:
                body(c, False)
            body(NC - 1, True)

        def conv_wait(eng, k):
            if k in CONV_ACT:
                eng.wait_ge(s_ca, (TAPS - 1) * (CONV_ACT.index(k) + 1))
            else:
                eng.wait_ge(s_cd, CONV_DVE.index(k) + 1)

        def SQ(i):
            return gbj[i % 2]

        LN_ORDER = list(range(KT))
        LN_POOL = (2, 5, 7)
        silu = [prod[i // 2][:, i % 2 * 512:i % 2 * 512 + 512] for i in range(6)]

        def ln_wait(eng, n):
            half_, k = n // KT, n % KT
            if k in LN_POOL:
                eng.wait_ge(s_zp, len(LN_POOL) * half_ + LN_POOL.index(k) + 1)
            else:
                eng.wait_ge(s_z, (KT - len(LN_POOL)) * half_ + k + 1 - sum(x < k for x in LN_POOL))

        def tap_schedule():
            left, opened, plan = list(CONV_DVE), [], []
            for p in list(range(len(GATED))) + [None]:
                now = len(GATED) if p is None else p + 1
                room = 10 ** 6 if p is None else (8 if p % 2 else 7) - (4 if p in (6, 7, 14, 15) else 0)
                taps_ = []
                while len(taps_) < room:
                    while len(opened) < 2 and left and input_done(left[0]) <= now:
                        opened.append([left.pop(0), 0])
                    if not opened:
                        break
                    x = opened.pop(0)
                    taps_.append(tuple(x))
                    if x[1] + 1 < TAPS:
                        opened.append([x[0], x[1] + 1])
                plan.append(taps_)
            return plan

        def pairs(body, eng):
            for q in range(2):
                body(q, q, True, False)
            with eng.Fori(1, NE // 2 - 1) as k:
                for q in range(2):
                    body(2 * k + q, q, False, False)
            for q in range(2):
                body(NE - 2 + q, q, False, True)

        def first_dev(u):
            return max(1, 2 * u)

        def second_dev(u):
            return 2 * u + 3 if u < TT - 1 else 2 * TT

        off = [0]

        def work(n, *shape):
            v = WORK[:, off[0]:off[0] + n]
            off[0] += n
            if len(shape) == 2:
                return v.rearrange("p (a b) -> p a b", a=shape[0])
            if len(shape) == 3:
                return v.rearrange("p (a b c) -> p a b c", a=shape[0], b=shape[1])
            return v

        BIG = 1e38
        rL = work(TT * 36, TT, 36)
        rG, rE = rL[:, :, 0:NG], rL[:, :, NG:NG + NE]
        rgm, rgx = work(TT), work(TT)
        rgo = work(TT * NG, TT, NG)
        rex = work(TT * NG, TT, NG)
        rEm = work(TT * NE, TT, NE)
        rtmp = work(TT * NE, TT, NE)
        roh = [work(TT * NE, TT, NE) for _ in range(2)]
        rm = [work(TT), work(TT)]
        rix = work(2 * TT, 2, TT)
        rde, rgs = work(TT), work(TT)
        rM = work(TT * NE // 2).bitcast(BF16).rearrange("p (t e) -> p t e", t=TT)
        rex_t = work(1)
        rcmp = work(NE)
        rexb = work(P // 2).bitcast(BF16)
        rthr = work(8)
        rrank, rbq, rst_ = work(2 * TT, 2, TT), work(2 * TT, 2, TT), work(2 * TT, 2, TT)
        rblk, rpos, rv = work(2 * TT, 2, TT), work(2 * TT, 2, TT), work(2 * TT, 2, TT)
        rc7 = work(2 * TT * 7, 2 * TT, 7)
        rinc = work(NE)
        rov = work((NOVER + 1) * NE, NOVER + 1, NE)
        rbe = work(NOVER + 1)
        off[0] = 2700
        rA = work(2 * TT * P // 2).bitcast(F16).rearrange("p (n c) -> p n c", n=2 * TT)
        rB = junk[:, 0:TT * (BLK_MAX + 1)].bitcast(F16).rearrange("p (n c) -> p n c", n=2 * TT)

        def bc(ap, n):
            return ap.unsqueeze(2).to_broadcast([P, ap.shape[1], n])

        def router(dve, ch):
            V_ = nc.vector
            io, iob = misc[:, M_IO:M_IO + P], misc[:, M_IOB:M_IOB + BLK_MAX + 1]
            rev = misc[:, M_REV:M_REV + NE]
            tok = misc[:, M_TOK:M_TOK + TT]
            dve.wait_ge(s_lg, 1)
            ch.done(V_.scalar_tensor_tensor(
                out=rL, in0=PS[:, 0, 0:TT * 36].rearrange("p (t c) -> p t c", t=TT), scalar=IWS,
                in1=rb.unsqueeze(1).to_broadcast([P, TT, 36]), op0=ALU.mult, op1=ALU.add))
            ch.done(V_.tensor_reduce(rgm, rG, AX.X, ALU.max))
            ch.done(V_.tensor_tensor(rex, rG, bc(rgm, NG), ALU.subtract))
            V_.tensor_scalar(rgo, rex, 0.0, None, ALU.is_ge).then_inc(s_rd, 1)
            dve.wait_ge(s_rd, 1)
            ch.done(V_.tensor_tensor(rgo, rgo, rev[:, NE - NG:NE].unsqueeze(1).to_broadcast([P, TT, NG]), ALU.mult))
            ch.done(V_.tensor_reduce(rgx, rgo, AX.X, ALU.max))
            ch.done(V_.tensor_tensor(rgo, rgo, bc(rgx, NG), ALU.is_equal))
            r4 = lambda v: v.rearrange("p t (g e) -> p (t g) e", g=NG)
            go = rgo.rearrange("p t g -> p (t g)")
            rE4 = [rE[:, :, g * EG:(g + 1) * EG] for g in range(NG)]
            for g in range(NG):
                V_.tensor_tensor(rEm[:, :, g * EG:(g + 1) * EG], rE4[g], bc(rgo[:, :, g], EG), ALU.mult)
            ch.done(V_.tensor_scalar(rtmp[:, :, 0:NG], rgo, BIG, -BIG, ALU.mult, ALU.add))
            for g in range(NG):
                part = rEm[:, :, g * EG:(g + 1) * EG]
                i = V_.tensor_tensor(part, part, bc(rtmp[:, :, g], EG), ALU.add)
            ch.done(i)
            for k in range(2):
                if k:
                    ch.done(V_.scalar_tensor_tensor(out=rEm, in0=roh[0], scalar=-BIG, in1=rEm,
                                                    op0=ALU.mult, op1=ALU.add))
                ch.done(V_.tensor_reduce(rm[k], rEm, AX.X, ALU.max))
                ch.done(V_.tensor_tensor(roh[k], rEm, bc(rm[k], NE), ALU.is_ge))
                ch.done(V_.tensor_tensor(roh[k], roh[k], rev.unsqueeze(1).to_broadcast([P, TT, NE]), ALU.mult))
                ch.done(V_.tensor_reduce(rix[:, k, :], roh[k], AX.X, ALU.max))
                ch.done(V_.tensor_tensor(roh[k], roh[k], bc(rix[:, k, :], NE), ALU.is_equal))
            V_.tensor_tensor(rde, rm[1], rm[0], ALU.subtract).then_inc(s_rd, 1)
            ch.done(V_.tensor_scalar(rix, rix, -1.0, float(NE), ALU.mult, ALU.add))
            V_.tensor_tensor(rM, roh[0], roh[1], ALU.add).then_inc(s_rt, 1)
            dve.wait_ge(s_rx, 2)
            ch.done(V_.tensor_reduce(rgs, rex, AX.X, ALU.add))
            ch.done(V_.tensor_scalar(rm[0], rde, 1.0, None, ALU.add))
            ch.done(V_.tensor_tensor(rgs, rgs, rm[0], ALU.mult))
            ch.done(V_.reciprocal(wk[:, 0, :], rgs))
            ch.done(V_.tensor_tensor(wk[:, 1, :], wk[:, 0, :], rde, ALU.mult))
            dve.wait_ge(s_rp, 1)
            ch.done(V_.tensor_copy(rex_t[0:NE, :], PS[0:NE, 2, 0:1]))
            ch.done(V_.tensor_scalar(rcmp[0:NE, 0:7], io[0:NE, 1:8], float(P), rex_t[0:NE, :], ALU.mult, ALU.is_lt))
            ch.done(V_.tensor_reduce(rex_t[0:NE, :], rcmp[0:NE, 0:7], AX.X, ALU.add))
            V_.tensor_scalar(rexb[0:NE, :], misc[0:NE, M_ONE:M_ONE + P], rex_t[0:NE, :], None, ALU.mult)\
                .then_inc(s_rt, 1)
            for k in range(2):
                ch.done(V_.tensor_tensor(rtmp, PS[:, 1, 0:TT * NE].rearrange("p (t e) -> p t e", t=TT), roh[k],
                                         ALU.mult))
                ch.done(V_.tensor_reduce(rrank[:, k, :], rtmp, AX.X, ALU.add))
            ch.done(V_.tensor_scalar(rthr[:, 0:7], io[:, 1:8], float(P), None, ALU.mult))
            rank = rrank.rearrange("p k t -> p (k t)")
            ch.done(V_.tensor_tensor(rc7, bc(rank, 7), rthr[:, 0:7].unsqueeze(1).to_broadcast([P, 2 * TT, 7]),
                                     ALU.is_ge))
            ch.done(V_.tensor_reduce(rbq.rearrange("p k t -> p (k t)"), rc7, AX.X, ALU.add))
            ch.done(V_.scalar_tensor_tensor(out=rpos, in0=rbq, scalar=-float(P), in1=rrank,
                                            op0=ALU.mult, op1=ALU.add))
            dve.wait_ge(s_rp, 2)
            for k in range(2):
                ch.done(V_.tensor_tensor(rtmp, PS[:, 3, 0:NE].unsqueeze(1).to_broadcast([P, TT, NE]), roh[k],
                                         ALU.mult))
                ch.done(V_.tensor_reduce(rst_[:, k, :], rtmp, AX.X, ALU.add))
            ch.done(V_.tensor_copy(rinc, PS[:, 3, NE:2 * NE]))
            ch.done(V_.tensor_tensor(rv, rst_, rbq, ALU.add))
            ch.done(V_.tensor_tensor(rv, rv, rix, ALU.subtract))
            ch.done(V_.tensor_scalar(rblk, rbq, 0.0, None, ALU.is_gt))
            ch.done(V_.scalar_tensor_tensor(out=rv, in0=rv, scalar=float(NE - 1), in1=rblk,
                                            op0=ALU.add, op1=ALU.mult))
            ch.done(V_.tensor_tensor(rblk, rv, rix, ALU.add))
            V_.scalar_tensor_tensor(out=slot, in0=rblk, scalar=float(P), in1=rpos, op0=ALU.mult, op1=ALU.add)
            V_.tensor_tensor(rA, io.unsqueeze(1).to_broadcast([P, 2 * TT, P]),
                             bc(rpos.rearrange("p k t -> p (k t)"), P), ALU.is_equal)
            ch.done(V_.tensor_tensor(rB, iob.unsqueeze(1).to_broadcast([P, 2 * TT, BLK_MAX + 1]),
                                     bc(rblk.rearrange("p k t -> p (k t)"), BLK_MAX + 1), ALU.is_equal))
            for k in range(2):
                i = V_.tensor_tensor(rB[:, k * TT:(k + 1) * TT, :], rB[:, k * TT:(k + 1) * TT, :],
                                     bc(tok, BLK_MAX + 1), ALU.mult)
            i.then_inc(s_rt, 1)
            ch.done(V_.tensor_tensor(rov[0:1], rinc[0:1, :].unsqueeze(1).to_broadcast([1, NOVER + 1, NE]),
                                     iob[0:1, 0:NOVER + 1].unsqueeze(2).to_broadcast([1, NOVER + 1, NE]),
                                     ALU.is_le))
            ch.done(V_.tensor_reduce(rbe[0:1, :], rov[0:1], AX.X, ALU.add))
            V_.tensor_scalar(over_e, rbe[0:1, :], float(NE - 1), None, ALU.min)
            V_.tensor_copy(n_over, rinc[0:1, NE - 1:NE])
            dve.wait_ge(s_rp, 3)
            V_.tensor_copy(tok_of, PS[:, 0, 0:BLK_MAX + 1]).then_inc(s_slots, 1)

        @block.sync
        def _(sp):
            for t in range(TT):
                sp.dma_start(H[:, t, :], a["x"][t]).then_inc(s_x[t], 16)
                if t == 0:
                    sp.dma_start(gb[:, :], a["gains"][0:1, :].to_broadcast([P, D])).then_inc(s_gain, 16)
                    sp.dma_start(misc[:, :], a["c_misc"]).then_inc(s_misc, 16)
                if t in (1, 3):
                    load_unit(sp, t // 2)
            for n in range(2, 4):
                load_unit(sp, n)
            sp.dma_start(halfw[:, :], a["c_half"]).then_inc(s_const, 16)
            sp.dma_start(ret, a["c_ret"]).then_inc(s_const, 16)
            sp.dma_start(pos, a["c_pos"]).then_inc(s_const, 16)
            sp.dma_start(subg, a["subln_g"].to_broadcast([P, DV])).then_inc(s_const, 16)
            for j in range(4):
                sp.dma_start(lam_in[:, j * DH:(j + 1) * DH], a["lambdas"][j:j + 1, :].to_broadcast([P, DH]))\
                    .then_inc(s_const, 16)
            for n in range(4, DENSE_A):
                load_unit(sp, n)
            for t in range(TT):
                sp.wait_ge(s_tr, TT + t + 1)
                sp.dma_start(H[:, t, :], a["x"][t]).then_inc(s_x[t], 16)
            sp.dma_start(rw, a["router_w"]).then_inc(s_router_w, 16)
            sp.dma_start(rb, a["router_b"].to_broadcast([P, NG + NE])).then_inc(s_router_w, 16)
            sp.dma_start(gb[:, :], a["gains"][1:2, :].to_broadcast([P, D])).then_inc(s_gain, 16)

            expert_load(sp, "gate", 0)

            def body(e, q, first, last):
                expert_load(sp, "up", e)
                if first and q == 0:
                    expert_load(sp, "down", e)
                if not (last and q):
                    expert_load(sp, "gate", e + 1)
                if not (first and q == 0):
                    expert_load(sp, "down", e)

            pairs(body, sp)

            def over(j):
                e = sp.value_load(over_e[:, bass.ds(j, 1)], min_val=0, max_val=NE - 1)
                for i in range(2):
                    sp.wait_ge(s_wh[4 + i], NE)
                    sp.wait_ge(s_wo[4 + i], NE)
                for u in range(6):
                    w = a[("w_gate", "w_up", "w_down")[u // 2]]
                    sp.dma_start(wO, w[bass.ds(2 * e + u % 2, 1), :, :].rearrange("o p c -> (o p) c"))\
                        .then_inc(s_ow, 16)
                    sp.wait_ge(s_ou, 6 * j + u + 1)
                sp.sem_inc(s_seen, 1)

            overflow(sp, over)
            sp.wait_ge(s_tr, 3 * TT)
            sp.wait_ge(s_xn, 3 * TT)
            sp.dma_start(gb[:, :], a["gains"][2:3, :].to_broadcast([P, D])).then_inc(s_gain, 16)
            sp.dma_start(gm, a["gains"][3:4, :].to_broadcast([P, D])).then_inc(s_gain, 16)
            for m in range(SLOTS):
                load_b(sp, m)
            sp.dma_start(cconv, a["conv_tables"]).then_inc(s_tab, 16)
            for t in range(TT):
                sp.wait_ge(s_x2, t + 1)
                sp.dma_start(x2_rows[t], H[:, t, :]).then_inc(s_x2s, 16)
            for m in range(SLOTS, 12):
                load_b(sp, m)
            sp.wait_ge(s_st, 1)
            sp.dma_start(bo, a["gains"][5:6, :].to_broadcast([P, D])).then_inc(s_bo, 16)
            sp.dma_start(gb[:, :], a["gains"][4:5, :].to_broadcast([P, D])).then_inc(s_gain, 16)
            sp.wait_ge(s_x2s, 16 * TT)
            for t in range(TT):
                sp.wait_ge(s_cl, KT + t + 1)
                sp.dma_start(H[:, t, :], x2_rows[t]).then_inc(s_x[t], 16)

            def body(c, last):
                for s in range(SLOTS):
                    sp.wait_ge(s_wh[s], RM + c)
                    sp.wait_ge(s_wo[s], RM + c)
                    src = a["w_mlp"][bass.ds(SLOTS * c + s, 1), :, :].rearrange("o p c -> (o p) c")
                    sp.dma_start(wstage(s), src).then_inc(s_wl[s], 16)

            mlp_chunks(sp, body)
            for t in range(TT):
                for n in range(2):
                    j = 8 + 2 * t + n
                    sp.wait_ge(s_free[j % 4], G_MLP + 6 * (NC - 1) + j // 4 + 1)
                sp.dma_start(out[t * P:(t + 1) * P, :], H[:, t, :]).then_inc(s_out, 16)
            sp.wait_ge(s_out, 16 * TT)

        @block.gpsimd
        def _(pool):
            zero = AR[:, 11264:12288]
            nc.gpsimd.memset(zero, 0.0).then_inc(s_zero, 1)
            pool.wait_ge(s_zero, 1)
            for b in range(NE, BLK_MAX + 1):
                pool.dma_start(y_rows[b * P:(b + 1) * P, :], zero).then_inc(s_cleared, 16)
            for t in range(TT):
                pool.wait_ge(s_xn, 2 * TT + t + 1)
                pool.dma_start(xn_rows[t * P:(t + 1) * P, :], xn[:, t % 2, :]).then_inc(s_xs[t % 2], 16)
            for i in range(2):
                pool.wait_ge(s_xs[i], 16 * TT // 2)
            pool.wait_ge(s_slots, 1)
            pool.wait_ge(s_tr, 3 * TT)

            def gather(e, q):
                nc.gpsimd.tensor_copy(idx[q], tok_of[:, bass.ds(e, 1)]).then_inc(s_ix, 1)
                pool.wait_ge(s_ix, e + 1)
                pool.sem_inc(s_seen, 1)
                pool.indirect_dma_start(out=XG[q], out_offset=None, in_=xn_rows,
                                        in_offset=bass.IndirectOffsetOnAxis(ap=idx[q], axis=0))\
                    .then_inc(s_gx[q], 16)

            def store(e, q):
                pool.wait_ge(s_y[0], e + 1)
                pool.wait_ge(s_y[1], e + 1)
                dst = y_rows[bass.ds(e * P, P), :]
                pool.dma_start(dst, y[q]).then_inc(s_ys[q], 16)

            gather(0, 0)
            gather(1, 1)
            pool.wait_ge(s_xt, 1)
            pool.wait_ge(s_gx[0], 16)
            gather(2, 0)

            def body(e, q, first, last):
                if not last:
                    pool.wait_ge(s_xt, e + 2)
                    gather(e + 3, 1 - q)
                if not (first and q == 0):
                    store(e - 1, 1 - q)
                if not last:
                    expert_lo_pool(pool, e + 1)

            pairs(body, pool)
            store(NE - 1, 1)
            for i in range(2):
                pool.wait_ge(s_ys[i], 16 * NE // 2)
            pool.wait_ge(s_gx[0], 16 * (NE // 2 + 1))

            def over(j):
                nc.gpsimd.tensor_copy(idx[0], tok_of[:, bass.ds(j + NE, 1)]).then_inc(s_oix, 1)
                pool.wait_ge(s_oix, j + 1)
                pool.sem_inc(s_seen, 1)
                pool.indirect_dma_start(out=XO, out_offset=None, in_=xn_rows,
                                        in_offset=bass.IndirectOffsetOnAxis(ap=idx[0], axis=0)).then_inc(s_ox, 16)
                pool.wait_ge(s_oy, j + 1)
                pool.dma_start(y_rows[bass.ds((j + NE) * P, P), :], y[0]).then_inc(s_oys, 16)
                pool.wait_ge(s_oys, 16 * j + 16)
                pool.sem_inc(s_seen, 1)

            overflow(pool, over)
            for t in range(TT):
                if t >= 4:
                    pool.wait_ge(s_cmb, 2 * (t - 3))
                for k in range(2):
                    pool.indirect_dma_start(out=YG[t % 4][k], out_offset=None, in_=y_rows,
                                            in_offset=bass.IndirectOffsetOnAxis(ap=slot[:, k, t:t + 1], axis=0))\
                        .then_inc(s_yg[t % 4], 16)
            pool.wait_ge(s_cmb, 2 * TT)
            nc.gpsimd.memset(U[:, :, 0:PAD], 0.0).then_inc(s_pad, 1)
            n = 0
            for i, k in enumerate(CONV_ACT):
                pool.wait_ge(s_c0, i + 1)
                for j in range(1, TAPS):
                    n += 1
                    pool.wait_ge(s_pr, n)
                    if j > 1:
                        pool.wait_ge(s_ca, n - 1)
                    nc.gpsimd.tensor_tensor(H[:, k, :], H[:, k, :], prod[n % 3], ALU.add).then_inc(s_ca, 1)
            pool.wait_ge(s_va, 1)
            for n in range(2):
                for i, k in enumerate(LN_POOL):
                    hs = slice(n * 512, n * 512 + 512)
                    nc.gpsimd.tensor_tensor(H[:, k, hs], H[:, k, hs], mean[:, hs], ALU.subtract).then_inc(s_zq, 1)
                    pool.wait_ge(s_zq, len(LN_POOL) * n + i + 1)
                    if n == 0 and i == 0:
                        pool.wait_ge(s_rv, 1)
                    nc.gpsimd.tensor_tensor(H[:, k, hs], H[:, k, hs], rdev[:, hs], ALU.mult).then_inc(s_zp, 1)

        @block.scalar
        def _(act):
            ch = Chain(act, s_act)
            act.wait_ge(s_misc, 16)
            for t in range(TT + 1):
                if t < TT:
                    act.wait_ge(s_x[t], 16)
                    norm_stats(act, ch, t)
                if t:
                    xt_hi(act, 0, t - 1)
                if t in (2, 4, 6, 8):
                    split_hi(act, t // 2 - 1)
            act.wait_ge(s_lam, 1)
            nc.scalar.activation(lexp, lsum, ACT.Exp).then_inc(s_lx, 1)

            def chunk(c):
                for g, ft, tk in chunk_groups(c):
                    if c == 2:
                        act.wait_ge(s_full[g % 4], g // 4 + 1)
                        if tk >= 2:
                            act.wait_ge(s_free[(g - 2) % 4], (g - 2) // 4 + 1)
                        nc.scalar.activation(xn[:, 0, (tk % 2) * 512:(tk % 2) * 512 + 512], PS[:, g % 4, :],
                                             ACT.Sigmoid, scale=IWS).then_inc(s_sig, 1)
                    elif g % 2 == 0:
                        act.wait_ge(s_full[g % 4], g // 4 + 1)
                        nc.scalar.activation(chunk_dest(c, ft, tk), PS[:, g % 4, :], ACT.Copy,
                                             scale=CHUNK_SCALE[c]).then_inc(s_free[g % 4], 1)
                for n in (2 * c + 4, 2 * c + 5):
                    split_hi(act, n)

            for c in range(3):
                chunk(c)
            for n in range(TT):
                act.wait_ge(s_ro, n + 1)
                if n:
                    act.wait_ge(s_rmix, n)
                for h in range(NH):
                    i = nc.scalar.activation(gb[:, h * DV:(h + 1) * DV],
                                             PT[:, 2 + n % 2, h * DV:(h + 1) * DV], ACT.Square,
                                             accum_out=ss4[:, h:h + 1])
                ch.done(i)
                nc.scalar.activation(std4, ss4, ACT.Sqrt, bias=eps, scale=1.0 / DV).then_inc(s_rss, 1)
            for c in range(3, 6):
                chunk(c)

            def t_evac(b):
                i, par = b % TT, b % 2
                act.wait_ge(s_at, b + 1)
                if b >= 2:
                    act.wait_ge(s_ao, b - 1)
                n = min(4, i + 1)
                nc.scalar.activation(aT(par)[:, 0:n, :], tpair(0)[:, 0:n, :], ACT.Copy).then_inc(s_aea, 1)

            def o_evac(b):
                h, i = b // TT, b % TT
                act.wait_ge(s_ao, b + 1)
                nc.scalar.activation(H[:, i, h * DV:(h + 1) * DV], PT[:, 2 + b % 2, 0:DV], ACT.Copy)
                nc.scalar.activation(gb[:, b % 8 * DV:b % 8 * DV + DV], PT[:, 2 + b % 2, 0:DV],
                                     ACT.Square, accum_out=ssA[:, b:b + 1]).then_inc(s_aoe, 1)

            for b in range(NB + 2):
                if b < NB:
                    W = P * (b % TT + 1)
                    for m in range(2):
                        act.wait_ge(s_amx, 2 * b + m + 1)
                        if b >= 2:
                            act.wait_ge(s_at, b - 1)
                        nc.scalar.activation(PB(b % 2, m)[:, 0:W], SC(m)[:, 0:W], ACT.Exp,
                                             bias=negmax[:, 2 * b + m:2 * b + m + 1],
                                             accum_out=rows_sum[:, 2 * b + m:2 * b + m + 1]).then_inc(s_ae, 1)
                if 1 <= b <= NB:
                    t_evac(b - 1)
                if b >= 2:
                    o_evac(b - 2)
            act.wait_ge(s_aoe, NB)
            nc.scalar.activation(stdA, ssA, ACT.Sqrt, bias=eps, scale=1.0 / DV).then_inc(s_std, 1)
            for t in range(TT):
                xt_hi(act, 1, t)
            for t in range(TT + 2):
                if t < TT:
                    g = 49 + 2 * t
                    act.wait_ge(s_free[g % 4], g // 4 + 1)
                    act.wait_ge(s_free[(g - 1) % 4], (g - 1) // 4 + 1)
                    norm_stats(act, ch, t)
                if t >= 2:
                    xt_hi(act, 2, t - 2)
            for g in range(60, 64):
                act.wait_ge(s_full[g % 4], 16)
            for i in range(2):
                expert_hi(act, 2 + i, 0)
            act.wait_ge(s_rd, 1)
            nc.scalar.activation(rex, rex, ACT.Exp).then_inc(s_rx, 1)
            for i in range(2):
                expert_hi(act, i, 0)
            act.wait_ge(s_rd, 2)
            nc.scalar.activation(rde, rde, ACT.Exp).then_inc(s_rx, 1)
            for i in range(2):
                expert_hi(act, 4 + i, 0)

            def xe_hi(e, q):
                act.wait_ge(s_xt, e + 1)
                nc.scalar.activation(xeh[q], tpair(0), ACT.Copy).then_inc(s_xeh, 1)

            for q in range(2):
                xe_hi(q, q)
            for i in range(2):
                expert_hi(act, 2 + i, 1)

            def body(e, q, first, last):
                act.wait_ge(s_g, e + 1)
                if not (first and q == 0):
                    act.wait_ge(s_t, e)
                nc.scalar.activation(sig, PS[:, q, :], ACT.Sigmoid, scale=IWS).then_inc(s_es, 1)
                if not (last and q):
                    for s in (0, 1):
                        expert_hi(act, s, e + 1)
                act.wait_ge(s_ht, e + 1)
                nc.scalar.activation(hTh, PS[:, 3, :].rearrange("p (k t) -> p k t", k=4), ACT.Copy)\
                    .then_inc(s_hh, 1)
                if not last:
                    xe_hi(e + 2, q)
                    for s in (2, 3):
                        expert_hi(act, s, e + 2)
                act.wait_ge(s_d[0], e + 1)
                if not (first):
                    act.wait_ge(s_ys[q], 8 * e if q == 0 else 8 * (e - 1))
                nc.scalar.activation(y[q][:, 0:512], PT[:, 2, :], ACT.Copy, scale=IWS).then_inc(s_y[0], 1)
                if not (last and q):
                    for s in (4, 5):
                        expert_hi(act, s, e + 1)

            pairs(body, act)

            def over(j):
                act.wait_ge(s_ot, 2 * j + 1)
                nc.scalar.activation(XOT.rearrange("p (k t) -> p k t", k=KT), tpair(0), ACT.Copy).then_inc(s_oc, 1)
                act.wait_ge(s_ou, 6 * j + 2)
                nc.scalar.activation(sO, PS[:, 0, :], ACT.Sigmoid).then_inc(s_os, 1)
                act.wait_ge(s_ot, 2 * j + 2)
                nc.scalar.activation(hOT, PS[:, 3, :], ACT.Copy).then_inc(s_oc, 1)
                act.wait_ge(s_ou, 6 * j + 6)
                act.wait_ge(s_ys[0], 16 * NE // 2)
                nc.scalar.activation(y[0], PT[:, 2:4, :].rearrange("p b c -> p (b c)"), ACT.Copy).then_inc(s_oy, 1)
                act.wait_ge(s_oys, 16 * j + 16)
                act.sem_inc(s_seen, 1)

            overflow(act, over)
            for m in range(SLOTS):
                if m == 0:
                    act.wait_ge(s_u, NE)
                    act.wait_ge(s_g, NE)
                hi_b(act, m)
            for t in range(TT + 2):
                if t < TT:
                    act.wait_ge(s_cmb, 2 * t + 2)
                    norm_stats(act, ch, t)
                if 1 <= t <= TT:
                    act.wait_ge(s_x2, t)
                    norm_stats(act, ch, t - 1)
                if t >= 2:
                    xt_hi(act, 3, t - 2)
            act.wait_ge(s_tab, 16)

            act.wait_ge(s_tr, 4 * TT)

            def gated(g):
                i, k, th = conv_in_group(g)
                p = GATED.index((k, th))
                if p >= 2 and i == 0:
                    act.wait_ge(s_cu, p - 1)
                act.wait_ge(s_full[g % 4], g // 4 + 1)
                dst, fn = ((av, ACT.Identity), (sv, ACT.Sigmoid))[i]
                nc.scalar.activation(dst[p % 2], PS[:, g % 4, :], fn, bias=b_in[:, 8 * i + k:8 * i + k + 1],
                                     scale=IWS).then_inc(s_free[g % 4], 1)

            n = [0]

            def product_tap(i, j):
                k = CONV_ACT[i]
                if j == 0:
                    act.wait_ge(s_cu, input_done(k))
                    act.wait_ge(s_pad, 1)
                    act.wait_ge(s_x2s, 16 * TT)
                    act.wait_ge(s_xn, 4 * TT)
                    nc.scalar.activation(H[:, k, :], U[:, k, 0:S], ACT.Identity, bias=cb[:, k:k + 1],
                                         scale=cw[:, k, 0:1]).then_inc(s_c0, 1)
                    return
                n[0] += 1
                if n[0] > 3:
                    act.wait_ge(s_ca, n[0] - 3)
                nc.scalar.activation(prod[n[0] % 3], U[:, k, j:j + S], ACT.Identity, scale=cw[:, k, j:j + 1])\
                    .then_inc(s_pr, 1)

            todo = [(i, j) for i in range(len(CONV_ACT)) for j in range(TAPS)]
            for g in range(64, 96):
                if g in (78, 94):
                    for m in range(2):
                        hi_b(act, 4 + m + (g - 78) // 4)
                gated(g)
                if g == 79:
                    for m in range(2):
                        hi_b(act, 6 + m)
                ready = (g - 63) // 2
                for _ in range(2 + g % 2):
                    if g >= 74 and todo and input_done(CONV_ACT[todo[0][0]]) < ready:
                        product_tap(*todo.pop(0))
            for m in range(10, 12):
                hi_b(act, m)
            for g in range(92, 96):
                act.wait_ge(s_full[g % 4], g // 4 + 1)
            done_sq = [0]

            def squares():
                k = CONV_DONE[done_sq[0]]
                conv_wait(act, k)
                if done_sq[0] >= 2:
                    act.wait_ge(s_st, done_sq[0] - 1)
                nc.scalar.activation(SQ(done_sq[0]), H[:, k, :], ACT.Square).then_inc(s_sq, 1)
                done_sq[0] += 1

            while todo:
                product_tap(*todo.pop(0))
                if todo and todo[0] in ((2, 12), (2, 15), (2, 18), (2, 21)):
                    squares()
            while done_sq[0] < KT:
                squares()
            act.wait_ge(s_va, 1)
            nc.scalar.activation(rdev, var, ACT.Sqrt, bias=eps, scale=1.0).then_inc(s_rd2, 1)
            for n_ in range(2 * KT + 1):
                if n_ < 2 * KT:
                    k, hs = LN_ORDER[n_ % KT], slice(n_ // KT * 512, n_ // KT * 512 + 512)
                    ln_wait(act, n_)
                    if n_ >= 6:
                        act.wait_ge(s_cl, n_ - 5)
                    nc.scalar.activation(silu[n_ % 6], H[:, k, hs], ACT.Silu, bias=lnb[:, k:k + 1],
                                         scale=lng[:, k:k + 1]).then_inc(s_si, 1)
                if n_:
                    act.wait_ge(s_si, n_)
                    k, hs = LN_ORDER[(n_ - 1) % KT], slice((n_ - 1) // KT * 512, (n_ - 1) // KT * 512 + 512)
                    nc.scalar.activation(XH[:, k, hs], silu[(n_ - 1) % 6], ACT.Copy).then_inc(s_ch, 1)
            for t in range(TT + 2):
                if t < TT:
                    g = 97 + 2 * t
                    act.wait_ge(s_free[g % 4], g // 4 + 1)
                    act.wait_ge(s_free[(g - 1) % 4], (g - 1) // 4 + 1)
                    norm_stats(act, ch, t)
                if t >= 2:
                    xt_hi(act, 4, t - 2)
            for s in range(SLOTS):
                mlp_hi(act, s, 0)

            def body(c, last):
                for j in range(9):
                    if j < 8:
                        act.wait_ge(s_full[j % 4], G_MLP + 6 * c + j // 4 + 1)
                        if j >= 2:
                            act.wait_ge(s_ml, 8 * c + j - 1)
                        nc.scalar.activation(relu[j % 2], PS[:, j % 4, :], ACT.Relu, scale=IWS)\
                            .then_inc(s_free[j % 4], 1)
                    if j:
                        h = j - 1
                        act.wait_ge(s_free[h % 4], G_MLP + 6 * c + h // 4 + 1)
                        nc.scalar.activation(HTh[:, h % 4, (h // 4) * 512:(h // 4) * 512 + 512], relu[h % 2],
                                             ACT.Square).then_inc(s_mh, 1)
                if not last:
                    for s in (0, 1):
                        act.wait_ge(s_full[3], G_MLP + 6 * c + 2)
                        mlp_hi(act, s, c + 1)
                    for s in (2, 3):
                        act.wait_ge(s_full[3], G_MLP + 6 * c + 6)
                        act.wait_ge(s_full[2], G_MLP + 6 * c + 6)
                        mlp_hi(act, s, c + 1)

            mlp_chunks(act, body)

        @block.vector
        def _(dve):
            ch = Chain(dve, s_dve)
            dve.wait_ge(s_misc, 16)
            dve.wait_ge(s_gain, 16)
            for t in range(TT + 1):
                if t < TT:
                    norm_scale(dve, ch, 0, t, t + 1)
                if t:
                    xt_lo(dve, 0, t - 1)
                if t in (2, 4, 6, 8):
                    split_lo(dve, t // 2 - 1)
            dve.wait_ge(s_const, 16 * 8)
            lam = lam_in.rearrange("p (j d) -> p j d", j=4)
            for j in range(2):
                ch.done(nc.vector.tensor_tensor(lam_dot[:, j, :], lam[:, 2 * j, :], lam[:, 2 * j + 1, :], ALU.mult))
            nc.vector.tensor_reduce(lsum, lam_dot, AX.X, ALU.add).then_inc(s_lam, 1)
            dve.wait_ge(s_lx, 1)
            ch.done(nc.vector.tensor_tensor(neglam, lexp[:, 1:2], lexp[:, 0:1], ALU.subtract))
            ch.done(nc.vector.tensor_scalar(neglam, neglam, LAMBDA_INIT, None, ALU.subtract))
            ch.done(nc.vector.tensor_scalar(subg, subg, 1.0 - LAMBDA_INIT, None, ALU.mult))

            def chunk(c):
                for g, ft, tk in chunk_groups(c):
                    if c == 2:
                        dve.wait_ge(s_sig, tk + 1)
                        nc.vector.scalar_tensor_tensor(
                            out=chunk_dest(c, ft, tk), in0=PS[:, g % 4, :], scalar=IWS,
                            in1=xn[:, 0, (tk % 2) * 512:(tk % 2) * 512 + 512], op0=ALU.mult, op1=ALU.mult)\
                            .then_inc(s_free[g % 4], 1)
                    elif g % 2 == 1:
                        dve.wait_ge(s_full[g % 4], g // 4 + 1)
                        nc.vector.tensor_scalar(chunk_dest(c, ft, tk), PS[:, g % 4, :], CHUNK_SCALE[c], None,
                                                ALU.mult).then_inc(s_free[g % 4], 1)
                for n in (2 * c + 4, 2 * c + 5):
                    split_lo(dve, n)

            for c in range(3):
                if c == 2:
                    dve.wait_ge(s_cleared, 16 * (NOVER + 1))
                chunk(c)

            def masked(n):
                par, blk = n % 2, slice(n * P, (n + 1) * P)
                dve.wait_ge(s_rsc, n + 1)
                if n >= 2:
                    dve.wait_ge(s_ro, n - 1)
                nc.vector.tensor_tensor(sT[par].rearrange("p (b c) -> p b c", b=2),
                                        PS[:, 2 * par:2 * par + 2, 0:256], decT, ALU.mult)
                nc.vector.tensor_tensor(ktok[par], PT[:, par, 0:256], kdec, ALU.mult)
                for t in range(2):
                    i = nc.vector.tensor_tensor(
                        qd[par][:, t * 256:t * 256 + 256].rearrange("p (j c) -> p j c", j=2),
                        QR[:, t:t + 1, blk].to_broadcast([P, 2, P]), qdec[:, t, :, :], ALU.mult)
                i.then_inc(s_rm, 1)

            def update(n):
                dve.wait_ge(s_ro, n + 1)
                if n == 0:
                    nc.vector.tensor_copy(state, PT[:, n % 2, 256:512]).then_inc(s_rst, 1)
                else:
                    ch.done(nc.vector.tensor_tensor(state, state, cdec, ALU.mult))
                    nc.vector.tensor_tensor(state, PT[:, n % 2, 256:512], state, ALU.add).then_inc(s_rst, 1)

            def mix(n):
                dve.wait_ge(s_rss, n + 1)
                ch.done(nc.vector.reciprocal(rst4, std4))
                for h in range(NH):
                    hs = slice(h * DV, (h + 1) * DV)
                    i = nc.vector.scalar_tensor_tensor(
                        out=H[:, n, 512 + h * DV:512 + (h + 1) * DV], in0=PT[:, 2 + n % 2, hs],
                        scalar=rst4[:, h:h + 1], in1=SG[:, n, hs], op0=ALU.mult, op1=ALU.mult)
                i.then_inc(s_rmix, 1)

            for n in range(TT + 1):
                if n < TT:
                    masked(n)
                if n:
                    update(n - 1)
                    mix(n - 1)
            for c in range(3, 6):
                chunk(c)

            for b in range(NB + 1):
                if b:
                    q, i = b - 1, (b - 1) % TT
                    W = P * (i + 1)
                    dve.wait_ge(s_ae, 2 * q + 2)
                    ch.done(nc.vector.reciprocal(rows_rec[:, 2 * q:2 * q + 2], rows_sum[:, 2 * q:2 * q + 2]))
                    ch.done(nc.vector.tensor_tensor(c1, rows_rec[:, 2 * q + 1:2 * q + 2], neglam, ALU.mult))
                    p0, p1 = PB(q % 2, 0)[:, 0:W], PB(q % 2, 1)[:, 0:W]
                    ch.done(nc.vector.tensor_scalar(p1, p1, c1, None, ALU.mult))
                    nc.vector.scalar_tensor_tensor(out=p0, in0=p0, scalar=rows_rec[:, 2 * q:2 * q + 1], in1=p1,
                                                   op0=ALU.mult, op1=ALU.add).then_inc(s_aa, 1)
                if b < NB:
                    W = P * (b % TT + 1)
                    for m in range(2):
                        dve.wait_ge(s_as, 2 * b + m + 1)
                        nc.vector.tensor_reduce(negmax[:, 2 * b + m:2 * b + m + 1], SC(m)[:, 0:W], AX.X, ALU.max,
                                                negate=True).then_inc(s_amx, 1)
                if b:
                    if i >= 4:
                        dve.wait_ge(s_at, q + 1)
                        if q >= 2:
                            dve.wait_ge(s_ao, q - 1)
                        nc.vector.tensor_copy(aT(q % 2)[:, 4:i + 1, :], tpair(0)[:, 4:i + 1, :])\
                            .then_inc(s_aed, 1)
            dve.wait_ge(s_std, TT + 1)
            ch.done(nc.vector.reciprocal(rstA, stdA))
            dve.wait_ge(s_rmix, TT)
            for t in range(TT + 1):
                if t < TT:
                    xn_wait(dve, 1, t)
                    for h in range(NH):
                        hs = slice(h * DV, (h + 1) * DV)
                        i = nc.vector.scalar_tensor_tensor(
                            out=xn[:, t % 2, hs], in0=H[:, t, hs], scalar=rstA[:, h * TT + t:h * TT + t + 1],
                            in1=subg, op0=ALU.mult, op1=ALU.mult)
                    i.then_inc(s_xn, 1)
                if t:
                    xt_lo(dve, 1, t - 1)
            dve.wait_ge(s_router_w, 32)
            ch.done(nc.vector.tensor_scalar(rwh, rw, WS, None, ALU.mult))
            nc.vector.scalar_tensor_tensor(out=rwl, in0=rw, scalar=WS, in1=rwh, op0=ALU.mult, op1=ALU.subtract)\
                .then_inc(s_rws, 1)
            dve.wait_ge(s_gain, 32)
            for t in range(TT + 2):
                if t < TT:
                    dve.wait_ge(s_x[t], 32)
                    for c in range(2):
                        g = 48 + 2 * t + c
                        dve.wait_ge(s_full[g % 4], g // 4 + 1)
                        nc.vector.scalar_tensor_tensor(out=H[:, t, c * 512:c * 512 + 512], in0=PS[:, g % 4, :],
                                                       scalar=IWS, in1=H[:, t, c * 512:c * 512 + 512],
                                                       op0=ALU.mult, op1=ALU.add).then_inc(s_free[g % 4], 1)
                if 1 <= t <= TT:
                    if t >= 3:
                        dve.wait_ge(s_xs[(t - 1) % 2], 16 * ((t - 1) // 2))
                    norm_scale(dve, ch, 2, t - 1, TT + 1 + t)
                if t >= 2:
                    xt_lo(dve, 2, t - 2)
            for i in range(2):
                expert_lo(dve, 2 + i, 0)
            router(dve, ch)

            for i in range(2):
                expert_lo(dve, i, 0)

            def xe_lo(e, q):
                dve.wait_ge(s_xeh, e + 1)
                nc.vector.tensor_tensor(xel[q], tpair(0), xeh[q], ALU.subtract).then_inc(s_xel, 1)

            for q in range(2):
                xe_lo(q, q)
            for i in range(2):
                expert_lo(dve, 4 + i, 0)
            for i in range(2):
                expert_lo(dve, 2 + i, 1)

            def body(e, q, first, last):
                dve.wait_ge(s_es, e + 1)
                nc.vector.scalar_tensor_tensor(out=tbuf, in0=PS[:, q, :], scalar=IWS, in1=sig,
                                               op0=ALU.mult, op1=ALU.mult).then_inc(s_t, 1)
                dve.wait_ge(s_u, e + 1)
                dve.wait_ge(s_t, e + 1)
                if not (first and q == 0):
                    dve.wait_ge(s_ht, e)
                nc.vector.scalar_tensor_tensor(out=hbuf, in0=PS[:, 2, :], scalar=IWS, in1=tbuf,
                                               op0=ALU.mult, op1=ALU.mult).then_inc(s_h, 1)
                if not (last and q):
                    expert_lo(dve, 0, e + 1)
                dve.wait_ge(s_hh, e + 1)
                nc.vector.tensor_tensor(hTl, PS[:, 3, :].rearrange("p (k t) -> p k t", k=4), hTh, ALU.subtract)\
                    .then_inc(s_hl, 1)
                if not (last and q):
                    expert_lo(dve, 1, e + 1)
                if not last:
                    xe_lo(e + 2, q)
                    for s in (2, 3):
                        expert_lo(dve, s, e + 2)
                dve.wait_ge(s_d[1], e + 1)
                if not (first):
                    dve.wait_ge(s_ys[q], 8 * e if q == 0 else 8 * (e - 1))
                nc.vector.tensor_scalar(y[q][:, 512:1024], PT[:, 3, :], IWS, None, ALU.mult).then_inc(s_y[1], 1)
                if not (last and q):
                    expert_lo(dve, 4, e + 1)
                if last and not q:
                    expert_lo(dve, 5, e + 1)

            pairs(body, dve)

            def over(j):
                dve.wait_ge(s_os, j + 1)
                nc.vector.tensor_tensor(sO, PS[:, 0, :], sO, ALU.mult).then_inc(s_og, 1)
                dve.wait_ge(s_og, j + 1)
                dve.wait_ge(s_ou, 6 * j + 4)
                nc.vector.tensor_tensor(hO, PS[:, 1, :], sO, ALU.mult).then_inc(s_oh, 1)

            overflow(dve, over)
            for m in range(SLOTS):
                lo_b(dve, m)
            dve.wait_ge(s_gain, 64)
            for t in range(TT + 3):
                if t < TT:
                    dve.wait_ge(s_yg[t % 4], 32 * (t // 4 + 1))
                    for k in range(2):
                        nc.vector.scalar_tensor_tensor(out=H[:, t, :], in0=YG[t % 4][k], scalar=wk[:, k, t:t + 1],
                                                       in1=H[:, t, :], op0=ALU.mult, op1=ALU.add).then_inc(s_cmb, 1)
                        dve.wait_ge(s_cmb, 2 * t + k + 1)
                if 1 <= t <= TT:
                    u = t - 1
                    dve.wait_ge(s_std, 2 * TT + 1 + first_dev(u))
                    ch.done(nc.vector.reciprocal(rstd[:, u:u + 1], std[:, u:u + 1]))
                    nc.vector.scalar_tensor_tensor(out=H[:, u, :], in0=H[:, u, :], scalar=rstd[:, u:u + 1],
                                                   in1=gb[:, :], op0=ALU.mult, op1=ALU.mult).then_inc(s_x2, 1)
                if 2 <= t <= TT + 1:
                    u = t - 2
                    dve.wait_ge(s_std, 2 * TT + 1 + second_dev(u))
                    ch.done(nc.vector.reciprocal(rstd[:, u:u + 1], std[:, u:u + 1]))
                    xn_wait(dve, 3, u)
                    nc.vector.scalar_tensor_tensor(out=xn[:, u % 2, :], in0=H[:, u, :], scalar=rstd[:, u:u + 1],
                                                   in1=gm, op0=ALU.mult, op1=ALU.mult).then_inc(s_xn, 1)
                if t >= 3:
                    xt_lo(dve, 3, t - 3)

            nw = {}
            started = []

            def tap(k, j):
                if j == 0:
                    if not started:
                        dve.wait_ge(s_x2s, 16 * TT)
                        dve.wait_ge(s_pad, 1)
                        started.append(k)
                    dve.wait_ge(s_cu, input_done(k))
                    i = nc.vector.tensor_scalar(H[:, k, :], U[:, k, 0:S], cw[:, k, 0:1], cb[:, k:k + 1],
                                                ALU.mult, ALU.add)
                else:
                    dve.wait_ge(s_dve, nw[k])
                    i = nc.vector.scalar_tensor_tensor(out=H[:, k, :], in0=U[:, k, j:j + S], scalar=cw[:, k, j:j + 1],
                                                       in1=H[:, k, :], op0=ALU.mult, op1=ALU.add)
                if j == TAPS - 1:
                    i.then_inc(s_cd, 1)
                else:
                    i.then_inc(s_dve, 1)
                    ch.n += 1
                    nw[k] = ch.n

            plan = tap_schedule()
            for p, (k, th) in enumerate(GATED):
                for g in gate_groups(p):
                    dve.wait_ge(s_free[g % 4], g // 4 + 1)
                nc.vector.tensor_tensor(U[:, k, PAD + th * 512:PAD + th * 512 + 512], av[p % 2], sv[p % 2], ALU.mult)\
                    .then_inc(s_cu, 1)
                if p in (6, 14):
                    for m in range(2):
                        lo_b(dve, 4 + m + (p - 6) // 2)
                for x in plan[p]:
                    tap(*x)
                if p == 7:
                    for m in range(2):
                        lo_b(dve, 6 + m)
            for m in range(10, 12):
                lo_b(dve, m)
            for x in plan[-1]:
                tap(*x)
            dve.wait_ge(s_st, KT)
            s1 = PS[:, 0:2, :].rearrange("p b c -> p (b c)")
            s2 = PS[:, 2:4, :].rearrange("p b c -> p (b c)")
            ch.done(nc.vector.tensor_scalar(mean, s1, 1.0 / D, None, ALU.mult))
            ch.done(nc.vector.tensor_tensor(var, mean, mean, ALU.mult))
            nc.vector.scalar_tensor_tensor(out=var, in0=s2, scalar=1.0 / D, in1=var, op0=ALU.mult, op1=ALU.subtract)\
                .then_inc(s_va, 1)
            halves = [(n // KT, n % KT) for n in range(2 * KT)]
            mine = [(hf, k) for hf, k in halves if k not in LN_POOL]

            def centre(hf, k):
                hs = slice(hf * 512, hf * 512 + 512)
                return nc.vector.tensor_tensor(H[:, k, hs], H[:, k, hs], mean[:, hs], ALU.subtract)

            for x in mine[0:2]:
                i = centre(*x)
            ch.done(i)
            dve.wait_ge(s_rd2, 1)
            nc.vector.reciprocal(rdev, rdev).then_inc(s_rv, 1)
            dve.wait_ge(s_rv, 1)
            centred = {x: None for x in mine[0:2]}
            for n in range(2 * KT + 2):
                if n < 2 * KT and halves[n] in mine:
                    q = mine.index(halves[n])
                    if mine[q] in centred and centred[mine[q]]:
                        dve.wait_ge(s_dve, centred[mine[q]])
                    hf, k = mine[q]
                    hs = slice(hf * 512, hf * 512 + 512)
                    nc.vector.tensor_tensor(H[:, k, hs], H[:, k, hs], rdev[:, hs], ALU.mult).then_inc(s_z, 1)
                    if q + 2 < len(mine):
                        centre(*mine[q + 2]).then_inc(s_dve, 1)
                        ch.n += 1
                        centred[mine[q + 2]] = ch.n
                if n >= 2:
                    k, hs = (n - 2) % KT, slice((n - 2) // KT * 512, (n - 2) // KT * 512 + 512)
                    dve.wait_ge(s_ch, n - 1)
                    nc.vector.tensor_tensor(XL[:, k, hs], silu[(n - 2) % 6], XH[:, k, hs], ALU.subtract)\
                        .then_inc(s_cl, 1)
            dve.wait_ge(s_bo, 16)
            dve.wait_ge(s_gain, 80)
            for t in range(TT + 2):
                if t < TT:
                    dve.wait_ge(s_x[t], 48)
                    ch.done(nc.vector.tensor_tensor(H[:, t, :], H[:, t, :], bo, ALU.add))
                    for c in range(2):
                        g = 96 + 2 * t + c
                        dve.wait_ge(s_full[g % 4], g // 4 + 1)
                        nc.vector.scalar_tensor_tensor(out=H[:, t, c * 512:c * 512 + 512], in0=PS[:, g % 4, :],
                                                       scalar=IWS, in1=H[:, t, c * 512:c * 512 + 512],
                                                       op0=ALU.mult, op1=ALU.add).then_inc(s_free[g % 4], 1)
                if 1 <= t <= TT:
                    norm_scale(dve, ch, 4, t - 1, 4 * TT + 1 + t)
                if t >= 2:
                    xt_lo(dve, 4, t - 2)
            for s in range(SLOTS):
                mlp_lo(dve, s, 0)

            def body(c, last):
                for j in range(9):
                    if j < 8:
                        dve.wait_ge(s_free[j % 4], G_MLP + 6 * c + j // 4 + 1)
                        nc.vector.tensor_tensor(relu2[j % 2], relu[j % 2], relu[j % 2], ALU.mult).then_inc(s_relu, 1)
                    if j:
                        h = j - 1
                        dve.wait_ge(s_mh, 8 * c + j)
                        dve.wait_ge(s_relu, 8 * c + j)
                        nc.vector.tensor_tensor(HTl[:, h % 4, (h // 4) * 512:(h // 4) * 512 + 512], relu2[h % 2],
                                                HTh[:, h % 4, (h // 4) * 512:(h // 4) * 512 + 512], ALU.subtract)\
                            .then_inc(s_ml, 1)
                if not last:
                    for s in (0, 1):
                        mlp_lo(dve, s, c + 1)
                for j in range(8, 24):
                    t, n = (j - 8) // 2, j % 2
                    hs = slice(n * 512, n * 512 + 512)
                    dve.wait_ge(s_full[j % 4], G_MLP + 6 * c + j // 4 + 1)
                    nc.vector.scalar_tensor_tensor(out=H[:, t, hs], in0=PS[:, j % 4, :], scalar=IWS, in1=H[:, t, hs],
                                                   op0=ALU.mult, op1=ALU.add).then_inc(s_free[j % 4], 1)
                if not last:
                    for s in (2, 3):
                        mlp_lo(dve, s, c + 1)

            mlp_chunks(dve, body)

        @block.tensor
        def _(pe):
            pe.wait_ge(s_misc, 16)
            from_xn = lambda t, k: xn[:, t % 2, k * P:(k + 1) * P]
            for t in range(TT // 2):
                transposes(pe, 0, t, from_xn)

            def chunk(c):
                gs = chunk_groups(c)
                for g, ft, tk in gs:
                    if c == 0:
                        pe.wait_ge(s_xl, TT if tk else TT // 2)
                    group(pe, g, (2 * c, 2 * c + 1), FM[c], ft, tk)
                    if g < TT // 2:
                        transposes(pe, 0, TT // 2 + g, from_xn)
                if c == 0:
                    pe.wait_ge(s_const, 16 * 8)

            for c in range(3):
                chunk(c)
            for b in range(4):
                pe.wait_ge(s_free[b], 6)

            def scores(n):
                par, blk = n % 2, slice(n * P, (n + 1) * P)
                if n >= 2:
                    pe.wait_ge(s_rm, n - 1)
                    pe.wait_ge(s_rst, n - 1)
                for h in range(NH):
                    t, r = h // 2, slice(DH * (h % 2), DH * (h % 2) + DH)
                    nc.tensor.matmul(PS[:, 2 * par + h % 2, t * P:(t + 1) * P], KR[r, t, blk], QR[r, t, blk],
                                     start=True, stop=True)
                for t in range(2):
                    i = nc.tensor.transpose(PT[:, par, t * P:(t + 1) * P], KR[:, t, blk], ident)
                i.then_inc(s_rsc, 1)

            def outputs(n):
                par = n % 2
                pe.wait_ge(s_rm, n + 1)
                if n:
                    pe.wait_ge(s_rst, n)
                for h in range(NH):
                    t, r0 = h // 2, DH * (h % 2)
                    nc.tensor.matmul(PT[r0:r0 + DH, par, 256 + t * DV:256 + (t + 1) * DV], ktok[par][:, h * DH:(h + 1) * DH],
                                     VR[:, n, h * DV:(h + 1) * DV], start=True, stop=True)
                if n >= 2:
                    pe.wait_ge(s_rmix, n - 1)
                for h in range(NH):
                    t, j = h // 2, 2 * (h % 2) + h // 2
                    o = PT[:, 2 + par, h * DV:(h + 1) * DV]
                    i = nc.tensor.matmul(o, sT[par][:, j * P:(j + 1) * P], VR[:, n, h * DV:(h + 1) * DV],
                                         start=True, stop=n == 0)
                    if n:
                        i = nc.tensor.matmul(o, qd[par][:, h * P:(h + 1) * P], state[:, t * DV:(t + 1) * DV],
                                             start=False, stop=True)
                i.then_inc(s_ro, 1)

            for n in range(TT + 1):
                if n < TT:
                    scores(n)
                if n:
                    outputs(n - 1)
            for c in range(3, 6):
                if c == 3:
                    pe.wait_ge(s_rm, TT)
                    pe.wait_ge(s_rst, TT)
                    pe.wait_ge(s_rmix, TT)
                chunk(c)
            for b in range(4):
                pe.wait_ge(s_free[b], 12)

            def att_scores(b):
                h, i = b // TT, b % TT
                W = P * (i + 1)
                qs = slice(i * P, (i + 1) * P)
                for m in range(2):
                    r = slice(m * DH, (m + 1) * DH)
                    if b:
                        pe.wait_ge(s_ae, 2 * (b - 1) + m + 1)
                    for c0 in range(0, W, 512):
                        n = min(512, W - c0)
                        o = SC(m)[:, c0:c0 + n]
                        diag = c0 + n == W
                        nc.tensor.matmul(o, Q[r, h, qs], K[r, h, c0:c0 + n], start=True, stop=False)
                        j = nc.tensor.matmul(o, pos_q[:, h, :], pos_k[:, S - W + c0:S - W + c0 + n],
                                             start=False, stop=not diag)
                        if diag:
                            j = nc.tensor.matmul(SC(m)[:, W - P:W], identb, corr[:, h, :], start=False, stop=True)
                    j.then_inc(s_as, 1)

            def att_transposes(b):
                i = b % TT
                pe.wait_ge(s_aa, b + 1)
                if b:
                    pe.wait_ge(s_aea, b)
                    pe.wait_ge(s_aed, late(b))
                for k in range(i + 1):
                    j = nc.tensor.transpose(tpair(0)[:, k, :], PB(b % 2, 0)[:, k * P:(k + 1) * P], ident)
                j.then_inc(s_at, 1)

            def late(b):
                return sum(1 for q in range(b) if q % TT >= 4)

            def att_out(b):
                h, i = b // TT, b % TT
                pe.wait_ge(s_aea, b + 1)
                pe.wait_ge(s_aed, late(b + 1))
                if b >= 2:
                    pe.wait_ge(s_aoe, b - 1)
                for k in range(i + 1):
                    j = nc.tensor.matmul(PT[:, 2 + b % 2, 0:DV], aT(b % 2)[:, k, :], V[:, k, h * DV:(h + 1) * DV],
                                         start=k == 0, stop=k == i)
                j.then_inc(s_ao, 1)

            for b in range(NB + 2):
                if b < NB:
                    att_scores(b)
                if 1 <= b <= NB:
                    att_transposes(b - 1)
                if b >= 2:
                    att_out(b - 2)
            mixed = lambda t, k: xn[:, t % 2, k * P:(k + 1) * P] if k < 4 else H[:, t, k * P:(k + 1) * P]
            for t in range(2):
                transposes(pe, 1, t, mixed)
            for t in range(TT + 2):
                if t < TT:
                    pe.wait_ge(s_xl, TT + t + 1)
                    for c in range(2):
                        g = 48 + 2 * t + c
                        group(pe, g, (12 + 2 * c, 13 + 2 * c), False, 0, t)
                        if g < 51:
                            for u in range(2):
                                transposes(pe, 1, 2 * (g - 47) + u, mixed)
                if t >= 2:
                    transposes(pe, 2, t - 2, from_xn)
            pe.wait_ge(s_rws, 1)
            pe.wait_ge(s_xl, 3 * TT)
            for b in range(4):
                pe.wait_ge(s_free[b], 16)
            for t in range(TT):
                for k in range(KT):
                    tk, c = slice(t * P, (t + 1) * P), slice(k * 36, k * 36 + 36)
                    i = product(pe, PS[:, 0, t * 36:(t + 1) * 36], XH[:, k, tk], XL[:, k, tk], rwh[:, c], rwl[:, c],
                                k == 0, k == KT - 1)
            i.then_inc(s_lg, 1)
            pe.wait_ge(s_rt, 1)
            for t in range(TT):
                for j in range(t + 1):
                    nc.tensor.matmul(PS[:, 1, t * NE:(t + 1) * NE], tri if j == t else onesb, rM[:, j, :],
                                     start=j == 0, stop=j == t)
            for j in range(TT):
                i = nc.tensor.matmul(PS[0:NE, 2, 0:1], rM[:, j, :], onesb[:, 0:1], start=j == 0, stop=j == TT - 1)
            i.then_inc(s_rp, 1)
            pe.wait_ge(s_rt, 2)
            nc.tensor.matmul(PS[:, 3, 0:NE], rexb[0:NE, :], tri[0:NE, 0:NE], start=True, stop=True)
            nc.tensor.matmul(PS[:, 3, NE:2 * NE], rexb[0:NE, :], tri[0:NE, 0:NE], start=True, stop=False)
            nc.tensor.matmul(PS[:, 3, NE:2 * NE], rexb[0:NE, :], identb[0:NE, 0:NE], start=False, stop=True)\
                .then_inc(s_rp, 1)
            pe.wait_ge(s_rt, 3)
            for n in range(2 * TT):
                i = nc.tensor.matmul(PS[:, 0, 0:BLK_MAX + 1], rA[:, n, :], rB[:, n, :],
                                     start=n == 0, stop=n == 2 * TT - 1)
            i.then_inc(s_rp, 1)

            def x_transposes(e, q):
                pe.wait_ge(s_gx[q], 16 * (e // 2 + 1) if isinstance(e, int) else 8 * (e - q) + 16)
                if not (isinstance(e, int) and e == 0):
                    pe.wait_ge(s_xel, e)
                for k in range(KT):
                    i = nc.tensor.transpose(tpair(0)[:, k, :], XG[q][:, k * P:(k + 1) * P], ident)
                i.then_inc(s_xt, 1)

            pe.wait_ge(s_slots, 1)
            for q in range(2):
                x_transposes(q, q)
            pe.wait_ge(s_xel, 1)
            expert_product(pe, PS[:, 0, :], 2, 0, xeh[0], xel[0], s_g)

            def h_transposes(e, very_first):
                pe.wait_ge(s_h, e + 1)
                if not very_first:
                    pe.wait_ge(s_hl, e)
                for k in range(4):
                    i = nc.tensor.transpose(PS[:, 3, k * P:(k + 1) * P], hbuf[:, k * P:(k + 1) * P], ident)
                i.then_inc(s_ht, 1)

            def body(e, q, first, last):
                if not (first and q == 0):
                    pe.wait_ge(s_h, e)
                expert_product(pe, PS[:, 2, :], 0, e, xeh[q], xel[q], s_u)
                if not (last and q):
                    if not (first and q == 0):
                        pe.wait_ge(s_t, e)
                    pe.wait_ge(s_xel, e + 2)
                    expert_product(pe, PS[:, 1 - q, :], 2, e + 1, xeh[1 - q], xel[1 - q], s_g,
                                   between=lambda: h_transposes(e, first and q == 0))
                else:
                    h_transposes(e, False)
                if not last:
                    x_transposes(e + 2, q)
                pe.wait_ge(s_hl, e + 1)
                for i in range(2):
                    s = 4 + i
                    pe.wait_ge(s_wo[s], BASE[s] + 1 + e)
                    if not (first and q == 0):
                        pe.wait_ge(s_y[i], e)
                    for k in range(UK):
                        c = slice(k * UC, k * UC + UC)
                        m = product(pe, PT[:, 2 + i, :], hTh[:, k, :], hTl[:, k, :], whi(s)[:, c], wlo(s)[:, c],
                                    k == 0, k == UK - 1)
                    m.then_inc(s_d[i], 1)

            pairs(body, pe)

            def over(j):
                for c in (s_h, s_t, s_hl, s_xel, s_y[0], s_y[1]):
                    pe.wait_ge(c, NE)
                pe.wait_ge(s_ox, 16 * j + 16)
                for k in range(KT):
                    i = nc.tensor.transpose(tpair(0)[:, k, :], XO[:, k * P:(k + 1) * P], ident)
                i.then_inc(s_ot, 1)
                pe.wait_ge(s_oc, 2 * j + 1)
                for u in range(6):
                    pe.wait_ge(s_ow, 96 * j + 16 * u + 16)
                    if u == 4:
                        pe.wait_ge(s_oh, j + 1)
                        for k in range(4):
                            i = nc.tensor.transpose(PS[:, 3, k * P:(k + 1) * P], hO[:, k * P:(k + 1) * P], ident)
                        i.then_inc(s_ot, 1)
                        pe.wait_ge(s_oc, 2 * j + 2)
                    for kk in range(UK):
                        c = slice(kk * UC, kk * UC + UC)
                        if u < 4:
                            k = u % 2 * UK + kk
                            i = nc.tensor.matmul(PS[:, u // 2, :], XOT[:, k * P:(k + 1) * P], wO[:, c],
                                                 start=k == 0, stop=k == KT - 1)
                        else:
                            i = nc.tensor.matmul(PT[:, u - 2, :], hOT[:, kk * P:(kk + 1) * P], wO[:, c],
                                                 start=kk == 0, stop=kk == UK - 1)
                    i.then_inc(s_ou, 1)
                pe.wait_ge(s_oy, j + 1)

            overflow(pe, over)
            for t in range(TT // 2):
                transposes(pe, 3, t, from_xn)
            for c in (s_h, s_t, s_hl):
                pe.wait_ge(c, NE)
            for g in range(64, 96):
                i, k, th = conv_in_group(g)
                pe.wait_ge(s_xl, 3 * TT + (TT if th else TT // 2))
                u = 4 * (k // 4) + 2 * i
                group_b(pe, g, (u, u + 1), True, k % 4, th)
                if g < 68:
                    transposes(pe, 3, TT // 2 + g - 64, from_xn)
            for b in range(4):
                pe.wait_ge(s_free[b], 24)
            ones = misc[:, M_ONE:M_ONE + P]
            for n, k in enumerate(CONV_DONE):
                conv_wait(pe, k)
                pe.wait_ge(s_sq, n + 1)
                for th in range(2):
                    hs = slice(th * 512, th * 512 + 512)
                    nc.tensor.matmul(PS[:, th, :], ones, H[:, k, hs], start=n == 0, stop=n == KT - 1)
                    i = nc.tensor.matmul(PS[:, 2 + th, :], ones, SQ(n)[:, hs], start=n == 0, stop=n == KT - 1)
                i.then_inc(s_st, 1)
            for t in range(TT + 2):
                if t < TT:
                    pe.wait_ge(s_cl, KT if t < TT // 2 else 2 * KT)
                    for c in range(2):
                        group_b(pe, 96 + 2 * t + c, (8 + 2 * c, 9 + 2 * c), False, 0, t)
                if t >= 2:
                    transposes(pe, 4, t - 2, from_xn)
            pe.wait_ge(s_xl, 5 * TT)

            def body(c, last):
                for j in range(8):
                    th, ft = j // 4, j % 4
                    pe.wait_ge(s_free[j % 4], G_MLP + 6 * c + j // 4)
                    for s in range(2):
                        pe.wait_ge(s_wo[s], RM + 1 + c)
                        for kk in range(UK):
                            k = s * UK + kk
                            cs = slice(kk * UC + ft * P, kk * UC + ft * P + P)
                            ts = slice(th * 512, th * 512 + 512)
                            i = product(pe, PS[:, j % 4, :], whi(s)[:, cs], wlo(s)[:, cs], XH[:, k, ts], XL[:, k, ts],
                                        k == 0, k == KT - 1)
                    i.then_inc(s_full[j % 4], 1)
                for j in range(8, 24):
                    t, n = (j - 8) // 2, j % 2
                    s = 2 + n
                    pe.wait_ge(s_free[j % 4], G_MLP + 6 * c + j // 4)
                    pe.wait_ge(s_wo[s], RM + 1 + c)
                    pe.wait_ge(s_ml, 8 * c + (4 if t < 4 else 8))
                    ts = slice(t * P, (t + 1) * P)
                    for k in range(UK):
                        cs = slice(k * UC, k * UC + UC)
                        i = product(pe, PS[:, j % 4, :], HTh[:, k, ts], HTl[:, k, ts], whi(s)[:, cs], wlo(s)[:, cs],
                                    k == 0, k == UK - 1)
                    i.then_inc(s_full[j % 4], 1)

            mlp_chunks(pe, body)


def unit_layout(w):
    k, n = w.shape
    u = w.reshape(k // (UK * P), UK, P, n // UC, UC).transpose(3, 0, 2, 1, 4)
    return u.reshape(-1, P, UK * UC)


def by_channel(v):
    return v.reshape(-1, P).T


def expert_layout(w):
    return np.concatenate([unit_layout(v) for v in w])


def kernel(**inputs):
    import concourse.bacc as _bacc
    from concourse.bass_utils import run_bass_kernel_spmd as _run

    f = {k: np.ascontiguousarray(v) for k, v in inputs.items()}
    w_in = unit_layout(f["w_in"][0])
    order = [3, 4, 5, 0, 1, 2]
    w_ai = unit_layout(f["a_w_in_2"][0])
    NCH = DFF // UC
    w_a = np.concatenate([w_in[2 * c:2 * c + 2] for c in order] + [unit_layout(f["w_out"][0])])
    arrays = {
        "x": f["x"].reshape(TT, P, D),
        "gains": np.concatenate([f["attn_norm_g"], f["ffn_norm_g"], f["final_norm_g"][None], f["mix_norm_2"],
                                 f["mlp_norm_2"], f["a_b_out_2"]]),
        "lambdas": np.concatenate([f["da_lambda_q1"], f["da_lambda_k1"], f["da_lambda_q2"], f["da_lambda_k2"]]),
        "subln_g": f["da_subln_g"],
        "w_dense_a": w_a,
        "router_w": np.concatenate([f["router_group_w"][0], f["router_expert_w"][0]], axis=1)
        .reshape(KT, P, NG + NE).transpose(1, 0, 2).reshape(P, -1),
        "router_b": np.concatenate([f["router_group_b"], f["router_expert_b"]], axis=1),
        "conv_tables": np.concatenate([
            f["a_conv_w_2"][0].reshape(TAPS, KT, P).transpose(2, 1, 0).reshape(P, -1),
            by_channel(f["a_conv_b_2"]), by_channel(f["a_ln_g_2"]), by_channel(f["a_ln_b_2"]),
            by_channel(f["a_b_in_2"])], axis=1),
        "w_dense_b": np.concatenate([w_ai[0:2], w_ai[4:6], w_ai[2:4], w_ai[6:8], unit_layout(f["a_w_out_2"][0])]),
        "w_mlp": np.concatenate([unit_layout(f["mlp_w1_2"][0]).reshape(NCH, 2, P, UK * UC),
                                 unit_layout(f["mlp_w2_2"][0]).reshape(2, NCH, P, UK * UC).transpose(1, 0, 2, 3)],
                                axis=1).reshape(-1, P, UK * UC),
        "w_gate": expert_layout(f["expert_w_gate"][0]),
        "w_up": expert_layout(f["expert_w_up"][0]),
        "w_down": expert_layout(f["expert_w_down"][0]),
        **constants(),
    }
    nc = _bacc.Bacc("TRN2", target_bir_lowering=False, num_devices=1)
    sent, aps = {}, {}
    for name, value in arrays.items():
        value = np.ascontiguousarray(value)
        sent["in_" + name] = value
        aps[name] = nc.dram_tensor("in_" + name, value.shape, mybir.dt.from_np(value.dtype),
                                   kind="ExternalInput").ap()
    out = nc.dram_tensor("out_0", (S, D), F32, kind="ExternalOutput").ap()
    build(nc, aps, out)
    r = _run(nc, [sent], core_ids=[0])
    return r.results[0]["out_0"].reshape(1, S, D)
```

```python
import math
from contextlib import ExitStack

import numpy as np
import concourse.bass as bass
from concourse import mybir

F32 = mybir.dt.float32
F16 = mybir.dt.float16
BF16 = mybir.dt.bfloat16
I32 = mybir.dt.int32
ALU = mybir.AluOpType
ACT = mybir.ActivationFunctionType
AX = mybir.AxisListType

P = 128
S = 1024
D = 1024
TT = S // P
KT = D // P
NH = 4
DH = 64
DV = 128
CHUNK = 64
EPS = 1e-6
NE = 32
NG = 4
EG = NE // NG
DFF = 4 * D
TAPS = 31
LAMBDA_INIT = 0.8 - 0.6 * math.exp(-0.3 * 0)
WS = 64.0
IWS = 1.0 / WS
UC = 512
UK = 4
SLOTS = 4
BLK_MAX = NE + 15
NOVER = BLK_MAX - NE
PAD = TAPS - 1

DENSE_A = 16


def constants():
    p = np.arange(P)
    slopes = 2.0 ** (-8.0 * np.arange(1, NH + 1) / NH)
    lg = np.log1p(-(2.0 ** (-5.0 - np.arange(NH))))
    rel = p[None, :] - p[:, None]
    by_bank = [0, 2, 1, 3]
    dec = np.where(rel[:, None, :] >= 0, np.exp(lg[None, :, None] * np.maximum(rel, 0)[:, None, :]), 0.0) * DH ** -0.5
    dec = dec[:, by_bank]
    kdec = np.repeat(np.exp(lg[None, :] * (P - 1 - p)[:, None]) * DH ** -0.5, DH, axis=1)
    head_of = lambda t: 2 * t + (p // DH)
    qdec = np.stack([np.where((p // DH == h % 2)[:, None], np.exp(lg[h] * (p + 1.0))[None, :], 0.0)
                     for h in range(NH)], axis=1)
    cdec = np.stack([np.repeat(np.exp(lg[head_of(t)] * P)[:, None], DV, axis=1) for t in range(2)], axis=1)
    ret = np.concatenate([dec.reshape(P, -1), kdec, qdec.reshape(P, -1), cdec.reshape(P, -1)], axis=1)
    ar = lambda n: np.tile(np.arange(n, dtype=np.float64), (P, 1))
    tok = np.arange(TT)[None, :] * P + p[:, None]
    misc = np.concatenate([np.eye(P), ar(P), ar(BLK_MAX + 1), NE - ar(NE), tok,
                           np.full((P, 1), EPS), np.ones((P, P))], axis=1)
    k, q = p[None, :], p[:, None]
    corr = np.stack([np.where(k // CHUNK > q // CHUNK, -1e30, np.where(k > q, -2.0 * s * (k - q), 0.0))
                     for s in slopes], axis=1)
    half = np.concatenate([np.eye(P), corr.reshape(P, -1), np.triu(np.ones((P, P)), 1), np.ones((P, P))],
                          axis=1).astype(np.float32)
    half = np.ascontiguousarray((half.view(np.uint32) >> 16).astype(np.uint16)).view(np.float32)
    pos_k = np.stack([np.arange(S) - (S - P), np.ones(S)])
    pos_q = np.stack([np.repeat(slopes, P), np.concatenate([-s * p for s in slopes])])
    pos = np.concatenate([pos_k, pos_q], axis=1).astype(np.float16)
    return {"c_ret": ret.astype(np.float32), "c_misc": misc.astype(np.float32), "c_half": half, "c_pos": pos}


RET_COLS = NH * P + NH * DH + NH * P + 2 * DV
M_ID, M_IO, M_IOB = 0, P, 2 * P
M_REV = M_IOB + BLK_MAX + 1
M_TOK = M_REV + NE
M_EPS = M_TOK + TT
M_ONE = M_EPS + 1
MISC_COLS = M_ONE + P


class Chain:

    def __init__(self, engine, sem, base=0):
        self.engine, self.sem, self.n, self.base = engine, sem, 0, base

    def done(self, instruction):
        self.n += 1
        instruction.then_inc(self.sem, 1)
        self.engine.wait_ge(self.sem, self.base + self.n)


def build(nc, a, out):
    with ExitStack() as ctx:
        def sb(name, cols, dt=F32, rows=P):
            return ctx.enter_context(nc.sbuf_tensor(name, [rows, cols], dt))

        def sem(name):
            return ctx.enter_context(nc.semaphore(name))

        H = sb("resid", TT * D)[:, :].rearrange("p (t d) -> p t d", t=TT)
        XTF = sb("xt", 2 * KT * S // 2)
        XH = XTF[:, 0:4096].bitcast(F16).rearrange("p (k t) -> p k t", k=KT)
        XL = XTF[:, 4096:8192].bitcast(F16).rearrange("p (k t) -> p k t", k=KT)
        stage = sb("stage", SLOTS * UK * UC)
        split = sb("split", SLOTS * 2 * UK * UC, F16)
        AR = sb("arena", 12288)
        xn = sb("xn", 2 * D)[:, :].rearrange("p (b d) -> p b d", b=2)
        junk = sb("junk", D)
        gb = sb("gb", D)
        misc = sb("misc", MISC_COLS)
        halfw = sb("half", 7 * P // 2)
        Z = sb("zone", 2304)
        cols = sb("cols", 512)

        ident = misc[:, M_ID:M_ID + P]
        eps = misc[:, M_EPS:M_EPS + 1]
        half = halfw[:, :].bitcast(BF16)
        identb = half[:, 0:P]
        corr = half[:, P:P + NH * P].rearrange("p (h k) -> p h k", h=NH)
        tri = half[:, 5 * P:6 * P]
        onesb = half[:, 6 * P:7 * P]
        ret = Z[:, 0:RET_COLS]
        decT = ret[:, 0:512].rearrange("p (b c) -> p b c", b=2)
        kdec = ret[:, 512:768]
        qdec = ret[:, 768:1280].rearrange("p (t j c) -> p t j c", t=2, j=2)
        cdec = ret[:, 1280:1536]
        pos = Z[0:2, RET_COLS:RET_COLS + (S + NH * P) // 2].bitcast(F16)
        pos_k = pos[:, 0:S]
        pos_q = pos[:, S:S + NH * P].rearrange("p (h q) -> p h q", h=NH)

        ss = cols[:, 0:8]
        std = cols[:, 8:16]
        rstd = cols[:, 16:24]
        ss4, std4, rst4 = cols[:, 24:28], cols[:, 28:32], cols[:, 32:36]
        lsum, lexp, neglam = cols[:, 36:38], cols[:, 38:40], cols[:, 40:41]
        c1 = cols[:, 41:42]
        negmax, rows_sum, rows_rec = cols[:, 64:128], cols[:, 128:192], cols[:, 192:256]
        ssA, stdA, rstA = cols[:, 256:288], cols[:, 288:320], cols[:, 320:352]
        subg = cols[:, 384:512]
        wk = cols[:, 64:80].rearrange("p (k t) -> p k t", k=2)
        slot = cols[:, 80:96].bitcast(I32).rearrange("p (k t) -> p k t", k=2)
        tok_of = cols[:, 96:96 + BLK_MAX + 1].bitcast(I32)
        idx = [cols[:, 144 + i:145 + i].bitcast(I32) for i in range(2)]
        over_e = cols[0:1, 146:146 + NOVER + 1].bitcast(I32)
        n_over = cols[0:1, 162:163].bitcast(I32)

        rw = Z[:, 0:288]
        rwh = Z[:, 288:432].bitcast(F16)
        rwl = Z[:, 432:576].bitcast(F16)
        rb = Z[:, 576:612]
        gm = Z[:, 1280:2304]
        WORK = AR[:, 8192:12288]
        y = [AR[:, 8192 + 1024 * i:9216 + 1024 * i] for i in range(2)]
        hbuf = AR[:, 10240:10752]
        tbuf = AR[:, 10752:11264]
        sig = AR[:, 11264:11776]
        hTh = AR[:, 11776:12032].bitcast(F16).rearrange("p (k t) -> p k t", k=4)
        hTl = AR[:, 12032:12288].bitcast(F16).rearrange("p (k t) -> p k t", k=4)
        XG = [XTF[:, 1024 * i:1024 * i + 1024] for i in range(2)]
        xeh = [XTF[:, 2048 + 1024 * i:2560 + 1024 * i].bitcast(F16).rearrange("p (k t) -> p k t", k=KT)
               for i in range(2)]
        xel = [XTF[:, 2560 + 1024 * i:3072 + 1024 * i].bitcast(F16).rearrange("p (k t) -> p k t", k=KT)
               for i in range(2)]
        YG = [[AR[:, 2048 * i + 1024 * k:2048 * i + 1024 * k + 1024] for k in range(2)] for i in range(4)]
        XO, XOT = XTF[:, 4096:5120], XTF[:, 5120:6144]
        hO, hOT, sO = XTF[:, 6144:6656], XTF[:, 6656:7168], XTF[:, 7168:7680]
        wO = AR[:, 0:2048]
        cconv = Z[:, 0:288]
        cw = cconv[:, 0:248].rearrange("p (k j) -> p k j", k=KT)
        cb, lng, lnb, b_in = cconv[:, 248:256], cconv[:, 256:264], cconv[:, 264:272], cconv[:, 272:288]
        U = AR[:, 0:KT * (PAD + S)].rearrange("p (k t) -> p k t", k=KT)
        prod = [AR[:, 8448 + 512 * i:8960 + 512 * i] for i in range(4)]
        silu = [AR[:, 10496 + 512 * i:11008 + 512 * i] for i in range(3)]
        av = [junk[:, 512 * i:512 * i + 512] for i in range(2)]
        sv = [xn[:, 0, 512 * i:512 * i + 512] for i in range(2)]
        mean, rdev, var = xn[:, 0, :], xn[:, 1, :], junk[:, :]
        bo = gm
        HTh = AR[:, 0:2048].bitcast(F16).rearrange("p (k t) -> p k t", k=4)
        HTl = AR[:, 2048:4096].bitcast(F16).rearrange("p (k t) -> p k t", k=4)
        relu = [AR[:, 4096 + 512 * i:4608 + 512 * i] for i in range(2)]
        relu2 = [AR[:, 5120 + 512 * i:5632 + 512 * i] for i in range(2)]
        xn_rows = nc.dram_tensor("xn_rows", (S, D), F32, kind="Internal").ap()
        y_rows = nc.dram_tensor("y_rows", ((BLK_MAX + 1) * P, D), F32, kind="Internal").ap()
        x2_rows = nc.dram_tensor("x2_rows", (TT, P, D), F32, kind="Internal").ap()

        PS = ctx.enter_context(nc.psum_tensor("ps", [P, 4, 512], F32))
        PT = ctx.enter_context(nc.psum_tensor("pt", [P, 4, 512], F32))

        def tpair(par):
            return PT[:, 2 * par:2 * par + 2, :].rearrange("p b (k c) -> p (b k) c", k=4)

        def wstage(s):
            return stage[:, s * 2048:(s + 1) * 2048] if s < SLOTS else AR[:, (s - 4) * 2048:(s - 3) * 2048]

        def whi(s):
            if s < SLOTS:
                return split[:, s * 4096:s * 4096 + 2048]
            return AR[:, 4096 + (s - 4) * 2048:4096 + (s - 4) * 2048 + 1024].bitcast(F16)

        def wlo(s):
            if s < SLOTS:
                return split[:, s * 4096 + 2048:(s + 1) * 4096]
            return AR[:, 4096 + (s - 4) * 2048 + 1024:4096 + (s - 3) * 2048].bitcast(F16)

        QR = AR[:, 0:2048].rearrange("p (t s) -> p t s", t=2)
        KR = AR[:, 2048:4096].rearrange("p (t s) -> p t s", t=2)
        VR = AR[:, 4096:8192].rearrange("p (t v) -> p t v", t=TT)
        SG = AR[:, 8192:12288].rearrange("p (t v) -> p t v", t=TT)
        Qh, Ql, Kh, Kl = [AR[:, 2048 * i:2048 * i + 2048].bitcast(F16).rearrange("p (h s) -> p h s", h=NH)
                          for i in range(4)]
        V = AR[:, 8192:12288].rearrange("p (t v) -> p t v", t=TT)

        s_const = sem("const_loaded")
        s_misc = sem("tables_loaded")
        s_gain = sem("gain_loaded")
        s_x = [sem(f"x_loaded{i}") for i in range(TT)]
        s_wl = [sem(f"w_landed{i}") for i in range(6)]
        s_wh = [sem(f"w_hi{i}") for i in range(6)]
        s_wo = [sem(f"w_lo{i}") for i in range(6)]
        s_full = [sem(f"bank_full{i}") for i in range(4)]
        s_free = [sem(f"bank_free{i}") for i in range(4)]
        s_std = sem("norm_std")
        s_xn = sem("norm_xn")
        s_tr = sem("norm_transposed")
        s_xh = sem("xt_hi")
        s_xl = sem("xt_lo")
        s_dve = sem("dve_step")
        s_act = sem("act_step")
        s_sig = sem("gate_sigmoid")
        s_rsc = sem("ret_scores")
        s_rm = sem("ret_masked")
        s_rst = sem("ret_state")
        s_ro = sem("ret_out")
        s_rss = sem("ret_std")
        s_rmix = sem("ret_mix")
        s_lam = sem("lambda")
        s_lx = sem("lambda_exp")
        s_qk = sem("query_key_hi")
        s_as = sem("att_scores")
        s_amx = sem("att_max")
        s_ae = sem("att_exp")
        s_aa = sem("att_mixed")
        s_at = sem("att_transposed")
        s_aea = sem("att_t_act")
        s_aed = sem("att_t_dve")
        s_ao = sem("att_out")
        s_aoe = sem("att_out_read")
        s_router_w = sem("router_loaded")
        s_rws = sem("router_split")
        s_xs = [sem(f"xn_stored{i}") for i in range(2)]
        s_lg = sem("logits")
        s_rt = sem("router_ready")
        s_rp = sem("router_products")
        s_rx = sem("router_exp")
        s_rd = sem("router_diff")
        s_slots = sem("slots_known")
        s_gx = [sem(f"x_gathered{i}") for i in range(2)]
        s_zero = sem("zero_tile")
        s_cleared = sem("overflow_rows_cleared")
        s_sc = sem("unit_scaled")
        s_seen = sem("wait_seen")
        s_ix = sem("index_column")
        s_xt = sem("x_transposed")
        s_xeh = sem("x_hi")
        s_xel = sem("x_lo")
        s_g = sem("gate_done")
        s_u = sem("up_done")
        s_es = sem("expert_sigmoid")
        s_t = sem("gate_silu")
        s_h = sem("hidden")
        s_ht = sem("hidden_transposed")
        s_hh = sem("hidden_hi")
        s_hl = sem("hidden_lo")
        s_d = [sem(f"down_done{i}") for i in range(2)]
        s_y = [sem(f"y_half{i}") for i in range(2)]
        s_ys = [sem(f"y_stored{i}") for i in range(2)]
        s_yg = [sem(f"y_gathered{i}") for i in range(4)]
        s_cmb = sem("combined")
        s_x2 = sem("second_input")
        s_x2s = sem("second_input_stored")
        s_ox = sem("over_rows_gathered")
        s_oix = sem("over_index_column")
        s_ow = sem("over_unit_landed")
        s_ou = sem("over_unit_used")
        s_ot = sem("over_transposed")
        s_oc = sem("over_copied")
        s_os = sem("over_sigmoid")
        s_og = sem("over_silu")
        s_oh = sem("over_hidden")
        s_oy = sem("over_output")
        s_oys = sem("over_stored")
        s_tab = sem("conv_tables_loaded")
        s_pad = sem("conv_pad")
        s_cu = sem("conv_input")
        s_pr = sem("conv_product")
        s_ca = sem("conv_added")
        s_cd = sem("conv_dve")
        s_c0 = sem("conv_first_tap")
        s_sq = sem("conv_squares")
        s_st = sem("conv_stats")
        s_va = sem("conv_var")
        s_rd2 = sem("conv_dev")
        s_z = sem("conv_normed")
        s_zp = sem("conv_normed_gpsimd")
        s_zq = sem("conv_centred_gpsimd")
        s_rv = sem("conv_rdev")
        s_si = sem("conv_silu")
        s_ch = sem("conv_hi")
        s_cl = sem("conv_lo")
        s_bo = sem("bias_loaded")
        s_relu = sem("mlp_relu")
        s_mh = sem("mlp_hi")
        s_ml = sem("mlp_lo")
        s_out = sem("out_stored")

        block = ctx.enter_context(nc.Block())

        def load_unit(eng, n):
            s, r = n % SLOTS, n // SLOTS
            if r:
                eng.wait_ge(s_wh[s], r)
                eng.wait_ge(s_wo[s], r)
            eng.dma_start(wstage(s), a["w_dense_a"][n]).then_inc(s_wl[s], 16)

        def split_hi(act, n):
            s, r = n % SLOTS, n // SLOTS
            act.wait_ge(s_wl[s], 16 * (r + 1))
            if r:
                g = last_group(n - SLOTS)
                act.wait_ge(s_full[g % 4], g // 4 + 1)
            nc.scalar.activation(whi(s), wstage(s), ACT.Copy, scale=WS).then_inc(s_wh[s], 1)

        def split_lo(dve, n):
            s, r = n % SLOTS, n // SLOTS
            dve.wait_ge(s_wh[s], r + 1)
            nc.vector.scalar_tensor_tensor(out=wlo(s), in0=wstage(s), scalar=WS, in1=whi(s),
                                           op0=ALU.mult, op1=ALU.subtract).then_inc(s_wo[s], 1)

        def product(pe, out_ap, lh, ll, rh, rl, start, stop):
            nc.tensor.matmul(out_ap, lh, rh, start=start, stop=False)
            nc.tensor.matmul(out_ap, lh, rl, start=False, stop=False)
            return nc.tensor.matmul(out_ap, ll, rh, start=False, stop=stop)

        def last_group(n):
            return 8 * (n // 2) + 7 if n < 12 else 62 + (n - 12) // 2

        def group(pe, g, units, feature_major, ft, tk):
            if g >= 4:
                pe.wait_ge(s_free[g % 4], g // 4)
            for ui, n in enumerate(units):
                s, r = n % SLOTS, n // SLOTS
                pe.wait_ge(s_wo[s], r + 1)
                for kk in range(UK):
                    k = ui * UK + kk
                    if feature_major:
                        c = slice(kk * UC + ft * P, kk * UC + ft * P + P)
                        t = slice(tk * 512, tk * 512 + 512)
                        i = product(pe, PS[:, g % 4, :], whi(s)[:, c], wlo(s)[:, c], XH[:, k, t], XL[:, k, t],
                                    k == 0, k == KT - 1)
                    else:
                        c = slice(kk * UC, kk * UC + UC)
                        t = slice(tk * P, tk * P + P)
                        i = product(pe, PS[:, g % 4, :], XH[:, k, t], XL[:, k, t], whi(s)[:, c], wlo(s)[:, c],
                                    k == 0, k == KT - 1)
            i.then_inc(s_full[g % 4], 1)
            return i

        def norm_stats(act, ch, t):
            ch.done(nc.scalar.activation(junk[:, :], H[:, t, :], ACT.Square, accum_out=ss[:, t:t + 1]))
            nc.scalar.activation(std[:, t:t + 1], ss[:, t:t + 1], ACT.Sqrt, bias=eps, scale=1.0 / D)\
                .then_inc(s_std, 1)

        def xn_wait(dve, r, t):
            n = TT * r + t
            if n >= 2:
                dve.wait_ge(s_tr, n - 1)

        def norm_scale(dve, ch, r, t, nstd):
            dve.wait_ge(s_std, nstd)
            ch.done(nc.vector.reciprocal(rstd[:, t:t + 1], std[:, t:t + 1]))
            xn_wait(dve, r, t)
            nc.vector.scalar_tensor_tensor(out=xn[:, t % 2, :], in0=H[:, t, :], scalar=rstd[:, t:t + 1],
                                           in1=gb[:, :], op0=ALU.mult, op1=ALU.mult).then_inc(s_xn, 1)

        def transposes(pe, r, t, src):
            n = TT * r + t
            pe.wait_ge(s_xn, n + 1)
            if n >= 2:
                pe.wait_ge(s_xl, n - 1)
            for k in range(KT):
                i = nc.tensor.transpose(tpair(t % 2)[:, k, :], src(t, k), ident)
            i.then_inc(s_tr, 1)

        def xt_hi(act, r, t):
            act.wait_ge(s_tr, TT * r + t + 1)
            nc.scalar.activation(XH[:, :, t * P:(t + 1) * P], tpair(t % 2), ACT.Copy).then_inc(s_xh, 1)

        def xt_lo(dve, r, t):
            dve.wait_ge(s_xh, TT * r + t + 1)
            nc.vector.tensor_tensor(XL[:, :, t * P:(t + 1) * P], tpair(t % 2), XH[:, :, t * P:(t + 1) * P],
                                    ALU.subtract).then_inc(s_xl, 1)

        FM = [True, False, False, True, True, False]

        def chunk_groups(c):
            if c == 0:
                return [(4 * th + ft, ft, th) for th in range(2) for ft in range(4)]
            if FM[c]:
                return [(8 * c + 2 * ft + th, ft, th) for ft in range(4) for th in range(2)]
            return [(8 * c + t, 0, t) for t in range(TT)]

        def chunk_dest(c, ft, tk):
            tok = slice(tk * 512, tk * 512 + 512)
            return [lambda: (QR if ft < 2 else KR)[:, ft % 2, tok], lambda: VR[:, tk, :], lambda: SG[:, tk, :],
                    lambda: (Qh[:, ft, tok], Ql[:, ft, tok]), lambda: (Kh[:, ft, tok], Kl[:, ft, tok]), lambda: V[:, tk, :]][c]()

        CHUNK_SCALE = [IWS, IWS, IWS, IWS * DH ** -0.5, IWS, IWS]
        BLOCKS = [(h, i) for h in range(NH) for i in range(TT)]
        NB = len(BLOCKS)

        def aT(par):
            return XTF[:, 4096 + par * 1024:4096 + (par + 1) * 1024].rearrange("p (k q) -> p k q", k=KT)

        def PB(par, m):
            return XTF[:, (2 * par + m) * 1024:(2 * par + m + 1) * 1024]

        def SC(m):
            return PS[:, 2 * m:2 * m + 2, :].rearrange("p b c -> p (b c)")

        sT = [xn[:, 0, 0:512], xn[:, 0, 512:1024]]
        qd = [xn[:, 1, 0:512], xn[:, 1, 512:1024]]
        ktok = [junk[:, 256:512], junk[:, 512:768]]
        state = junk[:, 0:256]
        lam_in = AR[:, 10240:10496]
        lam_dot = AR[:, 10496:10624].rearrange("p (j d) -> p j d", j=2)

        BASE = [4, 4, 4, 4, 0, 0]

        def expert_load(sp, kind, e):
            s0 = {"up": 0, "gate": 2, "down": 4}[kind]
            for i in range(2):
                s = s0 + i
                if not (isinstance(e, int) and BASE[s] + e == 0):
                    sp.wait_ge(s_wh[s], BASE[s] + e)
                    sp.wait_ge(s_wo[s], BASE[s] + e)
                src = a["w_" + kind][bass.ds(2 * e + i, 1), :, :].rearrange("o p c -> (o p) c")
                sp.dma_start(wstage(s), src).then_inc(s_wl[s], 16)

        def expert_hi(act, s, e):
            act.wait_ge(s_wl[s], 16 * (BASE[s] + 1) + 16 * e)
            if not (isinstance(e, int) and e == 0):
                act.wait_ge([s_u, s_u, s_g, s_g, s_d[0], s_d[1]][s], e)
            nc.scalar.activation(whi(s), wstage(s), ACT.Copy, scale=WS).then_inc(s_wh[s], 1)

        def expert_lo(dve, s, e):
            dve.wait_ge(s_wh[s], BASE[s] + 1 + e)
            nc.vector.scalar_tensor_tensor(out=wlo(s), in0=wstage(s), scalar=WS, in1=whi(s),
                                           op0=ALU.mult, op1=ALU.subtract).then_inc(s_wo[s], 1)

        def expert_lo_pool(pool, e):
            s = 5
            pool.wait_ge(s_wh[s], BASE[s] + 1 + e)
            pool.sem_inc(s_seen, 1)
            nc.gpsimd.tensor_scalar(wstage(s), wstage(s), WS, None, ALU.mult).then_inc(s_sc, 1)
            pool.wait_ge(s_sc, e + 2)
            nc.gpsimd.tensor_tensor(wlo(s), wstage(s), whi(s), ALU.subtract).then_inc(s_wo[s], 1)

        def expert_product(pe, bank, s0, e, lh, ll, done, between=None):
            for i in range(2):
                s = s0 + i
                if i and between:
                    between()
                pe.wait_ge(s_wo[s], BASE[s] + 1 + e)
                for kk in range(UK):
                    k, c = i * UK + kk, slice(kk * UC, kk * UC + UC)
                    m = product(pe, bank, lh[:, k, :], ll[:, k, :], whi(s)[:, c], wlo(s)[:, c], k == 0, k == KT - 1)
            m.then_inc(done, 1)

        def overflow(eng, body):
            eng.wait_ge(s_slots, 1)
            n = eng.value_load(n_over, min_val=0, max_val=NOVER)
            with eng.If(n > 0):
                with eng.Fori(0, NOVER) as j:
                    with eng.If(j < n):
                        body(j)

        RB = BASE[0] + NE

        def load_b(sp, m):
            s, r = m % SLOTS, RB + m // SLOTS
            sp.wait_ge(s_wh[s], r)
            sp.wait_ge(s_wo[s], r)
            sp.dma_start(wstage(s), a["w_dense_b"][m]).then_inc(s_wl[s], 16)

        def last_group_b(m):
            return 77 + 16 * (m // 4) + m % 4 // 2 * 2 if m < 8 else 110 + (m - 8) // 2

        def hi_b(act, m):
            s, r = m % SLOTS, RB + m // SLOTS
            act.wait_ge(s_wl[s], 16 * (r + 1))
            if m >= SLOTS:
                g = last_group_b(m - SLOTS)
                act.wait_ge(s_full[g % 4], g // 4 + 1)
            nc.scalar.activation(whi(s), wstage(s), ACT.Copy, scale=WS).then_inc(s_wh[s], 1)

        def lo_b(dve, m):
            s, r = m % SLOTS, RB + m // SLOTS
            dve.wait_ge(s_wh[s], r + 1)
            nc.vector.scalar_tensor_tensor(out=wlo(s), in0=wstage(s), scalar=WS, in1=whi(s),
                                           op0=ALU.mult, op1=ALU.subtract).then_inc(s_wo[s], 1)

        def group_b(pe, g, units, feature_major, ft, tk, before=None):
            pe.wait_ge(s_free[g % 4], g // 4)
            for ui, m in enumerate(units):
                s, r = m % SLOTS, RB + m // SLOTS
                pe.wait_ge(s_wo[s], r + 1)
                for kk in range(UK):
                    k = ui * UK + kk
                    if before:
                        before(k)
                    if feature_major:
                        c = slice(kk * UC + ft * P, kk * UC + ft * P + P)
                        t = slice(tk * 512, tk * 512 + 512)
                        i = product(pe, PS[:, g % 4, :], whi(s)[:, c], wlo(s)[:, c], XH[:, k, t], XL[:, k, t],
                                    k == 0, k == KT - 1)
                    else:
                        c = slice(kk * UC, kk * UC + UC)
                        t = slice(tk * P, tk * P + P)
                        i = product(pe, PS[:, g % 4, :], XH[:, k, t], XL[:, k, t], whi(s)[:, c], wlo(s)[:, c],
                                    k == 0, k == KT - 1)
            i.then_inc(s_full[g % 4], 1)

        RM = RB + 3
        G_MLP = 112 // 4
        NC = DFF // UC
        CONV_DVE = [(k, 0) for k in (0, 2, 3, 5, 6, 7)] + [(k, 1) for k in (0, 2, 3, 5)]
        CONV_ACT = [(1, 0), (1, 1), (4, 0), (4, 1), (7, 1), (6, 1)]
        GATED = [(k, th) for hf in range(2) for th in range(2) for k in range(4 * hf, 4 * hf + 4)]

        def gate_groups(p):
            if p not in (6, 7, 14, 15):
                return 64 + 2 * p, 65 + 2 * p
            return 64 + 2 * (p - p % 2) + p % 2, 66 + 2 * (p - p % 2) + p % 2

        def input_done(k, th):
            return GATED.index((k, th)) + 1

        def conv_in_group(g):
            for p, (k, th) in enumerate(GATED):
                if g in gate_groups(p):
                    return gate_groups(p).index(g), k, th

        def mlp_hi(act, s, c):
            act.wait_ge(s_wl[s], 16 * (RM + 1) + 16 * c)
            if isinstance(c, int) and c == 0:
                g = 110 + s // 2
                act.wait_ge(s_full[g % 4], g // 4 + 1)
            nc.scalar.activation(whi(s), wstage(s), ACT.Copy, scale=WS).then_inc(s_wh[s], 1)

        def mlp_lo(dve, s, c):
            dve.wait_ge(s_wh[s], RM + 1 + c)
            nc.vector.scalar_tensor_tensor(out=wlo(s), in0=wstage(s), scalar=WS, in1=whi(s),
                                           op0=ALU.mult, op1=ALU.subtract).then_inc(s_wo[s], 1)

        def mlp_chunks(eng, body):
            with eng.Fori(0, NC - 1) as c:
                body(c, False)
            body(NC - 1, True)

        def conv_wait(eng, x):
            if x in CONV_ACT:
                eng.wait_ge(s_ca, (TAPS - 1) * (CONV_ACT.index(x) + 1))
            else:
                eng.wait_ge(s_cd, CONV_ENDS.index(x) + 1)

        def HC(k, th):
            return H[:, 4 * th + k // 2, k % 2 * 512:k % 2 * 512 + 512]

        SUM_ORDER = [[0, 1, 2, 3, 4, 5, 6, 7], [0, 1, 2, 3, 4, 5, 7, 6]]
        SUM_PRODUCTS = [2, 3, 3, 3, 3, 3, 3, 3]
        squared = [gb[:, 512 * i:512 * i + 512] for i in range(2)]
        LN_POOL = [(), (2, 5, 7)]

        def ln_wait(eng, k, th):
            if k in LN_POOL[th]:
                eng.wait_ge(s_zp, LN_POOL[th].index(k) + 1)
            else:
                eng.wait_ge(s_z, KT * th + k + 1 - sum(x < k for x in LN_POOL[th]))

        def tap_schedule():
            left, opened, plan = list(CONV_DVE), [[], []], []
            turn = 0
            for p in list(range(len(GATED))) + [None]:
                now = len(GATED) if p is None else p + 1
                room = 10 ** 6 if p is None else TAP_ROOM.get(p, 14)
                taps_ = []
                while len(taps_) < room:
                    for x in [x for x in left if input_done(*x) <= now]:
                        if len(opened[x[1]]) < 3 - x[1]:
                            left.remove(x)
                            opened[x[1]].append((x[0], 0))
                    turn += 1
                    th = 0 if len(opened[0]) >= 2 else 1 if not opened[0] else turn % 2
                    if not opened[th]:
                        th = 1 - th
                    if not opened[th]:
                        break
                    k, j = opened[th].pop(0)
                    taps_.append((k, th, j))
                    if j + 1 < TAPS:
                        opened[th].append((k, j + 1))
                plan.append(taps_)
            return plan

        TAP_ROOM = {5: 12, 13: 12, 6: 5, 14: 5, 7: 10, 15: 3}
        LN_AFTER = 4
        seq = lambda text: [(w[0], int(w[1])) for w in (x.split(":") for x in text.split())]
        MLP_NORM_PE = seq("out:4 tr:0 tr:1 out:5 tr:2 tr:3 out:6 tr:4 out:7 tr:5 tr:6 tr:7")
        MLP_NORM_ACT = seq("stats:0 stats:1 stats:2 stats:3 hi:0 hi:1 stats:4 hi:2 hi:3 stats:5 hi:4 stats:6 hi:5 "
                           "unit:0 stats:7 unit:1 hi:6 hi:7 unit:2 unit:3")
        MLP_NORM_DVE = seq("norm:0 norm:1 out:4 lo:0 norm:2 lo:1 norm:3 out:5 lo:2 norm:4 lo:3 norm:5 out:6 lo:4 "
                           "norm:6 out:7 lo:5 unit:0 norm:7 unit:1 lo:6 lo:7 unit:2 unit:3")
        TAP_PLAN = tap_schedule()
        CONV_ENDS = [(k, th) for part in TAP_PLAN for k, th, j in part if j == TAPS - 1]

        def pairs(body, eng):
            for q in range(2):
                body(q, q, True, False)
            with eng.Fori(1, NE // 2 - 1) as k:
                for q in range(2):
                    body(2 * k + q, q, False, False)
            for q in range(2):
                body(NE - 2 + q, q, False, True)

        def first_dev(u):
            return max(1, 2 * u)

        def second_dev(u):
            return 2 * u + 3 if u < TT - 1 else 2 * TT

        off = [0]

        def work(n, *shape):
            v = WORK[:, off[0]:off[0] + n]
            off[0] += n
            if len(shape) == 2:
                return v.rearrange("p (a b) -> p a b", a=shape[0])
            if len(shape) == 3:
                return v.rearrange("p (a b c) -> p a b c", a=shape[0], b=shape[1])
            return v

        BIG = 1e38
        rL = work(TT * 36, TT, 36)
        rG, rE = rL[:, :, 0:NG], rL[:, :, NG:NG + NE]
        rgm, rgx = work(TT), work(TT)
        rgo = work(TT * NG, TT, NG)
        rex = work(TT * NG, TT, NG)
        rEm = work(TT * NE, TT, NE)
        rtmp = work(TT * NE, TT, NE)
        roh = [work(TT * NE, TT, NE) for _ in range(2)]
        rm = [work(TT), work(TT)]
        rix = work(2 * TT, 2, TT)
        rde, rgs = work(TT), work(TT)
        rM = work(TT * NE // 2).bitcast(BF16).rearrange("p (t e) -> p t e", t=TT)
        rex_t = work(1)
        rcmp = work(NE)
        rexb = work(P // 2).bitcast(BF16)
        rthr = work(8)
        rrank, rbq, rst_ = work(2 * TT, 2, TT), work(2 * TT, 2, TT), work(2 * TT, 2, TT)
        rblk, rpos, rv = work(2 * TT, 2, TT), work(2 * TT, 2, TT), work(2 * TT, 2, TT)
        rc7 = work(2 * TT * 7, 2 * TT, 7)
        rinc = work(NE)
        rov = work((NOVER + 1) * NE, NOVER + 1, NE)
        rbe = work(NOVER + 1)
        off[0] = 2700
        rA = work(2 * TT * P // 2).bitcast(F16).rearrange("p (n c) -> p n c", n=2 * TT)
        rB = junk[:, 0:TT * (BLK_MAX + 1)].bitcast(F16).rearrange("p (n c) -> p n c", n=2 * TT)

        def bc(ap, n):
            return ap.unsqueeze(2).to_broadcast([P, ap.shape[1], n])

        def router(dve, ch):
            V_ = nc.vector
            io, iob = misc[:, M_IO:M_IO + P], misc[:, M_IOB:M_IOB + BLK_MAX + 1]
            rev = misc[:, M_REV:M_REV + NE]
            tok = misc[:, M_TOK:M_TOK + TT]
            dve.wait_ge(s_lg, 1)
            ch.done(V_.scalar_tensor_tensor(
                out=rL, in0=PS[:, 0, 0:TT * 36].rearrange("p (t c) -> p t c", t=TT), scalar=IWS,
                in1=rb.unsqueeze(1).to_broadcast([P, TT, 36]), op0=ALU.mult, op1=ALU.add))
            ch.done(V_.tensor_reduce(rgm, rG, AX.X, ALU.max))
            ch.done(V_.tensor_tensor(rex, rG, bc(rgm, NG), ALU.subtract))
            V_.tensor_scalar(rgo, rex, 0.0, None, ALU.is_ge).then_inc(s_rd, 1)
            dve.wait_ge(s_rd, 1)
            ch.done(V_.tensor_tensor(rgo, rgo, rev[:, NE - NG:NE].unsqueeze(1).to_broadcast([P, TT, NG]), ALU.mult))
            ch.done(V_.tensor_reduce(rgx, rgo, AX.X, ALU.max))
            ch.done(V_.tensor_tensor(rgo, rgo, bc(rgx, NG), ALU.is_equal))
            rE4 = [rE[:, :, g * EG:(g + 1) * EG] for g in range(NG)]
            for g in range(NG):
                V_.tensor_tensor(rEm[:, :, g * EG:(g + 1) * EG], rE4[g], bc(rgo[:, :, g], EG), ALU.mult)
            ch.done(V_.tensor_scalar(rtmp[:, :, 0:NG], rgo, BIG, -BIG, ALU.mult, ALU.add))
            for g in range(NG):
                part = rEm[:, :, g * EG:(g + 1) * EG]
                i = V_.tensor_tensor(part, part, bc(rtmp[:, :, g], EG), ALU.add)
            ch.done(i)
            for k in range(2):
                if k:
                    ch.done(V_.scalar_tensor_tensor(out=rEm, in0=roh[0], scalar=-BIG, in1=rEm,
                                                    op0=ALU.mult, op1=ALU.add))
                ch.done(V_.tensor_reduce(rm[k], rEm, AX.X, ALU.max))
                ch.done(V_.tensor_tensor(roh[k], rEm, bc(rm[k], NE), ALU.is_ge))
                ch.done(V_.tensor_tensor(roh[k], roh[k], rev.unsqueeze(1).to_broadcast([P, TT, NE]), ALU.mult))
                ch.done(V_.tensor_reduce(rix[:, k, :], roh[k], AX.X, ALU.max))
                ch.done(V_.tensor_tensor(roh[k], roh[k], bc(rix[:, k, :], NE), ALU.is_equal))
            V_.tensor_tensor(rde, rm[1], rm[0], ALU.subtract).then_inc(s_rd, 1)
            ch.done(V_.tensor_scalar(rix, rix, -1.0, float(NE), ALU.mult, ALU.add))
            V_.tensor_tensor(rM, roh[0], roh[1], ALU.add).then_inc(s_rt, 1)
            dve.wait_ge(s_rx, 2)
            ch.done(V_.tensor_reduce(rgs, rex, AX.X, ALU.add))
            ch.done(V_.tensor_scalar(rm[0], rde, 1.0, None, ALU.add))
            ch.done(V_.tensor_tensor(rgs, rgs, rm[0], ALU.mult))
            ch.done(V_.reciprocal(wk[:, 0, :], rgs))
            ch.done(V_.tensor_tensor(wk[:, 1, :], wk[:, 0, :], rde, ALU.mult))
            dve.wait_ge(s_rp, 1)
            ch.done(V_.tensor_copy(rex_t[0:NE, :], PS[0:NE, 2, 0:1]))
            ch.done(V_.tensor_scalar(rcmp[0:NE, 0:7], io[0:NE, 1:8], float(P), rex_t[0:NE, :], ALU.mult, ALU.is_lt))
            ch.done(V_.tensor_reduce(rex_t[0:NE, :], rcmp[0:NE, 0:7], AX.X, ALU.add))
            V_.tensor_scalar(rexb[0:NE, :], misc[0:NE, M_ONE:M_ONE + P], rex_t[0:NE, :], None, ALU.mult)\
                .then_inc(s_rt, 1)
            for k in range(2):
                ch.done(V_.tensor_tensor(rtmp, PS[:, 1, 0:TT * NE].rearrange("p (t e) -> p t e", t=TT), roh[k],
                                         ALU.mult))
                ch.done(V_.tensor_reduce(rrank[:, k, :], rtmp, AX.X, ALU.add))
            ch.done(V_.tensor_scalar(rthr[:, 0:7], io[:, 1:8], float(P), None, ALU.mult))
            rank = rrank.rearrange("p k t -> p (k t)")
            ch.done(V_.tensor_tensor(rc7, bc(rank, 7), rthr[:, 0:7].unsqueeze(1).to_broadcast([P, 2 * TT, 7]),
                                     ALU.is_ge))
            ch.done(V_.tensor_reduce(rbq.rearrange("p k t -> p (k t)"), rc7, AX.X, ALU.add))
            ch.done(V_.scalar_tensor_tensor(out=rpos, in0=rbq, scalar=-float(P), in1=rrank,
                                            op0=ALU.mult, op1=ALU.add))
            dve.wait_ge(s_rp, 2)
            for k in range(2):
                ch.done(V_.tensor_tensor(rtmp, PS[:, 3, 0:NE].unsqueeze(1).to_broadcast([P, TT, NE]), roh[k],
                                         ALU.mult))
                ch.done(V_.tensor_reduce(rst_[:, k, :], rtmp, AX.X, ALU.add))
            ch.done(V_.tensor_copy(rinc, PS[:, 3, NE:2 * NE]))
            ch.done(V_.tensor_tensor(rv, rst_, rbq, ALU.add))
            ch.done(V_.tensor_tensor(rv, rv, rix, ALU.subtract))
            ch.done(V_.tensor_scalar(rblk, rbq, 0.0, None, ALU.is_gt))
            ch.done(V_.scalar_tensor_tensor(out=rv, in0=rv, scalar=float(NE - 1), in1=rblk,
                                            op0=ALU.add, op1=ALU.mult))
            ch.done(V_.tensor_tensor(rblk, rv, rix, ALU.add))
            V_.scalar_tensor_tensor(out=slot, in0=rblk, scalar=float(P), in1=rpos, op0=ALU.mult, op1=ALU.add)
            V_.tensor_tensor(rA, io.unsqueeze(1).to_broadcast([P, 2 * TT, P]),
                             bc(rpos.rearrange("p k t -> p (k t)"), P), ALU.is_equal)
            ch.done(V_.tensor_tensor(rB, iob.unsqueeze(1).to_broadcast([P, 2 * TT, BLK_MAX + 1]),
                                     bc(rblk.rearrange("p k t -> p (k t)"), BLK_MAX + 1), ALU.is_equal))
            for k in range(2):
                i = V_.tensor_tensor(rB[:, k * TT:(k + 1) * TT, :], rB[:, k * TT:(k + 1) * TT, :],
                                     bc(tok, BLK_MAX + 1), ALU.mult)
            i.then_inc(s_rt, 1)
            ch.done(V_.tensor_tensor(rov[0:1], rinc[0:1, :].unsqueeze(1).to_broadcast([1, NOVER + 1, NE]),
                                     iob[0:1, 0:NOVER + 1].unsqueeze(2).to_broadcast([1, NOVER + 1, NE]),
                                     ALU.is_le))
            ch.done(V_.tensor_reduce(rbe[0:1, :], rov[0:1], AX.X, ALU.add))
            V_.tensor_scalar(over_e, rbe[0:1, :], float(NE - 1), None, ALU.min)
            V_.tensor_copy(n_over, rinc[0:1, NE - 1:NE])
            dve.wait_ge(s_rp, 3)
            V_.tensor_copy(tok_of, PS[:, 0, 0:BLK_MAX + 1]).then_inc(s_slots, 1)

        @block.sync
        def _(sp):
            for t in range(TT):
                sp.dma_start(H[:, t, :], a["x"][t]).then_inc(s_x[t], 16)
                if t == 0:
                    sp.dma_start(gb[:, :], a["gains"][0:1, :].to_broadcast([P, D])).then_inc(s_gain, 16)
                    sp.dma_start(misc[:, :], a["c_misc"]).then_inc(s_misc, 16)
                if t in (1, 3):
                    load_unit(sp, t // 2)
            for n in range(2, 4):
                load_unit(sp, n)
            sp.dma_start(halfw[:, :], a["c_half"]).then_inc(s_const, 16)
            sp.dma_start(ret, a["c_ret"]).then_inc(s_const, 16)
            sp.dma_start(pos, a["c_pos"]).then_inc(s_const, 16)
            sp.dma_start(subg, a["subln_g"].to_broadcast([P, DV])).then_inc(s_const, 16)
            for j in range(4):
                sp.dma_start(lam_in[:, j * DH:(j + 1) * DH], a["lambdas"][j:j + 1, :].to_broadcast([P, DH]))\
                    .then_inc(s_const, 16)
            for n in range(4, DENSE_A):
                load_unit(sp, n)
            for t in range(TT):
                sp.wait_ge(s_tr, TT + t + 1)
                sp.dma_start(H[:, t, :], a["x"][t]).then_inc(s_x[t], 16)
            sp.dma_start(rw, a["router_w"]).then_inc(s_router_w, 16)
            sp.dma_start(rb, a["router_b"].to_broadcast([P, NG + NE])).then_inc(s_router_w, 16)
            sp.dma_start(gb[:, :], a["gains"][1:2, :].to_broadcast([P, D])).then_inc(s_gain, 16)

            expert_load(sp, "gate", 0)

            def body(e, q, first, last):
                expert_load(sp, "up", e)
                if first and q == 0:
                    expert_load(sp, "down", e)
                if not (last and q):
                    expert_load(sp, "gate", e + 1)
                if not (first and q == 0):
                    expert_load(sp, "down", e)

            pairs(body, sp)

            def over(j):
                e = sp.value_load(over_e[:, bass.ds(j, 1)], min_val=0, max_val=NE - 1)
                for i in range(2):
                    sp.wait_ge(s_wh[4 + i], NE)
                    sp.wait_ge(s_wo[4 + i], NE)
                for u in range(6):
                    w = a[("w_gate", "w_up", "w_down")[u // 2]]
                    sp.dma_start(wO, w[bass.ds(2 * e + u % 2, 1), :, :].rearrange("o p c -> (o p) c"))\
                        .then_inc(s_ow, 16)
                    sp.wait_ge(s_ou, 6 * j + u + 1)
                sp.sem_inc(s_seen, 1)

            overflow(sp, over)
            sp.wait_ge(s_tr, 3 * TT)
            sp.wait_ge(s_xn, 3 * TT)
            sp.dma_start(gb[:, :], a["gains"][2:3, :].to_broadcast([P, D])).then_inc(s_gain, 16)
            sp.dma_start(gm, a["gains"][3:4, :].to_broadcast([P, D])).then_inc(s_gain, 16)
            for m in range(SLOTS):
                load_b(sp, m)
            sp.dma_start(cconv, a["conv_tables"]).then_inc(s_tab, 16)
            for t in range(TT):
                sp.wait_ge(s_x2, t + 1)
                sp.dma_start(x2_rows[t], H[:, t, :]).then_inc(s_x2s, 16)
            for m in range(SLOTS, 12):
                load_b(sp, m)
            sp.wait_ge(s_xn, 4 * TT)
            sp.dma_start(bo, a["gains"][5:6, :].to_broadcast([P, D])).then_inc(s_bo, 16)
            sp.wait_ge(s_x2s, 16 * TT)
            for t in range(TT):
                if t == TT // 2:
                    sp.wait_ge(s_st, 2 * KT)
                    sp.dma_start(gb[:, :], a["gains"][4:5, :].to_broadcast([P, D])).then_inc(s_gain, 16)
                sp.wait_ge(s_cl, 2 * t + 2)
                sp.dma_start(H[:, t, :], x2_rows[t]).then_inc(s_x[t], 16)

            def body(c, last):
                for s in range(SLOTS):
                    sp.wait_ge(s_wh[s], RM + c)
                    sp.wait_ge(s_wo[s], RM + c)
                    src = a["w_mlp"][bass.ds(SLOTS * c + s, 1), :, :].rearrange("o p c -> (o p) c")
                    sp.dma_start(wstage(s), src).then_inc(s_wl[s], 16)

            mlp_chunks(sp, body)
            for t in range(TT):
                for n in range(2):
                    j = 8 + 2 * t + n
                    sp.wait_ge(s_free[j % 4], G_MLP + 6 * (NC - 1) + j // 4 + 1)
                sp.dma_start(out[t * P:(t + 1) * P, :], H[:, t, :]).then_inc(s_out, 16)
            sp.wait_ge(s_out, 16 * TT)

        @block.gpsimd
        def _(pool):
            zero = AR[:, 11264:12288]
            nc.gpsimd.memset(zero, 0.0).then_inc(s_zero, 1)
            pool.wait_ge(s_zero, 1)
            for b in range(NE, BLK_MAX + 1):
                pool.dma_start(y_rows[b * P:(b + 1) * P, :], zero).then_inc(s_cleared, 16)
            for i in range(2):
                n = 14 + i
                pool.wait_ge(s_wh[n % SLOTS], n // SLOTS + 1)
                nc.gpsimd.tensor_scalar(wstage(n % SLOTS), wstage(n % SLOTS), WS, None, ALU.mult).then_inc(s_sc, 1)
                pool.wait_ge(s_sc, i + 1)
                nc.gpsimd.tensor_tensor(wlo(n % SLOTS), wstage(n % SLOTS), whi(n % SLOTS), ALU.subtract)\
                    .then_inc(s_wo[n % SLOTS], 1)
            for t in range(TT):
                pool.wait_ge(s_xn, 2 * TT + t + 1)
                pool.dma_start(xn_rows[t * P:(t + 1) * P, :], xn[:, t % 2, :]).then_inc(s_xs[t % 2], 16)
            for i in range(2):
                pool.wait_ge(s_xs[i], 16 * TT // 2)
            pool.wait_ge(s_slots, 1)
            pool.wait_ge(s_tr, 3 * TT)

            def gather(e, q):
                nc.gpsimd.tensor_copy(idx[q], tok_of[:, bass.ds(e, 1)]).then_inc(s_ix, 1)
                pool.wait_ge(s_ix, e + 1)
                pool.sem_inc(s_seen, 1)
                pool.indirect_dma_start(out=XG[q], out_offset=None, in_=xn_rows,
                                        in_offset=bass.IndirectOffsetOnAxis(ap=idx[q], axis=0))\
                    .then_inc(s_gx[q], 16)

            def store(e, q):
                pool.wait_ge(s_y[0], e + 1)
                pool.wait_ge(s_y[1], e + 1)
                dst = y_rows[bass.ds(e * P, P), :]
                pool.dma_start(dst, y[q]).then_inc(s_ys[q], 16)

            gather(0, 0)
            gather(1, 1)
            pool.wait_ge(s_xt, 1)
            pool.wait_ge(s_gx[0], 16)
            gather(2, 0)

            def body(e, q, first, last):
                if not last:
                    pool.wait_ge(s_xt, e + 2)
                    gather(e + 3, 1 - q)
                if not (first and q == 0):
                    store(e - 1, 1 - q)
                if not last:
                    expert_lo_pool(pool, e + 1)

            pairs(body, pool)
            store(NE - 1, 1)
            for i in range(2):
                pool.wait_ge(s_ys[i], 16 * NE // 2)
            pool.wait_ge(s_gx[0], 16 * (NE // 2 + 1))

            def over(j):
                nc.gpsimd.tensor_copy(idx[0], tok_of[:, bass.ds(j + NE, 1)]).then_inc(s_oix, 1)
                pool.wait_ge(s_oix, j + 1)
                pool.sem_inc(s_seen, 1)
                pool.indirect_dma_start(out=XO, out_offset=None, in_=xn_rows,
                                        in_offset=bass.IndirectOffsetOnAxis(ap=idx[0], axis=0)).then_inc(s_ox, 16)
                pool.wait_ge(s_oy, j + 1)
                pool.dma_start(y_rows[bass.ds((j + NE) * P, P), :], y[0]).then_inc(s_oys, 16)
                pool.wait_ge(s_oys, 16 * j + 16)
                pool.sem_inc(s_seen, 1)

            overflow(pool, over)
            for t in range(TT):
                if t >= 4:
                    pool.wait_ge(s_cmb, 2 * (t - 3))
                for k in range(2):
                    pool.indirect_dma_start(out=YG[t % 4][k], out_offset=None, in_=y_rows,
                                            in_offset=bass.IndirectOffsetOnAxis(ap=slot[:, k, t:t + 1], axis=0))\
                        .then_inc(s_yg[t % 4], 16)
            pool.wait_ge(s_cmb, 2 * TT)
            nc.gpsimd.memset(U[:, :, 0:PAD], 0.0).then_inc(s_pad, 1)
            n = 0
            for i, (k, th) in enumerate(CONV_ACT):
                pool.wait_ge(s_c0, i + 1)
                for j in range(1, TAPS):
                    n += 1
                    pool.wait_ge(s_pr, n)
                    if j > 1:
                        pool.wait_ge(s_ca, n - 1)
                    nc.gpsimd.tensor_tensor(HC(k, th), HC(k, th), prod[n % 4], ALU.add).then_inc(s_ca, 1)
            hs = slice(512, 1024)
            pool.wait_ge(s_va, 2)
            for i, k in enumerate(LN_POOL[1]):
                nc.gpsimd.tensor_tensor(HC(k, 1), HC(k, 1), mean[:, hs], ALU.subtract).then_inc(s_zq, 1)
                pool.wait_ge(s_zq, i + 1)
                if i == 0:
                    pool.wait_ge(s_rv, 2)
                nc.gpsimd.tensor_tensor(HC(k, 1), HC(k, 1), rdev[:, hs], ALU.mult).then_inc(s_zp, 1)

        @block.scalar
        def _(act):
            ch = Chain(act, s_act)
            act.wait_ge(s_misc, 16)
            for t in range(TT + 1):
                if t < TT:
                    act.wait_ge(s_x[t], 16)
                    norm_stats(act, ch, t)
                if t:
                    xt_hi(act, 0, t - 1)
                if t in (2, 4, 6, 8):
                    split_hi(act, t // 2 - 1)

            def chunk(c):
                for g, ft, tk in chunk_groups(c):
                    if c == 2:
                        act.wait_ge(s_full[g % 4], g // 4 + 1)
                        if tk >= 2:
                            act.wait_ge(s_free[(g - 2) % 4], (g - 2) // 4 + 1)
                        nc.scalar.activation(xn[:, 0, (tk % 2) * 512:(tk % 2) * 512 + 512], PS[:, g % 4, :],
                                             ACT.Sigmoid, scale=IWS).then_inc(s_sig, 1)
                    elif c in (3, 4):
                        act.wait_ge(s_full[g % 4], g // 4 + 1)
                        nc.scalar.activation(chunk_dest(c, ft, tk)[0], PS[:, g % 4, :], ACT.Copy,
                                             scale=CHUNK_SCALE[c]).then_inc(s_qk, 1)
                    elif g % 2 == 0:
                        act.wait_ge(s_full[g % 4], g // 4 + 1)
                        nc.scalar.activation(chunk_dest(c, ft, tk), PS[:, g % 4, :], ACT.Copy,
                                             scale=CHUNK_SCALE[c]).then_inc(s_free[g % 4], 1)
                if c != 2:
                    for n in (2 * c + 4, 2 * c + 5):
                        split_hi(act, n)

            for c in range(3):
                chunk(c)
                if c == 0:
                    act.wait_ge(s_lam, 1)
                    nc.scalar.activation(lexp, lsum, ACT.Exp).then_inc(s_lx, 1)
            for n in range(TT):
                act.wait_ge(s_ro, n + 1)
                if n:
                    act.wait_ge(s_rmix, n)
                for h in range(NH):
                    i = nc.scalar.activation(gb[:, h * DV:(h + 1) * DV],
                                             PT[:, 2 + n % 2, h * DV:(h + 1) * DV], ACT.Square,
                                             accum_out=ss4[:, h:h + 1])
                ch.done(i)
                nc.scalar.activation(std4, ss4, ACT.Sqrt, bias=eps, scale=1.0 / DV).then_inc(s_rss, 1)
            for n in (8, 9):
                split_hi(act, n)
            for c in range(3, 6):
                chunk(c)

            def t_evac(b):
                par = b % 2
                act.wait_ge(s_at, b + 1)
                if b >= 2:
                    act.wait_ge(s_ao, b - 1)
                n = min(4, BLOCKS[b][1] + 1)
                nc.scalar.activation(aT(par)[:, 0:n, :], tpair(0)[:, 0:n, :], ACT.Copy).then_inc(s_aea, 1)

            def o_evac(b):
                h, i = BLOCKS[b]
                act.wait_ge(s_ao, b + 1)
                nc.scalar.activation(H[:, i, h * DV:(h + 1) * DV], PT[:, 2 + b % 2, 0:DV], ACT.Copy,
                                     scale=rows_rec[:, 2 * b:2 * b + 1])
                nc.scalar.activation(gb[:, b % 8 * DV:b % 8 * DV + DV], PT[:, 2 + b % 2, 0:DV],
                                     ACT.Square, scale=rows_rec[:, 2 * b:2 * b + 1],
                                     accum_out=ssA[:, h * TT + i:h * TT + i + 1]).then_inc(s_aoe, 1)

            for b in range(NB + 2):
                if b < NB:
                    W = P * (BLOCKS[b][1] + 1)
                    for m in range(2):
                        act.wait_ge(s_amx, 2 * b + m + 1)
                        if b >= 2:
                            act.wait_ge(s_at, b - 1)
                        nc.scalar.activation(PB(b % 2, m)[:, 0:W], SC(m)[:, 0:W], ACT.Exp,
                                             bias=negmax[:, 2 * b + m:2 * b + m + 1],
                                             accum_out=rows_sum[:, 2 * b + m:2 * b + m + 1]).then_inc(s_ae, 1)
                if 1 <= b <= NB:
                    t_evac(b - 1)
                if b >= 2:
                    o_evac(b - 2)
            act.wait_ge(s_aoe, NB)
            nc.scalar.activation(stdA, ssA, ACT.Sqrt, bias=eps, scale=1.0 / DV).then_inc(s_std, 1)
            for t in range(TT):
                xt_hi(act, 1, t)
            for t in range(TT + 2):
                if t < TT:
                    g = 49 + 2 * t
                    act.wait_ge(s_free[g % 4], g // 4 + 1)
                    act.wait_ge(s_free[(g - 1) % 4], (g - 1) // 4 + 1)
                    norm_stats(act, ch, t)
                if t >= 2:
                    xt_hi(act, 2, t - 2)
            for g in range(60, 64):
                act.wait_ge(s_full[g % 4], 16)
            for i in range(2):
                expert_hi(act, 2 + i, 0)
            act.wait_ge(s_rd, 1)
            nc.scalar.activation(rex, rex, ACT.Exp).then_inc(s_rx, 1)
            for i in range(2):
                expert_hi(act, i, 0)
            act.wait_ge(s_rd, 2)
            nc.scalar.activation(rde, rde, ACT.Exp).then_inc(s_rx, 1)
            for i in range(2):
                expert_hi(act, 4 + i, 0)

            def xe_hi(e, q):
                act.wait_ge(s_xt, e + 1)
                nc.scalar.activation(xeh[q], tpair(0), ACT.Copy).then_inc(s_xeh, 1)

            for q in range(2):
                xe_hi(q, q)
            for i in range(2):
                expert_hi(act, 2 + i, 1)

            def body(e, q, first, last):
                act.wait_ge(s_g, e + 1)
                if not (first and q == 0):
                    act.wait_ge(s_t, e)
                nc.scalar.activation(sig, PS[:, q, :], ACT.Sigmoid, scale=IWS).then_inc(s_es, 1)
                if not (last and q):
                    for s in (0, 1):
                        expert_hi(act, s, e + 1)
                act.wait_ge(s_ht, e + 1)
                nc.scalar.activation(hTh, PS[:, 3, :].rearrange("p (k t) -> p k t", k=4), ACT.Copy)\
                    .then_inc(s_hh, 1)
                if not last:
                    xe_hi(e + 2, q)
                    for s in (2, 3):
                        expert_hi(act, s, e + 2)
                act.wait_ge(s_d[0], e + 1)
                if not (first):
                    act.wait_ge(s_ys[q], 8 * e if q == 0 else 8 * (e - 1))
                nc.scalar.activation(y[q][:, 0:512], PT[:, 2, :], ACT.Copy, scale=IWS).then_inc(s_y[0], 1)
                if not (last and q):
                    for s in (4, 5):
                        expert_hi(act, s, e + 1)

            pairs(body, act)

            def over(j):
                act.wait_ge(s_ot, 2 * j + 1)
                nc.scalar.activation(XOT.rearrange("p (k t) -> p k t", k=KT), tpair(0), ACT.Copy).then_inc(s_oc, 1)
                act.wait_ge(s_ou, 6 * j + 2)
                nc.scalar.activation(sO, PS[:, 0, :], ACT.Sigmoid).then_inc(s_os, 1)
                act.wait_ge(s_ot, 2 * j + 2)
                nc.scalar.activation(hOT, PS[:, 3, :], ACT.Copy).then_inc(s_oc, 1)
                act.wait_ge(s_ou, 6 * j + 6)
                act.wait_ge(s_ys[0], 16 * NE // 2)
                nc.scalar.activation(y[0], PT[:, 2:4, :].rearrange("p b c -> p (b c)"), ACT.Copy).then_inc(s_oy, 1)
                act.wait_ge(s_oys, 16 * j + 16)
                act.sem_inc(s_seen, 1)

            overflow(act, over)
            for m in range(SLOTS):
                if m == 0:
                    act.wait_ge(s_u, NE)
                    act.wait_ge(s_g, NE)
                hi_b(act, m)
            for t in range(TT + 2):
                if t < TT:
                    act.wait_ge(s_cmb, 2 * t + 2)
                    norm_stats(act, ch, t)
                if 1 <= t <= TT:
                    act.wait_ge(s_x2, t)
                    norm_stats(act, ch, t - 1)
                if t >= 2:
                    xt_hi(act, 3, t - 2)
            act.wait_ge(s_tab, 16)

            act.wait_ge(s_tr, 4 * TT)

            def gated(g):
                i, k, th = conv_in_group(g)
                p = GATED.index((k, th))
                if p >= 2 and i == 0:
                    act.wait_ge(s_cu, p - 1)
                act.wait_ge(s_full[g % 4], g // 4 + 1)
                dst, fn = ((av, ACT.Identity), (sv, ACT.Sigmoid))[i]
                nc.scalar.activation(dst[p % 2], PS[:, g % 4, :], fn, bias=b_in[:, 8 * i + k:8 * i + k + 1],
                                     scale=IWS).then_inc(s_free[g % 4], 1)

            n = [0]

            def product_tap(i, j):
                k, th = CONV_ACT[i]
                if j == 0:
                    act.wait_ge(s_cu, input_done(k, th))
                    act.wait_ge(s_pad, 1)
                    act.wait_ge(s_x2s, 16 * TT)
                    act.wait_ge(s_xn, 4 * TT)
                    nc.scalar.activation(HC(k, th), U[:, k, th * 512:th * 512 + 512], ACT.Identity,
                                         bias=cb[:, k:k + 1], scale=cw[:, k, 0:1]).then_inc(s_c0, 1)
                    return
                n[0] += 1
                if n[0] > 4:
                    act.wait_ge(s_ca, n[0] - 4)
                nc.scalar.activation(prod[n[0] % 4], U[:, k, th * 512 + j:th * 512 + j + 512], ACT.Identity,
                                     scale=cw[:, k, j:j + 1]).then_inc(s_pr, 1)

            todo = [(i, j) for i in range(len(CONV_ACT)) for j in range(TAPS)]

            def products(most, inputs=len(GATED)):
                for _ in range(most):
                    if todo and input_done(*CONV_ACT[todo[0][0]]) <= inputs:
                        product_tap(*todo.pop(0))

            for g in range(64, 96):
                if g in (78, 94):
                    for m in range(2):
                        hi_b(act, 4 + m + (g - 78) // 4)
                gated(g)
                if g == 79:
                    for m in range(2):
                        hi_b(act, 6 + m)
                products(4 if g % 4 else 3, (g - 66) // 2)
            for m in range(10, 12):
                hi_b(act, m)

            def squares(x):
                k, th = x
                while x in CONV_ACT and todo and todo[0][0] <= CONV_ACT.index(x):
                    products(1)
                conv_wait(act, x)
                q = KT * th + SUM_ORDER[th].index(k)
                if q >= 2:
                    act.wait_ge(s_st, q - 1)
                nc.scalar.activation(squared[q % 2], HC(k, th), ACT.Square).then_inc(s_sq, 1)

            def silus(th, products_between):
                act.wait_ge(s_va, th + 1)
                hs = slice(th * 512, th * 512 + 512)
                nc.scalar.activation(rdev[:, hs], var[:, hs], ACT.Sqrt, bias=eps, scale=1.0).then_inc(s_rd2, 1)
                products(products_between)
                for k in range(KT + 1):
                    q = KT * th + k
                    if k < KT:
                        ln_wait(act, k, th)
                        if q >= 3:
                            act.wait_ge(s_cl, q - 2)
                        nc.scalar.activation(silu[q % 3], HC(k, th), ACT.Silu, bias=lnb[:, k:k + 1],
                                             scale=lng[:, k:k + 1]).then_inc(s_si, 1)
                    if k:
                        act.wait_ge(s_si, q)
                        nc.scalar.activation(XH[:, k - 1, hs], silu[(q - 1) % 3], ACT.Copy).then_inc(s_ch, 1)
                    products(products_between * (1 + k % 2))

            for g in range(92, 96):
                act.wait_ge(s_full[g % 4], g // 4 + 1)
            for m, k in enumerate(SUM_ORDER[0]):
                squares((k, 0))
                products(SUM_PRODUCTS[m])
            silus(0, 1)
            while todo:
                products(1)
            for k in SUM_ORDER[1]:
                squares((k, 1))
            silus(1, 0)
            for what, t in MLP_NORM_ACT:
                if what == "stats":
                    for g in (96 + 2 * t, 97 + 2 * t):
                        act.wait_ge(s_free[g % 4], g // 4 + 1)
                    norm_stats(act, ch, t)
                elif what == "hi":
                    xt_hi(act, 4, t)
                else:
                    mlp_hi(act, t, 0)

            def body(c, last):
                for j in range(9):
                    if j < 8:
                        act.wait_ge(s_full[j % 4], G_MLP + 6 * c + j // 4 + 1)
                        if j >= 2:
                            act.wait_ge(s_ml, 8 * c + j - 1)
                        nc.scalar.activation(relu[j % 2], PS[:, j % 4, :], ACT.Relu, scale=IWS)\
                            .then_inc(s_free[j % 4], 1)
                    if j:
                        h = j - 1
                        act.wait_ge(s_free[h % 4], G_MLP + 6 * c + h // 4 + 1)
                        nc.scalar.activation(HTh[:, h % 4, (h // 4) * 512:(h // 4) * 512 + 512], relu[h % 2],
                                             ACT.Square).then_inc(s_mh, 1)
                if not last:
                    for s in (0, 1):
                        act.wait_ge(s_full[3], G_MLP + 6 * c + 2)
                        mlp_hi(act, s, c + 1)
                    for s in (2, 3):
                        act.wait_ge(s_full[3], G_MLP + 6 * c + 6)
                        act.wait_ge(s_full[2], G_MLP + 6 * c + 6)
                        mlp_hi(act, s, c + 1)

            mlp_chunks(act, body)

        @block.vector
        def _(dve):
            ch = Chain(dve, s_dve)
            dve.wait_ge(s_misc, 16)
            dve.wait_ge(s_gain, 16)
            for t in range(TT + 1):
                if t < TT:
                    norm_scale(dve, ch, 0, t, t + 1)
                if t:
                    xt_lo(dve, 0, t - 1)
                if t in (2, 4, 6, 8):
                    split_lo(dve, t // 2 - 1)

            def lambdas():
                dve.wait_ge(s_const, 16 * 8)
                lam = lam_in.rearrange("p (j d) -> p j d", j=4)
                for j in range(2):
                    ch.done(nc.vector.tensor_tensor(lam_dot[:, j, :], lam[:, 2 * j, :], lam[:, 2 * j + 1, :], ALU.mult))
                nc.vector.tensor_reduce(lsum, lam_dot, AX.X, ALU.add).then_inc(s_lam, 1)
                dve.wait_ge(s_lx, 1)
                ch.done(nc.vector.tensor_tensor(neglam, lexp[:, 1:2], lexp[:, 0:1], ALU.subtract))
                ch.done(nc.vector.tensor_scalar(neglam, neglam, LAMBDA_INIT, None, ALU.subtract))
                ch.done(nc.vector.tensor_scalar(subg, subg, 1.0 - LAMBDA_INIT, None, ALU.mult))

            def chunk(c):
                for g, ft, tk in chunk_groups(c):
                    if c == 2:
                        dve.wait_ge(s_sig, tk + 1)
                        nc.vector.scalar_tensor_tensor(
                            out=chunk_dest(c, ft, tk), in0=PS[:, g % 4, :], scalar=IWS,
                            in1=xn[:, 0, (tk % 2) * 512:(tk % 2) * 512 + 512], op0=ALU.mult, op1=ALU.mult)\
                            .then_inc(s_free[g % 4], 1)
                    elif c in (3, 4):
                        dve.wait_ge(s_qk, g - 23)
                        hi, lo = chunk_dest(c, ft, tk)
                        nc.vector.scalar_tensor_tensor(out=lo, in0=PS[:, g % 4, :], scalar=CHUNK_SCALE[c], in1=hi,
                                                       op0=ALU.mult, op1=ALU.subtract).then_inc(s_free[g % 4], 1)
                    elif g % 2 == 1:
                        dve.wait_ge(s_full[g % 4], g // 4 + 1)
                        nc.vector.tensor_scalar(chunk_dest(c, ft, tk), PS[:, g % 4, :], CHUNK_SCALE[c], None,
                                                ALU.mult).then_inc(s_free[g % 4], 1)
                if c not in (2, 5):
                    for n in (2 * c + 4, 2 * c + 5):
                        split_lo(dve, n)

            for c in range(3):
                if c == 2:
                    dve.wait_ge(s_cleared, 16 * (NOVER + 1))
                chunk(c)
                if c == 0:
                    lambdas()

            def masked(n):
                par, blk = n % 2, slice(n * P, (n + 1) * P)
                dve.wait_ge(s_rsc, n + 1)
                if n >= 2:
                    dve.wait_ge(s_ro, n - 1)
                nc.vector.tensor_tensor(sT[par].rearrange("p (b c) -> p b c", b=2),
                                        PS[:, 2 * par:2 * par + 2, 0:256], decT, ALU.mult)
                nc.vector.tensor_tensor(ktok[par], PT[:, par, 0:256], kdec, ALU.mult)
                for t in range(2):
                    i = nc.vector.tensor_tensor(
                        qd[par][:, t * 256:t * 256 + 256].rearrange("p (j c) -> p j c", j=2),
                        QR[:, t:t + 1, blk].to_broadcast([P, 2, P]), qdec[:, t, :, :], ALU.mult)
                i.then_inc(s_rm, 1)

            def update(n):
                dve.wait_ge(s_ro, n + 1)
                if n == 0:
                    nc.vector.tensor_copy(state, PT[:, n % 2, 256:512]).then_inc(s_rst, 1)
                else:
                    ch.done(nc.vector.tensor_tensor(state, state, cdec, ALU.mult))
                    nc.vector.tensor_tensor(state, PT[:, n % 2, 256:512], state, ALU.add).then_inc(s_rst, 1)

            def mix(n):
                dve.wait_ge(s_rss, n + 1)
                ch.done(nc.vector.reciprocal(rst4, std4))
                for h in range(NH):
                    hs = slice(h * DV, (h + 1) * DV)
                    i = nc.vector.scalar_tensor_tensor(
                        out=H[:, n, 512 + h * DV:512 + (h + 1) * DV], in0=PT[:, 2 + n % 2, hs],
                        scalar=rst4[:, h:h + 1], in1=SG[:, n, hs], op0=ALU.mult, op1=ALU.mult)
                i.then_inc(s_rmix, 1)

            for n in range(TT + 1):
                if n < TT:
                    masked(n)
                if n:
                    update(n - 1)
                    mix(n - 1)
            for n in (8, 9):
                split_lo(dve, n)
            for c in range(3, 6):
                chunk(c)

            for b in range(NB + 1):
                if b:
                    q, i = b - 1, BLOCKS[b - 1][1]
                    W = P * (i + 1)
                    dve.wait_ge(s_ae, 2 * q + 2)
                    ch.done(nc.vector.reciprocal(rows_rec[:, 2 * q:2 * q + 2], rows_sum[:, 2 * q:2 * q + 2]))
                    ch.done(nc.vector.tensor_scalar(c1, rows_sum[:, 2 * q:2 * q + 1], rows_rec[:, 2 * q + 1:2 * q + 2],
                                                    neglam, ALU.mult, ALU.mult))
                    p0, p1 = PB(q % 2, 0)[:, 0:W], PB(q % 2, 1)[:, 0:W]
                    nc.vector.scalar_tensor_tensor(out=p0, in0=p1, scalar=c1, in1=p0,
                                                   op0=ALU.mult, op1=ALU.add).then_inc(s_aa, 1)
                if b < NB:
                    W = P * (BLOCKS[b][1] + 1)
                    for m in range(2):
                        dve.wait_ge(s_as, 2 * b + m + 1)
                        nc.vector.tensor_reduce(negmax[:, 2 * b + m:2 * b + m + 1], SC(m)[:, 0:W], AX.X, ALU.max,
                                                negate=True).then_inc(s_amx, 1)
                if b:
                    if i >= 4:
                        dve.wait_ge(s_at, q + 1)
                        if q >= 2:
                            dve.wait_ge(s_ao, q - 1)
                        nc.vector.tensor_copy(aT(q % 2)[:, 4:i + 1, :], tpair(0)[:, 4:i + 1, :])\
                            .then_inc(s_aed, 1)
            dve.wait_ge(s_std, TT + 1)
            ch.done(nc.vector.reciprocal(rstA, stdA))
            dve.wait_ge(s_rmix, TT)
            for t in range(TT + 1):
                if t < TT:
                    xn_wait(dve, 1, t)
                    for h in range(NH):
                        hs = slice(h * DV, (h + 1) * DV)
                        i = nc.vector.scalar_tensor_tensor(
                            out=xn[:, t % 2, hs], in0=H[:, t, hs], scalar=rstA[:, h * TT + t:h * TT + t + 1],
                            in1=subg, op0=ALU.mult, op1=ALU.mult)
                    i.then_inc(s_xn, 1)
                if t:
                    xt_lo(dve, 1, t - 1)
            dve.wait_ge(s_router_w, 32)
            ch.done(nc.vector.tensor_scalar(rwh, rw, WS, None, ALU.mult))
            nc.vector.scalar_tensor_tensor(out=rwl, in0=rw, scalar=WS, in1=rwh, op0=ALU.mult, op1=ALU.subtract)\
                .then_inc(s_rws, 1)
            dve.wait_ge(s_gain, 32)
            for t in range(TT + 2):
                if t < TT:
                    dve.wait_ge(s_x[t], 32)
                    for c in range(2):
                        g = 48 + 2 * t + c
                        dve.wait_ge(s_full[g % 4], g // 4 + 1)
                        nc.vector.scalar_tensor_tensor(out=H[:, t, c * 512:c * 512 + 512], in0=PS[:, g % 4, :],
                                                       scalar=IWS, in1=H[:, t, c * 512:c * 512 + 512],
                                                       op0=ALU.mult, op1=ALU.add).then_inc(s_free[g % 4], 1)
                if 1 <= t <= TT:
                    if t >= 3:
                        dve.wait_ge(s_xs[(t - 1) % 2], 16 * ((t - 1) // 2))
                    norm_scale(dve, ch, 2, t - 1, TT + 1 + t)
                if t >= 2:
                    xt_lo(dve, 2, t - 2)
            for i in range(2):
                expert_lo(dve, 2 + i, 0)
            router(dve, ch)

            for i in range(2):
                expert_lo(dve, i, 0)

            def xe_lo(e, q):
                dve.wait_ge(s_xeh, e + 1)
                nc.vector.tensor_tensor(xel[q], tpair(0), xeh[q], ALU.subtract).then_inc(s_xel, 1)

            for q in range(2):
                xe_lo(q, q)
            for i in range(2):
                expert_lo(dve, 4 + i, 0)
            for i in range(2):
                expert_lo(dve, 2 + i, 1)

            def body(e, q, first, last):
                dve.wait_ge(s_es, e + 1)
                nc.vector.scalar_tensor_tensor(out=tbuf, in0=PS[:, q, :], scalar=IWS, in1=sig,
                                               op0=ALU.mult, op1=ALU.mult).then_inc(s_t, 1)
                dve.wait_ge(s_u, e + 1)
                dve.wait_ge(s_t, e + 1)
                if not (first and q == 0):
                    dve.wait_ge(s_ht, e)
                nc.vector.scalar_tensor_tensor(out=hbuf, in0=PS[:, 2, :], scalar=IWS, in1=tbuf,
                                               op0=ALU.mult, op1=ALU.mult).then_inc(s_h, 1)
                if not (last and q):
                    expert_lo(dve, 0, e + 1)
                dve.wait_ge(s_hh, e + 1)
                nc.vector.tensor_tensor(hTl, PS[:, 3, :].rearrange("p (k t) -> p k t", k=4), hTh, ALU.subtract)\
                    .then_inc(s_hl, 1)
                if not (last and q):
                    expert_lo(dve, 1, e + 1)
                if not last:
                    xe_lo(e + 2, q)
                    for s in (2, 3):
                        expert_lo(dve, s, e + 2)
                dve.wait_ge(s_d[1], e + 1)
                if not (first):
                    dve.wait_ge(s_ys[q], 8 * e if q == 0 else 8 * (e - 1))
                nc.vector.tensor_scalar(y[q][:, 512:1024], PT[:, 3, :], IWS, None, ALU.mult).then_inc(s_y[1], 1)
                if not (last and q):
                    expert_lo(dve, 4, e + 1)
                if last and not q:
                    expert_lo(dve, 5, e + 1)

            pairs(body, dve)

            def over(j):
                dve.wait_ge(s_os, j + 1)
                nc.vector.tensor_tensor(sO, PS[:, 0, :], sO, ALU.mult).then_inc(s_og, 1)
                dve.wait_ge(s_og, j + 1)
                dve.wait_ge(s_ou, 6 * j + 4)
                nc.vector.tensor_tensor(hO, PS[:, 1, :], sO, ALU.mult).then_inc(s_oh, 1)

            overflow(dve, over)
            for m in range(SLOTS):
                lo_b(dve, m)
            dve.wait_ge(s_gain, 64)
            for t in range(TT + 3):
                if t < TT:
                    dve.wait_ge(s_yg[t % 4], 32 * (t // 4 + 1))
                    for k in range(2):
                        nc.vector.scalar_tensor_tensor(out=H[:, t, :], in0=YG[t % 4][k], scalar=wk[:, k, t:t + 1],
                                                       in1=H[:, t, :], op0=ALU.mult, op1=ALU.add).then_inc(s_cmb, 1)
                        dve.wait_ge(s_cmb, 2 * t + k + 1)
                if 1 <= t <= TT:
                    u = t - 1
                    dve.wait_ge(s_std, 2 * TT + 1 + first_dev(u))
                    ch.done(nc.vector.reciprocal(rstd[:, u:u + 1], std[:, u:u + 1]))
                    nc.vector.scalar_tensor_tensor(out=H[:, u, :], in0=H[:, u, :], scalar=rstd[:, u:u + 1],
                                                   in1=gb[:, :], op0=ALU.mult, op1=ALU.mult).then_inc(s_x2, 1)
                if 2 <= t <= TT + 1:
                    u = t - 2
                    dve.wait_ge(s_std, 2 * TT + 1 + second_dev(u))
                    ch.done(nc.vector.reciprocal(rstd[:, u:u + 1], std[:, u:u + 1]))
                    xn_wait(dve, 3, u)
                    nc.vector.scalar_tensor_tensor(out=xn[:, u % 2, :], in0=H[:, u, :], scalar=rstd[:, u:u + 1],
                                                   in1=gm, op0=ALU.mult, op1=ALU.mult).then_inc(s_xn, 1)
                if t >= 3:
                    xt_lo(dve, 3, t - 3)

            nw = {}
            started = []

            def tap(k, th, j):
                t0 = th * 512 + j
                if j == 0:
                    if not started:
                        dve.wait_ge(s_x2s, 16 * TT)
                        dve.wait_ge(s_pad, 1)
                        started.append(k)
                    dve.wait_ge(s_cu, input_done(k, th))
                    i = nc.vector.tensor_scalar(HC(k, th), U[:, k, t0:t0 + 512], cw[:, k, 0:1], cb[:, k:k + 1],
                                                ALU.mult, ALU.add)
                else:
                    dve.wait_ge(s_dve, nw[k, th])
                    i = nc.vector.scalar_tensor_tensor(out=HC(k, th), in0=U[:, k, t0:t0 + 512],
                                                       scalar=cw[:, k, j:j + 1], in1=HC(k, th),
                                                       op0=ALU.mult, op1=ALU.add)
                if j == TAPS - 1:
                    i.then_inc(s_cd, 1)
                else:
                    i.then_inc(s_dve, 1)
                    ch.n += 1
                    nw[k, th] = ch.n

            for p, (k, th) in enumerate(GATED):
                for g in gate_groups(p):
                    dve.wait_ge(s_free[g % 4], g // 4 + 1)
                nc.vector.tensor_tensor(U[:, k, PAD + th * 512:PAD + th * 512 + 512], av[p % 2], sv[p % 2], ALU.mult)\
                    .then_inc(s_cu, 1)
                for x in TAP_PLAN[p][0:3]:
                    tap(*x)
                if p in (7, 15):
                    for m in range(2):
                        lo_b(dve, p - 1 + m if p == 7 else 10 + m)
                for x in TAP_PLAN[p][3:]:
                    tap(*x)
                if p in (5, 13):
                    for m in range(2):
                        lo_b(dve, 4 + m + (p - 5) // 2)

            def out_tile(t, part):
                if part == 0:
                    dve.wait_ge(s_x[t], 48)
                    dve.wait_ge(s_bo, 16)
                    ch.done(nc.vector.tensor_tensor(H[:, t, :], H[:, t, :], bo, ALU.add))
                g, c = 96 + 2 * t + part, slice(part * 512, part * 512 + 512)
                dve.wait_ge(s_full[g % 4], g // 4 + 1)
                nc.vector.scalar_tensor_tensor(out=H[:, t, c], in0=PS[:, g % 4, :], scalar=IWS, in1=H[:, t, c],
                                               op0=ALU.mult, op1=ALU.add).then_inc(s_free[g % 4], 1)

            def layer_norm(th):
                hs = slice(th * 512, th * 512 + 512)
                dve.wait_ge(s_st, KT * (th + 1))
                ch.done(nc.vector.tensor_scalar(mean[:, hs], PT[:, 2 * th, :], 1.0 / D, None, ALU.mult))
                ch.done(nc.vector.tensor_tensor(var[:, hs], mean[:, hs], mean[:, hs], ALU.mult))
                nc.vector.scalar_tensor_tensor(out=var[:, hs], in0=PT[:, 2 * th + 1, :], scalar=1.0 / D,
                                               in1=var[:, hs], op0=ALU.mult, op1=ALU.subtract).then_inc(s_va, 1)
                mine = [k for k in range(KT) if k not in LN_POOL[th]]
                centred = {}

                def centre(k):
                    nc.vector.tensor_tensor(HC(k, th), HC(k, th), mean[:, hs], ALU.subtract).then_inc(s_dve, 1)
                    ch.n += 1
                    centred[k] = ch.n

                for k in mine[0:2]:
                    centre(k)
                dve.wait_ge(s_rd2, th + 1)
                nc.vector.reciprocal(rdev[:, hs], rdev[:, hs]).then_inc(s_rv, 1)
                dve.wait_ge(s_rv, th + 1)
                for k in range(KT + 2):
                    if k in mine:
                        dve.wait_ge(s_dve, centred[k])
                        nc.vector.tensor_tensor(HC(k, th), HC(k, th), rdev[:, hs], ALU.mult).then_inc(s_z, 1)
                        if mine.index(k) + 2 < len(mine):
                            centre(mine[mine.index(k) + 2])
                    if k >= 2:
                        q = KT * th + k - 2
                        dve.wait_ge(s_ch, q + 1)
                        nc.vector.tensor_tensor(XL[:, k - 2, hs], silu[q % 3], XH[:, k - 2, hs], ALU.subtract)\
                            .then_inc(s_cl, 1)

            rest = list(TAP_PLAN[-1])
            while any(th == 0 for _, th, _ in rest):
                tap(*rest.pop(0))
            for _ in range(LN_AFTER):
                tap(*rest.pop(0))
            layer_norm(0)
            for i in range(TT):
                for _ in range(7):
                    if rest:
                        tap(*rest.pop(0))
                out_tile(i // 2, i % 2)
            while rest:
                tap(*rest.pop(0))
            layer_norm(1)
            dve.wait_ge(s_gain, 80)
            for what, t in MLP_NORM_DVE:
                if what == "out":
                    out_tile(t, 0)
                    out_tile(t, 1)
                elif what == "norm":
                    norm_scale(dve, ch, 4, t, 4 * TT + 2 + t)
                elif what == "lo":
                    xt_lo(dve, 4, t)
                else:
                    mlp_lo(dve, t, 0)

            def body(c, last):
                for j in range(9):
                    if j < 8:
                        dve.wait_ge(s_free[j % 4], G_MLP + 6 * c + j // 4 + 1)
                        nc.vector.tensor_tensor(relu2[j % 2], relu[j % 2], relu[j % 2], ALU.mult).then_inc(s_relu, 1)
                    if j:
                        h = j - 1
                        dve.wait_ge(s_mh, 8 * c + j)
                        dve.wait_ge(s_relu, 8 * c + j)
                        nc.vector.tensor_tensor(HTl[:, h % 4, (h // 4) * 512:(h // 4) * 512 + 512], relu2[h % 2],
                                                HTh[:, h % 4, (h // 4) * 512:(h // 4) * 512 + 512], ALU.subtract)\
                            .then_inc(s_ml, 1)
                if not last:
                    for s in (0, 1):
                        mlp_lo(dve, s, c + 1)
                for j in range(8, 24):
                    t, n = (j - 8) // 2, j % 2
                    hs = slice(n * 512, n * 512 + 512)
                    dve.wait_ge(s_full[j % 4], G_MLP + 6 * c + j // 4 + 1)
                    nc.vector.scalar_tensor_tensor(out=H[:, t, hs], in0=PS[:, j % 4, :], scalar=IWS, in1=H[:, t, hs],
                                                   op0=ALU.mult, op1=ALU.add).then_inc(s_free[j % 4], 1)
                if not last:
                    for s in (2, 3):
                        mlp_lo(dve, s, c + 1)

            mlp_chunks(dve, body)

        @block.tensor
        def _(pe):
            pe.wait_ge(s_misc, 16)
            from_xn = lambda t, k: xn[:, t % 2, k * P:(k + 1) * P]
            for t in range(TT // 2):
                transposes(pe, 0, t, from_xn)

            def chunk(c):
                gs = chunk_groups(c)
                for g, ft, tk in gs:
                    if c == 0:
                        pe.wait_ge(s_xl, TT if tk else TT // 2)
                    group(pe, g, (2 * c, 2 * c + 1), FM[c], ft, tk)
                    if g < TT // 2:
                        transposes(pe, 0, TT // 2 + g, from_xn)
                if c == 0:
                    pe.wait_ge(s_const, 16 * 8)

            for c in range(3):
                chunk(c)
            for b in range(4):
                pe.wait_ge(s_free[b], 6)

            def scores(n):
                par, blk = n % 2, slice(n * P, (n + 1) * P)
                if n >= 2:
                    pe.wait_ge(s_rm, n - 1)
                    pe.wait_ge(s_rst, n - 1)
                for h in range(NH):
                    t, r = h // 2, slice(DH * (h % 2), DH * (h % 2) + DH)
                    nc.tensor.matmul(PS[:, 2 * par + h % 2, t * P:(t + 1) * P], KR[r, t, blk], QR[r, t, blk],
                                     start=True, stop=True)
                for t in range(2):
                    i = nc.tensor.transpose(PT[:, par, t * P:(t + 1) * P], KR[:, t, blk], ident)
                i.then_inc(s_rsc, 1)

            def outputs(n):
                par = n % 2
                pe.wait_ge(s_rm, n + 1)
                if n:
                    pe.wait_ge(s_rst, n)
                for h in range(NH):
                    t, r0 = h // 2, DH * (h % 2)
                    nc.tensor.matmul(PT[r0:r0 + DH, par, 256 + t * DV:256 + (t + 1) * DV], ktok[par][:, h * DH:(h + 1) * DH],
                                     VR[:, n, h * DV:(h + 1) * DV], start=True, stop=True)
                if n >= 2:
                    pe.wait_ge(s_rmix, n - 1)
                for h in range(NH):
                    t, j = h // 2, 2 * (h % 2) + h // 2
                    o = PT[:, 2 + par, h * DV:(h + 1) * DV]
                    i = nc.tensor.matmul(o, sT[par][:, j * P:(j + 1) * P], VR[:, n, h * DV:(h + 1) * DV],
                                         start=True, stop=n == 0)
                    if n:
                        i = nc.tensor.matmul(o, qd[par][:, h * P:(h + 1) * P], state[:, t * DV:(t + 1) * DV],
                                             start=False, stop=True)
                i.then_inc(s_ro, 1)

            for n in range(TT + 1):
                if n < TT:
                    scores(n)
                if n:
                    outputs(n - 1)
            for c in range(3, 6):
                if c == 3:
                    pe.wait_ge(s_rm, TT)
                    pe.wait_ge(s_rst, TT)
                    pe.wait_ge(s_rmix, TT)
                chunk(c)
            for b in range(4):
                pe.wait_ge(s_free[b], 12)

            def att_scores(b):
                h, i = BLOCKS[b]
                W = P * (i + 1)
                qs = slice(i * P, (i + 1) * P)
                for m in range(2):
                    r = slice(m * DH, (m + 1) * DH)
                    if b:
                        pe.wait_ge(s_ae, 2 * (b - 1) + m + 1)
                    for c0 in range(0, W, 512):
                        n = min(512, W - c0)
                        o = SC(m)[:, c0:c0 + n]
                        diag = c0 + n == W
                        ks = slice(c0, c0 + n)
                        nc.tensor.matmul(o, Qh[r, h, qs], Kh[r, h, ks], start=True, stop=False)
                        nc.tensor.matmul(o, Qh[r, h, qs], Kl[r, h, ks], start=False, stop=False)
                        nc.tensor.matmul(o, Ql[r, h, qs], Kh[r, h, ks], start=False, stop=False)
                        j = nc.tensor.matmul(o, pos_q[:, h, :], pos_k[:, S - W + c0:S - W + c0 + n],
                                             start=False, stop=not diag)
                        if diag:
                            j = nc.tensor.matmul(SC(m)[:, W - P:W], identb, corr[:, h, :], start=False, stop=True)
                    j.then_inc(s_as, 1)

            def att_transposes(b):
                i = BLOCKS[b][1]
                pe.wait_ge(s_aa, b + 1)
                if b:
                    pe.wait_ge(s_aea, b)
                    pe.wait_ge(s_aed, late(b))
                for k in range(i + 1):
                    j = nc.tensor.transpose(tpair(0)[:, k, :], PB(b % 2, 0)[:, k * P:(k + 1) * P], ident)
                j.then_inc(s_at, 1)

            def late(b):
                return sum(1 for q in range(b) if BLOCKS[q][1] >= 4)

            def att_out(b):
                h, i = BLOCKS[b]
                pe.wait_ge(s_aea, b + 1)
                pe.wait_ge(s_aed, late(b + 1))
                if b >= 2:
                    pe.wait_ge(s_aoe, b - 1)
                for k in range(i + 1):
                    j = nc.tensor.matmul(PT[:, 2 + b % 2, 0:DV], aT(b % 2)[:, k, :], V[:, k, h * DV:(h + 1) * DV],
                                         start=k == 0, stop=k == i)
                j.then_inc(s_ao, 1)

            for b in range(NB + 2):
                if b < NB:
                    att_scores(b)
                if 1 <= b <= NB:
                    att_transposes(b - 1)
                if b >= 2:
                    att_out(b - 2)
            mixed = lambda t, k: xn[:, t % 2, k * P:(k + 1) * P] if k < 4 else H[:, t, k * P:(k + 1) * P]
            for t in range(2):
                transposes(pe, 1, t, mixed)
            for t in range(TT + 2):
                if t < TT:
                    pe.wait_ge(s_xl, TT + t + 1)
                    for c in range(2):
                        g = 48 + 2 * t + c
                        group(pe, g, (12 + 2 * c, 13 + 2 * c), False, 0, t)
                        if g < 51:
                            for u in range(2):
                                transposes(pe, 1, 2 * (g - 47) + u, mixed)
                if t >= 2:
                    transposes(pe, 2, t - 2, from_xn)
            pe.wait_ge(s_rws, 1)
            pe.wait_ge(s_xl, 3 * TT)
            for b in range(4):
                pe.wait_ge(s_free[b], 16)
            for t in range(TT):
                for k in range(KT):
                    tk, c = slice(t * P, (t + 1) * P), slice(k * 36, k * 36 + 36)
                    i = product(pe, PS[:, 0, t * 36:(t + 1) * 36], XH[:, k, tk], XL[:, k, tk], rwh[:, c], rwl[:, c],
                                k == 0, k == KT - 1)
            i.then_inc(s_lg, 1)
            pe.wait_ge(s_rt, 1)
            for t in range(TT):
                for j in range(t + 1):
                    nc.tensor.matmul(PS[:, 1, t * NE:(t + 1) * NE], tri if j == t else onesb, rM[:, j, :],
                                     start=j == 0, stop=j == t)
            for j in range(TT):
                i = nc.tensor.matmul(PS[0:NE, 2, 0:1], rM[:, j, :], onesb[:, 0:1], start=j == 0, stop=j == TT - 1)
            i.then_inc(s_rp, 1)
            pe.wait_ge(s_rt, 2)
            nc.tensor.matmul(PS[:, 3, 0:NE], rexb[0:NE, :], tri[0:NE, 0:NE], start=True, stop=True)
            nc.tensor.matmul(PS[:, 3, NE:2 * NE], rexb[0:NE, :], tri[0:NE, 0:NE], start=True, stop=False)
            nc.tensor.matmul(PS[:, 3, NE:2 * NE], rexb[0:NE, :], identb[0:NE, 0:NE], start=False, stop=True)\
                .then_inc(s_rp, 1)
            pe.wait_ge(s_rt, 3)
            for n in range(2 * TT):
                i = nc.tensor.matmul(PS[:, 0, 0:BLK_MAX + 1], rA[:, n, :], rB[:, n, :],
                                     start=n == 0, stop=n == 2 * TT - 1)
            i.then_inc(s_rp, 1)

            def x_transposes(e, q):
                pe.wait_ge(s_gx[q], 16 * (e // 2 + 1) if isinstance(e, int) else 8 * (e - q) + 16)
                if not (isinstance(e, int) and e == 0):
                    pe.wait_ge(s_xel, e)
                for k in range(KT):
                    i = nc.tensor.transpose(tpair(0)[:, k, :], XG[q][:, k * P:(k + 1) * P], ident)
                i.then_inc(s_xt, 1)

            pe.wait_ge(s_slots, 1)
            for q in range(2):
                x_transposes(q, q)
            pe.wait_ge(s_xel, 1)
            expert_product(pe, PS[:, 0, :], 2, 0, xeh[0], xel[0], s_g)

            def h_transposes(e, very_first):
                pe.wait_ge(s_h, e + 1)
                if not very_first:
                    pe.wait_ge(s_hl, e)
                for k in range(4):
                    i = nc.tensor.transpose(PS[:, 3, k * P:(k + 1) * P], hbuf[:, k * P:(k + 1) * P], ident)
                i.then_inc(s_ht, 1)

            def body(e, q, first, last):
                if not (first and q == 0):
                    pe.wait_ge(s_h, e)
                expert_product(pe, PS[:, 2, :], 0, e, xeh[q], xel[q], s_u)
                if not (last and q):
                    if not (first and q == 0):
                        pe.wait_ge(s_t, e)
                    pe.wait_ge(s_xel, e + 2)
                    expert_product(pe, PS[:, 1 - q, :], 2, e + 1, xeh[1 - q], xel[1 - q], s_g,
                                   between=lambda: h_transposes(e, first and q == 0))
                else:
                    h_transposes(e, False)
                if not last:
                    x_transposes(e + 2, q)
                pe.wait_ge(s_hl, e + 1)
                for i in range(2):
                    s = 4 + i
                    pe.wait_ge(s_wo[s], BASE[s] + 1 + e)
                    if not (first and q == 0):
                        pe.wait_ge(s_y[i], e)
                    for k in range(UK):
                        c = slice(k * UC, k * UC + UC)
                        m = product(pe, PT[:, 2 + i, :], hTh[:, k, :], hTl[:, k, :], whi(s)[:, c], wlo(s)[:, c],
                                    k == 0, k == UK - 1)
                    m.then_inc(s_d[i], 1)

            pairs(body, pe)

            def over(j):
                for c in (s_h, s_t, s_hl, s_xel, s_y[0], s_y[1]):
                    pe.wait_ge(c, NE)
                pe.wait_ge(s_ox, 16 * j + 16)
                for k in range(KT):
                    i = nc.tensor.transpose(tpair(0)[:, k, :], XO[:, k * P:(k + 1) * P], ident)
                i.then_inc(s_ot, 1)
                pe.wait_ge(s_oc, 2 * j + 1)
                for u in range(6):
                    pe.wait_ge(s_ow, 96 * j + 16 * u + 16)
                    if u == 4:
                        pe.wait_ge(s_oh, j + 1)
                        for k in range(4):
                            i = nc.tensor.transpose(PS[:, 3, k * P:(k + 1) * P], hO[:, k * P:(k + 1) * P], ident)
                        i.then_inc(s_ot, 1)
                        pe.wait_ge(s_oc, 2 * j + 2)
                    for kk in range(UK):
                        c = slice(kk * UC, kk * UC + UC)
                        if u < 4:
                            k = u % 2 * UK + kk
                            i = nc.tensor.matmul(PS[:, u // 2, :], XOT[:, k * P:(k + 1) * P], wO[:, c],
                                                 start=k == 0, stop=k == KT - 1)
                        else:
                            i = nc.tensor.matmul(PT[:, u - 2, :], hOT[:, kk * P:(kk + 1) * P], wO[:, c],
                                                 start=kk == 0, stop=kk == UK - 1)
                    i.then_inc(s_ou, 1)
                pe.wait_ge(s_oy, j + 1)

            overflow(pe, over)
            for t in range(TT // 2):
                transposes(pe, 3, t, from_xn)
            for c in (s_h, s_t, s_hl):
                pe.wait_ge(c, NE)
            for g in range(64, 96):
                i, k, th = conv_in_group(g)
                pe.wait_ge(s_xl, 3 * TT + (TT if th else TT // 2))
                u = 4 * (k // 4) + 2 * i
                group_b(pe, g, (u, u + 1), True, k % 4, th)
                for t in {64: (4,), 65: (5, 6), 66: (7,)}.get(g, ()):
                    transposes(pe, 3, t, from_xn)
            ones = misc[:, M_ONE:M_ONE + P]

            def sums(th):
                for n, k in enumerate(SUM_ORDER[th]):
                    conv_wait(pe, (k, th))
                    nc.tensor.matmul(PT[:, 2 * th, :], ones, HC(k, th), start=n == 0, stop=n == KT - 1)
                    pe.wait_ge(s_sq, KT * th + n + 1)
                    nc.tensor.matmul(PT[:, 2 * th + 1, :], ones, squared[n % 2], start=n == 0, stop=n == KT - 1)\
                        .then_inc(s_st, 1)

            def out_groups(t):
                half_ = t // (TT // 2)
                for c in range(2):
                    first = lambda k: pe.wait_ge(s_cl, KT * half_ + k + 1)
                    group_b(pe, 96 + 2 * t + c, (8 + 2 * c, 9 + 2 * c), False, 0, t,
                            before=first if t % (TT // 2) == 0 and c == 0 else None)

            sums(0)
            for t in range(TT // 2):
                out_groups(t)
            sums(1)
            for what, t in MLP_NORM_PE:
                if what == "out":
                    out_groups(t)
                else:
                    transposes(pe, 4, t, from_xn)
            def body(c, last):
                for j in range(8):
                    th, ft = j // 4, j % 4
                    if j % 4 == 0:
                        pe.wait_ge(s_xl, 4 * TT + (th + 1) * TT // 2)
                    pe.wait_ge(s_free[j % 4], G_MLP + 6 * c + j // 4)
                    for s in range(2):
                        pe.wait_ge(s_wo[s], RM + 1 + c)
                        for kk in range(UK):
                            k = s * UK + kk
                            cs = slice(kk * UC + ft * P, kk * UC + ft * P + P)
                            ts = slice(th * 512, th * 512 + 512)
                            i = product(pe, PS[:, j % 4, :], whi(s)[:, cs], wlo(s)[:, cs], XH[:, k, ts], XL[:, k, ts],
                                        k == 0, k == KT - 1)
                    i.then_inc(s_full[j % 4], 1)
                for j in range(8, 24):
                    t, n = (j - 8) // 2, j % 2
                    s = 2 + n
                    pe.wait_ge(s_free[j % 4], G_MLP + 6 * c + j // 4)
                    pe.wait_ge(s_wo[s], RM + 1 + c)
                    pe.wait_ge(s_ml, 8 * c + (4 if t < 4 else 8))
                    ts = slice(t * P, (t + 1) * P)
                    for k in range(UK):
                        cs = slice(k * UC, k * UC + UC)
                        i = product(pe, PS[:, j % 4, :], HTh[:, k, ts], HTl[:, k, ts], whi(s)[:, cs], wlo(s)[:, cs],
                                    k == 0, k == UK - 1)
                    i.then_inc(s_full[j % 4], 1)

            mlp_chunks(pe, body)


def unit_layout(w):
    k, n = w.shape
    u = w.reshape(k // (UK * P), UK, P, n // UC, UC).transpose(3, 0, 2, 1, 4)
    return u.reshape(-1, P, UK * UC)


def by_channel(v):
    return v.reshape(-1, P).T


def expert_layout(w):
    return np.concatenate([unit_layout(v) for v in w])


def kernel(**inputs):
    import concourse.bacc as _bacc
    from concourse.bass_utils import run_bass_kernel_spmd as _run

    f = {k: np.ascontiguousarray(v) for k, v in inputs.items()}
    w_in = unit_layout(f["w_in"][0])
    order = [3, 4, 5, 0, 1, 2]
    w_ai = unit_layout(f["a_w_in_2"][0])
    NCH = DFF // UC
    w_a = np.concatenate([w_in[2 * c:2 * c + 2] for c in order] + [unit_layout(f["w_out"][0])])
    arrays = {
        "x": f["x"].reshape(TT, P, D),
        "gains": np.concatenate([f["attn_norm_g"], f["ffn_norm_g"], f["final_norm_g"][None], f["mix_norm_2"],
                                 f["mlp_norm_2"], f["a_b_out_2"]]),
        "lambdas": np.concatenate([f["da_lambda_q1"], f["da_lambda_k1"], f["da_lambda_q2"], f["da_lambda_k2"]]),
        "subln_g": f["da_subln_g"],
        "w_dense_a": w_a,
        "router_w": np.concatenate([f["router_group_w"][0], f["router_expert_w"][0]], axis=1)
        .reshape(KT, P, NG + NE).transpose(1, 0, 2).reshape(P, -1),
        "router_b": np.concatenate([f["router_group_b"], f["router_expert_b"]], axis=1),
        "conv_tables": np.concatenate([
            f["a_conv_w_2"][0].reshape(TAPS, KT, P).transpose(2, 1, 0).reshape(P, -1),
            by_channel(f["a_conv_b_2"]), by_channel(f["a_ln_g_2"]), by_channel(f["a_ln_b_2"]),
            by_channel(f["a_b_in_2"])], axis=1),
        "w_dense_b": np.concatenate([w_ai[0:2], w_ai[4:6], w_ai[2:4], w_ai[6:8], unit_layout(f["a_w_out_2"][0])]),
        "w_mlp": np.concatenate([unit_layout(f["mlp_w1_2"][0]).reshape(NCH, 2, P, UK * UC),
                                 unit_layout(f["mlp_w2_2"][0]).reshape(2, NCH, P, UK * UC).transpose(1, 0, 2, 3)],
                                axis=1).reshape(-1, P, UK * UC),
        "w_gate": expert_layout(f["expert_w_gate"][0]),
        "w_up": expert_layout(f["expert_w_up"][0]),
        "w_down": expert_layout(f["expert_w_down"][0]),
        **constants(),
    }
    nc = _bacc.Bacc("TRN2", target_bir_lowering=False, num_devices=1)
    sent, aps = {}, {}
    for name, value in arrays.items():
        value = np.ascontiguousarray(value)
        sent["in_" + name] = value
        aps[name] = nc.dram_tensor("in_" + name, value.shape, mybir.dt.from_np(value.dtype),
                                   kind="ExternalInput").ap()
    out = nc.dram_tensor("out_0", (S, D), F32, kind="ExternalOutput").ap()
    build(nc, aps, out)
    r = _run(nc, [sent], core_ids=[0])
    return r.results[0]["out_0"].reshape(1, S, D)
```
